# Optimizing a Trainium2 kernel written in Bass

```python
import math
import jax, jax.numpy as jnp
from jax import lax
import numpy as np

D_MODEL = 1024
BATCH = 1
SEQ = 1024
DEPTH = 1
DEC_BATCH = 1
DEC_SEQ = 64
PAST_LEN = 512

CHUNK = 64
EPS = 1e-6
BRANCH_W = D_MODEL // 2
GLA_HEADS = 4
GLA_DK = BRANCH_W // 8
GLA_DV = BRANCH_W // GLA_HEADS
GLA_LOWRANK = 16
GLA_TAU = 16.0
GDN_HEADS = 4
GDN_DK = BRANCH_W // GDN_HEADS
GDN_DV = BRANCH_W // GDN_HEADS
CONV_W = 4
S5_WIDTH = BRANCH_W
S5_GROUP = 16
S5_GROUPS = S5_WIDTH // S5_GROUP
S5_STATE = 64
GLA_QK = GLA_HEADS * GLA_DK
GLA_V = GLA_HEADS * GLA_DV
GDN_QK = GDN_HEADS * GDN_DK
GDN_V = GDN_HEADS * GDN_DV
GDN_CONV_CH = 2 * GDN_QK + GDN_V
IN_SIZES = (GLA_QK, GLA_QK, GLA_V, GLA_V, GLA_LOWRANK, GDN_CONV_CH, GDN_HEADS, GDN_HEADS, GDN_V, S5_WIDTH)
D_IN = 2 * GLA_QK + 2 * GLA_V + GLA_LOWRANK + GDN_CONV_CH + 2 * GDN_HEADS + GDN_V + S5_WIDTH
MOE_GROUPS = 4
EXPERTS_PER_GROUP = 4
N_EXPERTS = MOE_GROUPS * EXPERTS_PER_GROUP
TOP_K = 2
D_FF_EXPERT = D_MODEL // 4

kernel_name = 'hybrid_gla_gdn_s5_hmoe_streaming_step'

def rmsnorm(x, w):
    xf = x.astype(jnp.float32)
    y = xf * lax.rsqrt(jnp.mean(xf * xf, axis=-1, keepdims=True) + EPS)
    return (y * w.astype(jnp.float32)).astype(x.dtype)

def l2norm(x):
    xf = x.astype(jnp.float32)
    return xf * lax.rsqrt(jnp.sum(xf * xf, axis=-1, keepdims=True) + EPS)

def split_cols(z, sizes):
    idx, acc = [], 0
    for s in sizes[:-1]:
        acc += s
        idx.append(acc)
    return jnp.split(z, idx, axis=-1)

def to_chunks(t, L):
    B, T, H, d = t.shape
    return t.reshape(B, T // L, L, H, d).transpose(1, 0, 3, 2, 4)

def from_chunks(t):
    n, B, H, L, d = t.shape
    return t.transpose(1, 0, 3, 2, 4).reshape(B, n * L, H, d)

def gla_recurrence(q, k, v, log_a, s0):
    T = q.shape[1]
    L = min(CHUNK, T)
    causal = jnp.tril(jnp.ones((L, L), dtype=bool))

    def step(S, inp):
        qc, kc, vc, ac = inp
        b = jnp.cumsum(ac, axis=2)
        diff = b[:, :, :, None, :] - b[:, :, None, :, :]
        decay = jnp.exp(jnp.where(causal[:, :, None], diff, -jnp.inf))
        att = jnp.einsum('bhtd,bhsd,bhtsd->bhts', qc, kc, decay)
        o = jnp.einsum('bhts,bhsv->bhtv', att, vc) + jnp.einsum('bhtd,bhdv->bhtv', qc * jnp.exp(b), S)
        b_last = b[:, :, -1:, :]
        S = S * jnp.exp(b_last[:, :, 0, :, None]) + jnp.einsum('bhsd,bhsv->bhdv', kc * jnp.exp(b_last - b), vc)
        return S, o

    f = lambda t: to_chunks(t.astype(jnp.float32), L)
    S, o = lax.scan(step, s0.astype(jnp.float32), (f(q), f(k), f(v), f(log_a)))
    return from_chunks(o), S

def gdn_recurrence(q, k, v, beta, log_g, s0):
    T = q.shape[1]
    L = min(CHUNK, T)
    causal = jnp.tril(jnp.ones((L, L), dtype=bool))
    strict = jnp.tril(jnp.ones((L, L), dtype=bool), k=-1)
    eye = jnp.eye(L, dtype=jnp.float32)

    def step(S, inp):
        qc, kc, vc, bc, gc = inp
        G = jnp.cumsum(gc, axis=-1)
        dec = jnp.exp(jnp.where(causal, G[..., :, None] - G[..., None, :], -jnp.inf))
        a = jnp.where(strict, bc[..., :, None] * jnp.einsum('bhtd,bhsd->bhts', kc, kc) * dec, 0.0)
        rhs = jnp.concatenate([bc[..., None] * vc, (bc * jnp.exp(G))[..., None] * kc], axis=-1)
        sol = lax.linalg.triangular_solve(a + eye, rhs, left_side=True, lower=True, unit_diagonal=True)
        w_v, w_k = sol[..., :GDN_DV], sol[..., GDN_DV:]
        u = w_v - jnp.einsum('bhtd,bhdv->bhtv', w_k, S)
        qk = jnp.einsum('bhtd,bhsd->bhts', qc, kc) * dec
        o = jnp.einsum('bhts,bhsv->bhtv', qk, u) + jnp.einsum('bhtd,bhdv->bhtv', qc * jnp.exp(G)[..., None], S)
        g_last = G[..., -1:]
        S = S * jnp.exp(g_last)[..., None] + jnp.einsum('bhsd,bhsv->bhdv', kc * jnp.exp(g_last - G)[..., None], u)
        return S, o

    f = lambda t: to_chunks(t.astype(jnp.float32), L)
    fs = lambda t: to_chunks(t.astype(jnp.float32)[..., None], L)[..., 0]
    S, o = lax.scan(step, s0.astype(jnp.float32), (f(q), f(k), f(v), fs(beta), fs(log_g)))
    return from_chunks(o), S

def s5_scan(u, a_re, a_im, log_dt, b_re, b_im, c_re, c_im, d, h0_re, h0_im):
    B, T, _ = u.shape
    L = min(CHUNK, T)
    f32 = jnp.float32
    lam = lax.complex(a_re.astype(f32), a_im.astype(f32))
    lam_bar = jnp.exp(lam * jnp.exp(log_dt.astype(f32))[:, None])
    b_bar = ((lam_bar - 1.0) / lam)[..., None] * lax.complex(b_re.astype(f32), b_im.astype(f32))
    c = lax.complex(c_re.astype(f32), c_im.astype(f32))
    u_blocks = jnp.moveaxis(u.astype(f32).reshape(B, T // L, L, S5_GROUPS, S5_GROUP), 1, 0)

    def combine(e1, e2):
        a1, b1 = e1
        a2, b2 = e2
        return a1 * a2, a2 * b1 + b2

    def step(h, u_blk):
        bu = jnp.einsum('gpc,blgc->blgp', b_bar, u_blk.astype(jnp.complex64))
        a_cum, h_loc = lax.associative_scan(combine, (jnp.broadcast_to(lam_bar, bu.shape), bu), axis=1)
        hs = h_loc + a_cum * h[:, None]
        y = jnp.einsum('gcp,blgp->blgc', c, hs).real
        return hs[:, -1], y

    h0 = lax.complex(h0_re.astype(f32), h0_im.astype(f32))
    h, y = lax.scan(step, h0, u_blocks)
    y = jnp.moveaxis(y, 0, 1).reshape(B, T, S5_WIDTH) + d.astype(f32) * u.astype(f32)
    return y, jnp.real(h), jnp.imag(h)

def mixer(h, p, s_gla, s_gdn, conv_buf, s5_re, s5_im):
    B, T, _ = h.shape
    f32 = jnp.float32
    z = h @ p['w_in']
    qa, ka, va, ga, aa, qkv_b, beta_b, a_b, gb, u_c = split_cols(z, IN_SIZES)
    qa = qa.reshape(B, T, GLA_HEADS, GLA_DK) * GLA_DK ** -0.5
    ka = ka.reshape(B, T, GLA_HEADS, GLA_DK)
    va = va.reshape(B, T, GLA_HEADS, GLA_DV)
    log_a = jax.nn.log_sigmoid((aa @ p['w_alpha_up'] + p['b_alpha']).astype(f32)) / GLA_TAU
    o_a, s_gla_new = gla_recurrence(qa, ka, va, log_a.reshape(B, T, GLA_HEADS, GLA_DK), s_gla)
    o_a = rmsnorm(o_a, p['gla_norm_w']) * jax.nn.silu(ga.reshape(B, T, GLA_HEADS, GLA_DV).astype(f32))
    y_a = o_a.reshape(B, T, GLA_V).astype(h.dtype) @ p['w_br_a']
    xp = jnp.concatenate([conv_buf.astype(qkv_b.dtype), qkv_b], axis=1)
    conv = xp[:, 0:T] * p['conv_w'][0]
    for j in range(1, CONV_W):
        conv = conv + xp[:, j:j + T] * p['conv_w'][j]
    conv_buf_new = xp[:, T:]
    qb, kb, vb = split_cols(jax.nn.silu(conv), (GDN_QK, GDN_QK, GDN_V))
    qb = l2norm(qb.reshape(B, T, GDN_HEADS, GDN_DK)) * GDN_DK ** -0.5
    kb = l2norm(kb.reshape(B, T, GDN_HEADS, GDN_DK))
    vb = vb.reshape(B, T, GDN_HEADS, GDN_DV)
    beta = jax.nn.sigmoid(beta_b.astype(f32))
    log_g = -jnp.exp(p['gdn_a_log'].astype(f32)) * jax.nn.softplus(a_b.astype(f32) + p['gdn_dt_bias'].astype(f32))
    o_b, s_gdn_new = gdn_recurrence(qb, kb, vb, beta, log_g, s_gdn)
    o_b = rmsnorm(o_b, p['gdn_norm_w']) * jax.nn.silu(gb.reshape(B, T, GDN_HEADS, GDN_DV).astype(f32))
    y_b = o_b.reshape(B, T, GDN_V).astype(h.dtype) @ p['w_br_b']
    y_c, s5_re_new, s5_im_new = s5_scan(u_c, p['s5_a_re'], p['s5_a_im'], p['s5_log_dt'], p['s5_b_re'], p['s5_b_im'],
                                        p['s5_c_re'], p['s5_c_im'], p['s5_d'], s5_re, s5_im)
    y_c = jax.nn.gelu(y_c).astype(h.dtype)
    y_c = (y_c * jax.nn.sigmoid(y_c @ p['w_glu'] + p['b_glu'])) @ p['w_br_c']
    g_a, g_b, g_c = jnp.split(jax.nn.sigmoid(h @ p['w_gate'] + p['b_gate']), 3, axis=-1)
    out = (g_a * y_a + g_b * y_b + g_c * y_c) @ p['w_out']
    return out, (s_gla_new, s_gdn_new, conv_buf_new, s5_re_new, s5_im_new)

def hier_moe(h, p):
    B, T, D = h.shape
    hf = h.reshape(B * T, D)
    g_logits = (hf @ p['w_route_group'] + p['b_route_group']).astype(jnp.float32)
    p_group = jax.nn.softmax(g_logits, axis=-1)
    g_sel = jnp.argmax(g_logits, axis=-1)
    e_logits = (hf @ p['w_route_expert'] + p['b_route_expert']).astype(jnp.float32)
    e_logits = e_logits.reshape(B * T, MOE_GROUPS, EXPERTS_PER_GROUP)
    in_group = jnp.take_along_axis(e_logits, g_sel[:, None, None], axis=1)[:, 0]
    top_v, top_i = lax.top_k(in_group, TOP_K)
    w = jnp.take_along_axis(p_group, g_sel[:, None], axis=1) * jax.nn.softmax(top_v, axis=-1)
    e_idx = g_sel[:, None] * EXPERTS_PER_GROUP + top_i
    combine = jnp.einsum('nk,nke->ne', w, jax.nn.one_hot(e_idx, N_EXPERTS, dtype=jnp.float32)).astype(h.dtype)
    out = jnp.zeros_like(hf)
    for e in range(N_EXPERTS):
        he = jax.nn.silu(hf @ p['w_exp_gate'][e]) * (hf @ p['w_exp_up'][e])
        out = out + combine[:, e:e + 1] * (he @ p['w_exp_down'][e])
    return out.reshape(B, T, D)

def layer(x, c, p, st):
    mod = jax.nn.silu(c) @ p['w_ada'] + p['b_ada']
    sh1, sc1, g1, sh2, sc2, g2 = jnp.split(mod[:, None, :], 6, axis=-1)
    h = rmsnorm(x, p['norm1_w']) * (1.0 + sc1) + sh1
    m, new_st = mixer(h, p, *st)
    x = x + g1 * m
    h = rmsnorm(x, p['norm2_w']) * (1.0 + sc2) + sh2
    x = x + g2 * hier_moe(h, p)
    return x, new_st

def trunk(x, c, params, states, final_norm_w):
    new = []
    for l in range(DEPTH):
        x, st = layer(x, c, params[l], states[l])
        new.append(st)
    y = rmsnorm(x, final_norm_w)
    return y, [jnp.stack([new[l][i] for l in range(DEPTH)]) for i in range(5)]

def setup_inputs(seed: int = 0) -> dict:
    key = jax.random.key(seed)
    keys = jax.random.split(key, 64)
    kit = iter([keys[i] for i in range(64)])
    f32 = jnp.float32
    D = D_MODEL

    def nrm(shape, scale):
        return jax.random.normal(next(kit), shape, f32) * scale

    def uni(shape, lo, hi):
        return jax.random.uniform(next(kit), shape, f32, lo, hi)

    gdn_dt = jnp.exp(uni((DEPTH, GDN_HEADS), math.log(1e-3), math.log(1e-1)))
    return {
        'x_prompt': nrm((BATCH, SEQ, D), 1.0),
        'x_sample': nrm((DEC_BATCH, DEC_SEQ, D), 1.0),
        'c_prompt': nrm((BATCH, D), 1.0),
        'c_sample': nrm((DEC_BATCH, D), 1.0),
        'state_gla': nrm((DEPTH, DEC_BATCH, GLA_HEADS, GLA_DK, GLA_DV), 0.1),
        'state_gdn': nrm((DEPTH, DEC_BATCH, GDN_HEADS, GDN_DK, GDN_DV), 0.1),
        'cache_gdn_conv': nrm((DEPTH, DEC_BATCH, CONV_W - 1, GDN_CONV_CH), 1.0),
        'state_s5_re': nrm((DEPTH, DEC_BATCH, S5_GROUPS, S5_STATE), 0.1),
        'state_s5_im': nrm((DEPTH, DEC_BATCH, S5_GROUPS, S5_STATE), 0.1),
        'norm1_w': 1.0 + nrm((DEPTH, D), 0.01),
        'norm2_w': 1.0 + nrm((DEPTH, D), 0.01),
        'final_norm_w': 1.0 + nrm((D,), 0.01),
        'w_ada': nrm((DEPTH, D, 6 * D), 0.5 * D ** -0.5),
        'b_ada': nrm((DEPTH, 6 * D), 0.01),
        'w_in': nrm((DEPTH, D, D_IN), D ** -0.5),
        'w_alpha_up': nrm((DEPTH, GLA_LOWRANK, GLA_QK), GLA_LOWRANK ** -0.5),
        'b_alpha': nrm((DEPTH, GLA_QK), 0.1),
        'gla_norm_w': 1.0 + nrm((DEPTH, GLA_DV), 0.01),
        'conv_w': nrm((DEPTH, CONV_W, GDN_CONV_CH), CONV_W ** -0.5),
        'gdn_a_log': jnp.log(uni((DEPTH, GDN_HEADS), 1.0, 16.0)),
        'gdn_dt_bias': gdn_dt + jnp.log(-jnp.expm1(-gdn_dt)),
        'gdn_norm_w': 1.0 + nrm((DEPTH, GDN_DV), 0.01),
        's5_a_re': -0.5 + nrm((DEPTH, S5_GROUPS, S5_STATE), 0.01),
        's5_a_im': jnp.pi * jnp.arange(S5_STATE, dtype=f32) + nrm((DEPTH, S5_GROUPS, S5_STATE), 0.01),
        's5_log_dt': uni((DEPTH, S5_GROUPS), math.log(1e-3), math.log(1e-1)),
        's5_b_re': nrm((DEPTH, S5_GROUPS, S5_STATE, S5_GROUP), (2 * S5_GROUP) ** -0.5),
        's5_b_im': nrm((DEPTH, S5_GROUPS, S5_STATE, S5_GROUP), (2 * S5_GROUP) ** -0.5),
        's5_c_re': nrm((DEPTH, S5_GROUPS, S5_GROUP, S5_STATE), (2 * S5_STATE) ** -0.5),
        's5_c_im': nrm((DEPTH, S5_GROUPS, S5_GROUP, S5_STATE), (2 * S5_STATE) ** -0.5),
        's5_d': nrm((DEPTH, S5_WIDTH), 1.0),
        'w_glu': nrm((DEPTH, S5_WIDTH, S5_WIDTH), S5_WIDTH ** -0.5),
        'b_glu': nrm((DEPTH, S5_WIDTH), 0.01),
        'w_br_a': nrm((DEPTH, GLA_V, D), GLA_V ** -0.5),
        'w_br_b': nrm((DEPTH, GDN_V, D), GDN_V ** -0.5),
        'w_br_c': nrm((DEPTH, S5_WIDTH, D), S5_WIDTH ** -0.5),
        'w_gate': nrm((DEPTH, D, 3 * D), D ** -0.5),
        'b_gate': nrm((DEPTH, 3 * D), 0.01),
        'w_out': nrm((DEPTH, D, D), D ** -0.5),
        'w_route_group': nrm((DEPTH, D, MOE_GROUPS), D ** -0.5),
        'b_route_group': nrm((DEPTH, MOE_GROUPS), 0.01),
        'w_route_expert': nrm((DEPTH, D, N_EXPERTS), D ** -0.5),
        'b_route_expert': nrm((DEPTH, N_EXPERTS), 0.01),
        'w_exp_gate': nrm((DEPTH, N_EXPERTS, D, D_FF_EXPERT), D ** -0.5),
        'w_exp_up': nrm((DEPTH, N_EXPERTS, D, D_FF_EXPERT), D ** -0.5),
        'w_exp_down': nrm((DEPTH, N_EXPERTS, D_FF_EXPERT, D), D_FF_EXPERT ** -0.5),
    }

def reference(x_prompt, x_sample, c_prompt, c_sample, state_gla, state_gdn, cache_gdn_conv, state_s5_re, state_s5_im,
              norm1_w, norm2_w, final_norm_w, w_ada, b_ada, w_in, w_alpha_up, b_alpha, gla_norm_w, conv_w,
              gdn_a_log, gdn_dt_bias, gdn_norm_w, s5_a_re, s5_a_im, s5_log_dt, s5_b_re, s5_b_im, s5_c_re, s5_c_im,
              s5_d, w_glu, b_glu, w_br_a, w_br_b, w_br_c, w_gate, b_gate, w_out, w_route_group, b_route_group,
              w_route_expert, b_route_expert, w_exp_gate, w_exp_up, w_exp_down):
    params = [dict(norm1_w=norm1_w[l], norm2_w=norm2_w[l], w_ada=w_ada[l], b_ada=b_ada[l], w_in=w_in[l],
                   w_alpha_up=w_alpha_up[l], b_alpha=b_alpha[l], gla_norm_w=gla_norm_w[l], conv_w=conv_w[l],
                   gdn_a_log=gdn_a_log[l], gdn_dt_bias=gdn_dt_bias[l], gdn_norm_w=gdn_norm_w[l],
                   s5_a_re=s5_a_re[l], s5_a_im=s5_a_im[l], s5_log_dt=s5_log_dt[l], s5_b_re=s5_b_re[l],
                   s5_b_im=s5_b_im[l], s5_c_re=s5_c_re[l], s5_c_im=s5_c_im[l], s5_d=s5_d[l], w_glu=w_glu[l],
                   b_glu=b_glu[l], w_br_a=w_br_a[l], w_br_b=w_br_b[l], w_br_c=w_br_c[l], w_gate=w_gate[l],
                   b_gate=b_gate[l], w_out=w_out[l], w_route_group=w_route_group[l],
                   b_route_group=b_route_group[l], w_route_expert=w_route_expert[l],
                   b_route_expert=b_route_expert[l], w_exp_gate=w_exp_gate[l], w_exp_up=w_exp_up[l],
                   w_exp_down=w_exp_down[l])
              for l in range(DEPTH)]
    bp = x_prompt.shape[0]
    f32 = jnp.float32
    prompt_states = [(jnp.zeros((bp, GLA_HEADS, GLA_DK, GLA_DV), f32),
                      jnp.zeros((bp, GDN_HEADS, GDN_DK, GDN_DV), f32),
                      jnp.zeros((bp, CONV_W - 1, GDN_CONV_CH), x_prompt.dtype),
                      jnp.zeros((bp, S5_GROUPS, S5_STATE), f32),
                      jnp.zeros((bp, S5_GROUPS, S5_STATE), f32)) for _ in range(DEPTH)]
    y_prompt, new_p = trunk(x_prompt, c_prompt, params, prompt_states, final_norm_w)
    gla_p, gdn_p, conv_p, s5re_p, s5im_p = new_p
    sample_states = [(state_gla[l], state_gdn[l], cache_gdn_conv[l], state_s5_re[l], state_s5_im[l])
                     for l in range(DEPTH)]
    y_sample, new_s = trunk(x_sample, c_sample, params, sample_states, final_norm_w)
    gla_s, gdn_s, conv_s, s5re_s, s5im_s = new_s
    return (y_prompt, y_sample, gla_p, gdn_p, conv_p, s5re_p, s5im_p, gla_s, gdn_s, conv_s, s5re_s, s5im_s)


_drawn_inputs = setup_inputs


def setup_inputs(seed=0):
    import zlib

    import numpy as np

    out = dict(_drawn_inputs(seed))
    spreads = {}
    factors = {'state_gla': 28.598,
     'norm1_w': 3.824,
     'norm2_w': 6.225,
     'final_norm_w': 200.0,
     'gla_norm_w': 8.0,
     'gdn_norm_w': 8.0,
     's5_a_re': 67.516,
     's5_c_re': 8.0,
     's5_c_im': 8.0,
     'w_glu': 2.897,
     'b_glu': 85.399,
     'b_gate': 8.0,
     'b_route_group': 5.093,
     'b_route_expert': 22.106}
    for name, (base, spread) in spreads.items():
        noise = np.random.default_rng([zlib.crc32(name.encode()), seed]).standard_normal(out[name].shape)
        drawn = base * np.exp(spread * noise) if base else spread * noise
        out[name] = __import__('jax').numpy.asarray(drawn.astype(out[name].dtype))
    for name, factor in factors.items():
        out[name] = (out[name] * factor).astype(out[name].dtype)
    return out
```

```python
from contextlib import ExitStack

import numpy as np
import concourse.bass as bass
import concourse.mybir as mybir

F32 = mybir.dt.float32
I32 = mybir.dt.int32
U32 = mybir.dt.uint32
ALU = mybir.AluOpType
ACT = mybir.ActivationFunctionType
AX = mybir.AxisListType

P = 128
D = 1024
KD = D // P
SEQ = 1024
DEC = 64
TOK = SEQ + DEC
NT = 9
TP = NT * P
CHUNK = 64
EPS = 1e-6
BR = D // 2
KB = BR // P
HEADS = 4
GDK = 64
DV = 128
LOWR = 16
TAU = 16.0
CONVCH = 3 * BR
NCV = CONVCH // P
CW = 4
GROUPS = 32
GC = 16
ST = 64
PAIRS = GROUPS // 2
LB = 8
NBP = SEQ // LB
NBS = DEC // LB
NB = NBP + NBS
NE = 16
NG = 4
FF = D // 4
MT = 32
COL = dict(qa=0, ka=256, va=512, ga=1024, aa=1536, qkv=1552, beta=3088, a=3092, gb=3096, u=3608)
PIECES = [(0, 364), (364, 364), (728, 360)]
PW = 364


SOFTWARE_DMA = ("bias_loaded", "norm_loaded", "rows_loaded", "route_loaded", "scattered", "x_loaded0", "x_loaded1",
                "gathered0", "gathered1", "gathered2")


class Shared:
    pass


def rows_view(w):
    return w.rearrange("(k p) n -> p k n", p=P)


def stage_start(nc, g, d):
    with ExitStack() as ctx:
        def sb(name, shape, dt=F32):
            return ctx.enter_context(nc.sbuf_tensor(name, shape, dt))

        def sem(name):
            return (g.kept if name in SOFTWARE_DMA else ctx).enter_context(nc.semaphore(name))

        x_tiles = sb("x_tiles", [P, NT, D])
        x_sq = sb("x_sq", [P, D])
        x_ssq = sb("x_ssq", [P, NT])
        x_std = sb("x_std", [P, NT])
        x_rstd = sb("x_rstd", [P, NT])
        x_hat = sb("x_hat", [P, 2, D])
        c_cols = sb("c_cols", [P, KD, 2])
        c_silu = sb("c_silu", [P, KD, 2])
        ada_w = sb("ada_w", [P, 3, KD, 512])
        mod_rows = sb("mod_rows", [2, 6 * D])
        bias_rows = sb("bias_rows", [2, 6 * D])
        norm_cols = sb("norm_cols", [P, 2, KD])
        norm_scale = sb("norm_scale", [P, KD, 2])

        x_loaded = sem("x_loaded")
        c_loaded = sem("c_loaded")
        bias_loaded = sem("bias_loaded")
        norm_loaded = sem("norm_loaded")
        ada_loaded = [sem(f"ada_loaded{b}") for b in range(3)]
        masks_done = sem("masks_done")
        pad_zero = sem("pad_zero")
        ssq_done = sem("ssq_done")
        std_done = sem("std_done")
        rstd_done = sem("rstd_done")
        hat_done = sem("hat_done")
        turned = sem("turned")
        h_raw = sem("h_raw")
        silu_done = sem("silu_done")
        mod_psum = sem("mod_psum")
        mod_done = sem("mod_done")
        mod_stored = sem("mod_stored")
        mod_turned = sem("mod_turned")
        mod_cols_done = sem("mod_cols_done")
        scale_done = sem("scale_done")
        h_done = sem("h_done")

        turn_ps = [ctx.enter_context(nc.psum_tensor(f"turn_ps{b}", [P, 512], F32)) for b in range(4)]
        mod_ps = [ctx.enter_context(nc.psum_tensor(f"mod_ps{b}", [2, 512], F32)) for b in range(2)]
        cols_ps = ctx.enter_context(nc.psum_tensor("cols_ps", [P, 48, 2], F32))
        block = ctx.enter_context(nc.Block())
        ada_view = rows_view(d["w_ada"][0])

        @block.sync
        def _(sp):
            sp.dma_start(c_cols[:, :, 0], d["c_prompt"][0].rearrange("(k p) -> p k", p=P),
                         allow_slow_non_contiguous=True).then_inc(c_loaded, 16)
            sp.dma_start(c_cols[:, :, 1], d["c_sample"][0].rearrange("(k p) -> p k", p=P),
                         allow_slow_non_contiguous=True).then_inc(c_loaded, 16)
            sp.dma_start(x_tiles[:, 0:8, :], d["x_prompt"][0].rearrange("(i p) c -> p i c", p=P)).then_inc(x_loaded, 16)
            sp.dma_start(x_tiles[0:64, 8, :], d["x_sample"][0]).then_inc(x_loaded, 16)
            for b in range(3):
                sp.dma_start(ada_w[:, b], ada_view[:, :, 512 * b:512 * b + 512]).then_inc(ada_loaded[b], 16)
            with sp.Fori(1, 4) as r:
                for b in range(3):
                    sp.wait_ge(mod_psum, r * 3 + (b - 2))
                    sp.dma_start(ada_w[:, b], ada_view[:, :, bass.ds(r * 1536 + 512 * b, 512)]).then_inc(ada_loaded[b], 16)
            sp.wait_ge(mod_done, 12)
            sp.dma_start(g.mod_dram, mod_rows[:]).then_inc(mod_stored, 16)
            sp.wait_ge(mod_stored, 16)

        @block.gpsimd
        def _(pool):
            steps = [(t, slice(0, P), slice(0, P), 1.0) for t in (g.ident, g.upto, g.after, g.ones)]
            steps += [(g.eps, slice(0, P), slice(0, 1), EPS), (g.row_sel, slice(0, P), slice(0, 2 * P), 0.0)]
            steps += [(g.row_sel, slice(0, 64), slice(0, P), 1.0), (g.row_sel, slice(64, P), slice(P, 2 * P), 1.0)]
            n = 0
            for t, rows, cols, value in steps:
                if n:
                    pool.wait_ge(masks_done, n)
                nc.gpsimd.memset(t[rows, cols], value).then_inc(masks_done, 1)
                n += 1
            for t, op, step, cm in ((g.ident, ALU.is_equal, 1, -1), (g.upto, ALU.is_ge, 1, -1), (g.after, ALU.is_gt, -1, 1)):
                pool.wait_ge(masks_done, n)
                nc.gpsimd.affine_select(out=t[:], in_=t[:], compare_op=op, fill=0.0, base=0,
                                        pattern=[[step, P]], channel_multiplier=cm).then_inc(masks_done, 1)
                n += 1
            pool.wait_ge(masks_done, n)
            nc.gpsimd.memset(g.upto[0:64, 64:128], 0.0).then_inc(masks_done, 1)
            pool.wait_ge(masks_done, n + 1)
            nc.gpsimd.memset(g.after[64:128, 0:64], 0.0).then_inc(masks_done, 1)
            pool.dma_start(bias_rows[:], d["b_ada"].broadcast_to([2, 6 * D])).then_inc(bias_loaded, 16)
            pool.dma_start(norm_cols[:, 0], d["norm1_w"][0].rearrange("(k p) -> p k", p=P),
                           allow_slow_non_contiguous=True).then_inc(norm_loaded, 16)
            pool.dma_start(norm_cols[:, 1], d["norm2_w"][0].rearrange("(k p) -> p k", p=P),
                           allow_slow_non_contiguous=True).then_inc(norm_loaded, 16)

        @block.vector
        def _(dve):
            nc.vector.memset(x_tiles[64:128, 8, :], 0.0).then_inc(pad_zero, 1)
            dve.wait_ge(std_done, 1)
            nc.vector.reciprocal(x_rstd[:], x_std[:]).then_inc(rstd_done, 1)
            dve.wait_ge(rstd_done, 1)

            def normalise(i, b, freed):
                if freed is not None:
                    dve.wait_ge(turned, freed)
                nc.vector.tensor_scalar(x_hat[:, b], x_tiles[:, i] if isinstance(i, int) else x_tiles[:, bass.ds(i, 1)].rearrange("p o c -> p (o c)"),
                                        x_rstd[:, i:i + 1] if isinstance(i, int) else x_rstd[:, bass.ds(i, 1)],
                                        None, ALU.mult).then_inc(hat_done, 1)

            normalise(0, 0, None)
            normalise(1, 1, None)
            with dve.Fori(1, 4) as r:
                for b in range(2):
                    normalise(r * 2 + b, b, r * 2 + (b - 1))
            normalise(8, 0, 7)
            dve.wait_ge(bias_loaded, 16)
            with dve.Fori(0, 6) as r:
                for b in range(2):
                    dve.wait_ge(mod_psum, r * 2 + (b + 1))
                    sl = bass.ds(r * 1024 + 512 * b, 512)
                    nc.vector.tensor_tensor(mod_rows[:, sl], mod_ps[b][:], bias_rows[:, sl], ALU.add).then_inc(mod_done, 1)
            dve.wait_ge(mod_turned, 1)
            nc.vector.tensor_copy(g.mod_cols[:], cols_ps[:]).then_inc(mod_cols_done, 1)
            dve.wait_ge(mod_cols_done, 1)
            dve.wait_ge(norm_loaded, 32)
            nc.vector.tensor_scalar(norm_scale[:], g.mod_cols[:, KD:2 * KD, :], 1.0, None, ALU.add).then_inc(scale_done, 1)
            dve.wait_ge(scale_done, 1)
            nc.vector.tensor_tensor(norm_scale[:], norm_scale[:], norm_cols[:, 0, :].unsqueeze(2).broadcast_to([P, KD, 2]),
                                    ALU.mult).then_inc(scale_done, 1)
            dve.wait_ge(scale_done, 2)
            dve.wait_ge(h_raw, 2 * NT)
            for k in range(KD):
                for who, (a, b) in enumerate(((0, SEQ), (SEQ, TOK))):
                    nc.vector.tensor_scalar(g.h[:, k, a:b], g.h[:, k, a:b], norm_scale[:, k, who:who + 1],
                                            g.mod_cols[:, k, who:who + 1], ALU.mult, ALU.add).then_inc(h_done, 1)

        @block.scalar
        def _(act):
            act.wait_ge(c_loaded, 32)
            nc.scalar.activation(c_silu[:], c_cols[:], ACT.Silu).then_inc(silu_done, 1)
            act.wait_ge(x_loaded, 32)
            act.wait_ge(pad_zero, 1)
            for i in range(NT):
                if i:
                    act.wait_ge(ssq_done, i)
                nc.scalar.activation(x_sq[:], x_tiles[:, i], ACT.Square, accum_out=x_ssq[:, i:i + 1]).then_inc(ssq_done, 1)
            act.wait_ge(ssq_done, NT)
            act.wait_ge(masks_done, 13)
            nc.scalar.activation(x_std[:], x_ssq[:], ACT.Sqrt, scale=1.0 / D, bias=g.eps[:]).then_inc(std_done, 1)

            def unload(i, b):
                for q in range(2):
                    act.wait_ge(turned, i + 1)
                    dst = g.h[:, 4 * q:4 * q + 4, bass.ds(i * P, P)] if not isinstance(i, int) else g.h[:, 4 * q:4 * q + 4, i * P:i * P + P]
                    nc.scalar.activation(dst, turn_ps[2 * b + q][:].rearrange("p (k t) -> p k t", k=4), ACT.Copy).then_inc(h_raw, 1)

            with act.Fori(0, 4) as r:
                for b in range(2):
                    unload(r * 2 + b, b)
            unload(8, 0)

        @block.tensor
        def _(pe):
            pe.wait_ge(masks_done, 13)

            def turn(i, b, freed):
                pe.wait_ge(hat_done, i + 1)
                if freed is not None:
                    pe.wait_ge(h_raw, freed)
                for k in range(KD):
                    last = nc.tensor.transpose(turn_ps[2 * b + k // 4][:, P * (k % 4):P * (k % 4) + P],
                                               x_hat[:, b, P * k:P * k + P], g.ident[:])
                last.then_inc(turned, 1)

            turn(0, 0, None)
            turn(1, 1, None)
            with pe.Fori(1, 4) as r:
                for b in range(2):
                    turn(r * 2 + b, b, r * 4 + (2 * b - 2))
            turn(8, 0, 14)
            pe.wait_ge(silu_done, 1)

            def ada(s, b, q, rounds, freed):
                pe.wait_ge(ada_loaded[b], rounds)
                if freed is not None:
                    pe.wait_ge(mod_done, freed)
                for k in range(KD):
                    last = nc.tensor.matmul(mod_ps[q][:], c_silu[:, k], ada_w[:, b, k], start=k == 0, stop=k == KD - 1)
                last.then_inc(mod_psum, 1)

            ada(0, 0, 0, 16, None)
            ada(1, 1, 1, 16, None)
            for s in range(2, 12):
                ada(s, s % 3, s % 2, 16 * (s // 3 + 1), s - 1)
            pe.wait_ge(mod_done, 12)
            for j in range(48):
                last = nc.tensor.transpose(cols_ps[:, j, :], mod_rows[0:2, P * j:P * j + P], g.ident[0:2, 0:2])
            last.then_inc(mod_turned, 1)



TWO_PI_HI = 6.28125
TWO_PI_LO = 2 * float(np.pi) - TWO_PI_HI
PI_IN = 3.1415925


def stage_s5_tables(nc, g, d):
    with ExitStack() as ctx:
        def sb(name, shape, dt=F32):
            return ctx.enter_context(nc.sbuf_tensor(name, shape, dt))

        def sem(name):
            return ctx.enter_context(nc.semaphore(name))

        a_re, a_im, log_dt, dt, z_re, z_im, mag, turns, sin_z, sin_half, cos_z, num, den, t_a, t_b = (
            sb(f"s5_{n}", [P, PAIRS]) for n in
            "a_re a_im log_dt dt z_re z_im mag turns sin_z sin_half cos_z num den t_a t_b".split())
        whole = sb("s5_whole_turns", [P, PAIRS], I32)
        coef = sb("s5_coef", [P, 2, PAIRS])
        b_in = sb("s5_b_in", [P, 2, PAIRS, GC])
        c_rows = sb("s5_c_rows", [P, 2, 2, P])
        powers = sb("s5_powers", [P, 4, 3, PAIRS])
        b_pow = sb("s5_b_pow", [P, 2, PAIRS, LB, GC])
        tmp = sb("s5_tmp", [P, 2, 2, PAIRS, 4 * GC])
        lags = sb("s5_lags", [GC, GROUPS, LB, GC])
        d_cols = sb("s5_d_cols", [GC, GROUPS])
        d_diag = sb("s5_d_diag", [GC, GROUPS, GC])

        loaded = sem("s5_loaded")
        b_loaded = sem("s5_b_loaded")
        c_loaded = sem("s5_c_loaded")
        step = sem("s5_step")
        acts = sem("s5_acts")
        dt_ready = sem("s5_dt_ready")
        z_ready = sem("s5_z_ready")
        reduced = sem("s5_reduced")
        c_turned = sem("s5_c_turned")
        b_ready = sem("s5_b_ready")
        q_ready = sem("s5_q_ready")
        b_turned = sem("s5_b_turned")
        b_cols_done = sem("s5_b_cols_done")
        lag_psum = sem("s5_lag_psum")
        lag_out = sem("s5_lag_out")
        lags_done = sem("s5_lags_done")
        zeroed = sem("s5_zeroed")
        placed = sem("s5_placed")
        turn_ps = [ctx.enter_context(nc.psum_tensor(f"s5_turn_ps{b}", [P, 512], F32)) for b in range(4)]
        lag_ps = [ctx.enter_context(nc.psum_tensor(f"s5_lag_ps{b}", [GC, 4, LB, GC], F32)) for b in range(2)]
        block = ctx.enter_context(nc.Block())

        def both(x):
            return x.rearrange("(p h) s -> (h s) p", h=2)

        @block.sync
        def _(sp):
            sp.dma_start(a_re[:], d["s5_a_re"][0].rearrange("(p h) s -> (h s) p", h=2),
                         allow_slow_non_contiguous=True).then_inc(loaded, 16)
            sp.dma_start(a_im[:], d["s5_a_im"][0].rearrange("(p h) s -> (h s) p", h=2),
                         allow_slow_non_contiguous=True).then_inc(loaded, 16)
            for h in range(2):
                src = d["s5_log_dt"][0].rearrange("(p h) -> h p", h=2)[h:h + 1, :].broadcast_to([ST, PAIRS])
                sp.dma_start(log_dt[ST * h:ST * h + ST, :], src, allow_slow_non_contiguous=True).then_inc(loaded, 16)
            for r, name in enumerate(("s5_b_re", "s5_b_im")):
                sp.dma_start(b_in[:, r], d[name][0].rearrange("(p h) s c -> (h s) p c", h=2)).then_inc(b_loaded, 16)
            for r, name in enumerate(("s5_c_re", "s5_c_im")):
                for p in range(PAIRS):
                    src = d[name][0, 2 * p:2 * p + 2].rearrange("h c s -> c h s")
                    sp.dma_start(c_rows[GC * (p % 8):GC * (p % 8) + GC, r, p // 8].rearrange("c (h s) -> c h s", h=2),
                                 src).then_inc(c_loaded, 16)
            sp.dma_start(d_cols[:], d["s5_d"][0].rearrange("(g c) -> c g", c=GC),
                         allow_slow_non_contiguous=True).then_inc(loaded, 16)
            sp.wait_ge(lags_done, 1)
            sp.wait_ge(zeroed, 1)
            for l in range(LB):
                sp.dma_start(g.s5_toeplitz[GC * l:GC * l + GC, :, l:, :], lags[:, :, 0:LB - l, :]).then_inc(placed, 16)
            sp.wait_ge(placed, 16 * LB)

        @block.gpsimd
        def _(pool):
            nc.gpsimd.memset(g.s5_toeplitz[:], 0.0).then_inc(zeroed, 1)

        @block.scalar
        def _(act):
            act.wait_ge(loaded, 80)
            nc.scalar.activation(dt[:], log_dt[:], ACT.Exp).then_inc(dt_ready, 1)
            act.wait_ge(z_ready, 1)
            nc.scalar.activation(mag[:], z_re[:], ACT.Exp).then_inc(acts, 1)
            act.wait_ge(reduced, 1)
            nc.scalar.activation(sin_z[:], turns[:], ACT.Sin).then_inc(acts, 1)
            nc.scalar.activation(sin_half[:], turns[:], ACT.Sin, scale=0.5).then_inc(acts, 1)
            for q in range(8):
                act.wait_ge(b_turned, q + 1)
                r, p = q // 4, 4 * (q % 4)
                nc.scalar.activation(g.s5_b_cols[:, r, p:p + 4, :], turn_ps[q % 4][:].rearrange("p (a s) -> p a s", a=4),
                                     ACT.Copy).then_inc(b_cols_done, 1)

        @block.vector
        def _(dve):
            n = [0]

            def link(ins):
                n[0] += 1
                ins.then_inc(step, 1)
                dve.wait_ge(step, n[0])

            def tt(out, a, b, op):
                link(nc.vector.tensor_tensor(out, a, b, op))

            def ts(out, a, s1, s2, op0, op1=None):
                link(nc.vector.tensor_scalar(out, a, s1, s2, op0, op1) if op1 is not None else
                     nc.vector.tensor_scalar(out, a, s1, None, op0))

            dve.wait_ge(loaded, 80)
            dve.wait_ge(dt_ready, 1)
            tt(z_re[:], a_re[:], dt[:], ALU.mult)
            tt(z_im[:], a_im[:], dt[:], ALU.mult)
            ts(turns[:], z_im[:], 1.0 / (TWO_PI_HI + TWO_PI_LO), None, ALU.mult)
            link(nc.vector.tensor_copy(whole[:], turns[:]))
            nc.vector.tensor_copy(t_a[:], whole[:]).then_inc(z_ready, 1)
            dve.wait_ge(z_ready, 1)
            link(nc.vector.scalar_tensor_tensor(turns[:], t_a[:], -TWO_PI_HI, z_im[:], ALU.mult, ALU.add))
            link(nc.vector.scalar_tensor_tensor(turns[:], t_a[:], -TWO_PI_LO, turns[:], ALU.mult, ALU.add))
            nc.vector.tensor_scalar(turns[:], turns[:], -PI_IN, PI_IN, ALU.max, ALU.min).then_inc(reduced, 1)
            dve.wait_ge(acts, 3)
            tt(t_a[:], sin_half[:], sin_half[:], ALU.mult)
            ts(cos_z[:], t_a[:], -2.0, 1.0, ALU.mult, ALU.add)
            tt(powers[:, 0, 0], mag[:], cos_z[:], ALU.mult)
            tt(powers[:, 0, 1], mag[:], sin_z[:], ALU.mult)
            for q in range(4):
                ts(powers[:, q, 2], powers[:, q, 1], -1.0, None, ALU.mult)
                if q == 3:
                    break
                tt(t_a[:], powers[:, q, 0], powers[:, q, 1], ALU.subtract)
                tt(t_b[:], powers[:, q, 0], powers[:, q, 1], ALU.add)
                tt(powers[:, q + 1, 0], t_a[:], t_b[:], ALU.mult)
                link(nc.vector.scalar_tensor_tensor(powers[:, q + 1, 1], powers[:, q, 0], 2.0, powers[:, q, 1],
                                                    ALU.mult, ALU.mult))
            link(nc.vector.tensor_copy(g.s5_step[:, 0, 0], powers[:, 3, 0]))
            link(nc.vector.tensor_copy(g.s5_step[:, 0, 1], powers[:, 3, 0]))
            link(nc.vector.tensor_copy(g.s5_step[:, 1, 0], powers[:, 3, 2]))
            link(nc.vector.tensor_copy(g.s5_step[:, 1, 1], powers[:, 3, 1]))
            ts(num[:], powers[:, 0, 0], -1.0, None, ALU.add)
            tt(t_a[:], a_re[:], a_re[:], ALU.mult)
            tt(t_b[:], a_im[:], a_im[:], ALU.mult)
            tt(den[:], t_a[:], t_b[:], ALU.add)
            link(nc.vector.reciprocal(den[:], den[:]))
            tt(t_a[:], num[:], a_re[:], ALU.mult)
            tt(t_b[:], powers[:, 0, 1], a_im[:], ALU.mult)
            tt(t_a[:], t_a[:], t_b[:], ALU.add)
            tt(coef[:, 0], t_a[:], den[:], ALU.mult)
            tt(t_a[:], powers[:, 0, 1], a_re[:], ALU.mult)
            tt(t_b[:], num[:], a_im[:], ALU.mult)
            tt(t_a[:], t_a[:], t_b[:], ALU.subtract)
            tt(coef[:, 1], t_a[:], den[:], ALU.mult)
            ts(t_a[:], coef[:, 1], -1.0, None, ALU.mult)
            dve.wait_ge(b_loaded, 32)

            def times(out, a, w_re, w_a, w_b, width):
                def wide(w):
                    return w.unsqueeze(2).broadcast_to([P, PAIRS, width])
                for r in range(2):
                    tt(tmp[:, 0, r, :, 0:width], a[r], wide(w_re), ALU.mult)
                tt(tmp[:, 1, 0, :, 0:width], a[1], wide(w_a), ALU.mult)
                tt(tmp[:, 1, 1, :, 0:width], a[0], wide(w_b), ALU.mult)
                for r in range(2):
                    tt(out[r], tmp[:, 0, r, :, 0:width], tmp[:, 1, r, :, 0:width], ALU.add)

            def b_at(lo, hi):
                return [b_pow[:, r, :, lo:hi, :].rearrange("p a l c -> p a (l c)") for r in range(2)]

            def q_at(lo, hi):
                return [g.s5_c_pow[:, r, :, lo:hi, :].rearrange("p a l c -> p a (l c)") for r in range(2)]

            times(b_at(7, 8), [b_in[:, 0], b_in[:, 1]], coef[:, 0], t_a[:], coef[:, 1], GC)
            times(b_at(6, 7), b_at(7, 8), powers[:, 0, 0], powers[:, 0, 2], powers[:, 0, 1], GC)
            times(b_at(4, 6), b_at(6, 8), powers[:, 1, 0], powers[:, 1, 2], powers[:, 1, 1], 2 * GC)
            times(b_at(0, 4), b_at(4, 8), powers[:, 2, 0], powers[:, 2, 2], powers[:, 2, 1], 4 * GC)
            nc.vector.tensor_copy(t_b[:], t_a[:]).then_inc(b_ready, 1)
            dve.wait_ge(c_turned, 1)
            for r in range(2):
                for half in range(2):
                    src = turn_ps[2 * r + half][:, 0:P].rearrange("p (a c) -> p a c", c=GC)
                    ts(g.s5_c_pow[:, r, 8 * half:8 * half + 8, 0, :], src, -1.0 if r else 1.0, None, ALU.mult)
            times(q_at(1, 2), q_at(0, 1), powers[:, 0, 0], powers[:, 0, 1], powers[:, 0, 2], GC)
            times(q_at(2, 4), q_at(0, 2), powers[:, 1, 0], powers[:, 1, 1], powers[:, 1, 2], 2 * GC)
            times(q_at(4, 8), q_at(0, 4), powers[:, 2, 0], powers[:, 2, 1], powers[:, 2, 2], 4 * GC)
            times(q_at(8, 9), q_at(0, 1), powers[:, 3, 0], powers[:, 3, 1], powers[:, 3, 2], GC)
            nc.vector.tensor_copy(t_b[:], t_a[:]).then_inc(q_ready, 1)
            for q in range(8):
                dve.wait_ge(lag_psum, q + 1)
                first = 8 * (q // 2) + q % 2
                nc.vector.tensor_copy(lags[:, first:first + 7:2], lag_ps[q % 2][:]).then_inc(lag_out, 1)
            tt(d_diag[:], g.ident[0:GC, 0:GC].unsqueeze(1).broadcast_to([GC, GROUPS, GC]),
               d_cols[:].unsqueeze(2).broadcast_to([GC, GROUPS, GC]), ALU.mult)
            dve.wait_ge(lag_out, 8)
            nc.vector.tensor_tensor(lags[:, :, 0, :], lags[:, :, 0, :], d_diag[:], ALU.add).then_inc(lags_done, 1)

        @block.tensor
        def _(pe):
            pe.wait_ge(c_loaded, 32 * PAIRS)
            for r in range(2):
                for half in range(2):
                    last = nc.tensor.transpose(turn_ps[2 * r + half][:, 0:P], c_rows[:, r, half], g.ident[:])
            last.then_inc(c_turned, 1)
            pe.wait_ge(q_ready, 1)
            for q in range(8):
                if q >= 4:
                    pe.wait_ge(b_cols_done, q - 3)
                r, p = q // 4, 4 * (q % 4)
                for a in range(4):
                    last = nc.tensor.transpose(turn_ps[q % 4][:, P * a:P * a + P],
                                               b_pow[:, r, p + a].rearrange("p l c -> p (l c)"), g.ident[:])
                last.then_inc(b_turned, 1)
            for q in range(8):
                if q >= 2:
                    pe.wait_ge(lag_out, q - 1)
                for a in range(4):
                    pair, h = 4 * (q // 2) + a, q % 2
                    rows = slice(ST * h, ST * h + ST)
                    for r in range(2):
                        last = nc.tensor.matmul(lag_ps[q % 2][:, a], b_pow[rows, r, pair, LB - 1, :],
                                                g.s5_c_pow[rows, r, pair, 0:LB, :], start=a == 0 and r == 0,
                                                stop=a == 3 and r == 1, skip_group_check=True)
                last.then_inc(lag_psum, 1)


def stage_s5(nc, g, d, out):
    with ExitStack() as ctx:
        def sb(name, shape, dt=F32):
            return ctx.enter_context(nc.sbuf_tensor(name, shape, dt))

        def sem(name):
            return ctx.enter_context(nc.semaphore(name))

        space_p = sb("s5_blocks_p", [P, LB * BR])
        space_s = sb("s5_blocks_s", [NBS, LB * BR])
        u_p, u_s = (x[:].rearrange("b (g l c) -> b g l c", l=LB, c=GC) for x in (space_p, space_s))
        blocks_p, blocks_s = (x[:].rearrange("b (l c) -> b l c", l=LB) for x in (space_p, space_s))
        u_rows_s = sb("s5_u_rows_s", [DEC, BR])
        u_cols = sb("s5_u_cols", [P, GROUPS, NB])
        before_space = sb("s5_before", [P, (NB + 2) * 2 * PAIRS])
        before = before_space[:].rearrange("p (n r a) -> p n r a", r=2, a=PAIRS)
        w_u = before_space[:, 0:KD * BR].rearrange("p (k c) -> p k c", k=KD)
        first_s = NBP + 1
        prod = sb("s5_prod", [P, 2, 2, 2, PAIRS])

        w_loaded = sem("w_u_loaded")
        state_in = sem("s5_state_in")
        zero_state = sem("s5_zero_state")
        u_psum = sem("u_psum")
        u_out = sem("u_out")
        u_rows_in = sem("u_rows_in")
        u_turned = sem("u_turned")
        u_cols_done = sem("u_cols_done")
        v_psum = sem("s5_v_psum")
        v_done = sem("s5_v_done")
        scan = sem("s5_scan")
        y_psum = sem("s5_y_psum")
        y_done = sem("s5_y_done")
        y_turned = sem("s5_y_turned")
        y_cols_done = sem("s5_y_cols_done")
        stored = sem("s5_stored")
        ps = [ctx.enter_context(nc.psum_tensor(f"s5_ps{b}", [P, 512], F32)) for b in range(8)]
        block = ctx.enter_context(nc.Block())
        GQ = GROUPS // 2
        SETS = [(h, 4 * q) for q in range(PAIRS // 4) for h in range(2)]

        def groups_of(h, pair0):
            return slice(2 * pair0 + h, 2 * pair0 + h + 7, 2)

        @block.sync
        def _(sp):
            sp.dma_start(w_u, rows_view(d["w_in"][0])[:, :, COL["u"]:COL["u"] + BR]).then_inc(w_loaded, 16)
            sp.wait_ge(u_psum, LB + 1)
            for r, name in enumerate(("state_s5_re", "state_s5_im")):
                sp.dma_start(before[:, first_s, r], d[name][0, 0].rearrange("(p h) s -> (h s) p", h=2),
                             allow_slow_non_contiguous=True).then_inc(state_in, 16)
            sp.wait_ge(u_out, LB + 1)
            for l in range(LB):
                sp.dma_start(u_s[:, :, l], u_rows_s[l:DEC:LB].rearrange("b (g c) -> b g c", c=GC)).then_inc(u_rows_in, 16)
            sp.wait_ge(scan, 4 * NB)
            n = 0
            for where, at in ((0, NBP), (1, first_s + NBS)):
                for r in range(2):
                    sp.dma_start(out["s5"][where][r][0, 0].rearrange("(p h) s -> (h s) p", h=2), before[:, at, r],
                                 allow_slow_non_contiguous=True).then_inc(stored, 16)
                    n += 1
            sp.wait_ge(stored, 16 * n)

        @block.tensor
        def _(pe):
            pe.wait_ge(w_loaded, 16)
            for l in range(LB):
                if l >= 4:
                    pe.wait_ge(u_out, l - 3)
                for k in range(KD):
                    last = nc.tensor.matmul(ps[l % 4][:], g.h[:, k, l:SEQ:LB], w_u[:, k], start=k == 0, stop=k == KD - 1)
                last.then_inc(u_psum, 1)
            pe.wait_ge(u_out, LB - 3)
            for k in range(KD):
                last = nc.tensor.matmul(ps[0][0:DEC, :], g.h[:, k, SEQ:TOK], w_u[:, k], start=k == 0, stop=k == KD - 1)
            last.then_inc(u_psum, 1)
            pe.wait_ge(u_out, LB)
            pe.wait_ge(u_rows_in, 16 * LB)
            for q in range(GQ):
                if q >= 4:
                    pe.wait_ge(u_cols_done, q - 3)
                for a in range(2):
                    grp = 2 * q + a
                    nc.tensor.transpose(ps[4 + q % 4][:, NB * a:NB * a + NBP], space_p[:, P * grp:P * grp + P], g.ident[:])
                    last = nc.tensor.transpose(ps[4 + q % 4][:, NB * a + NBP:NB * a + NB], space_s[:, P * grp:P * grp + P],
                                               g.ident[0:NBS, 0:NBS])
                last.then_inc(u_turned, 1)
            for p in range(PAIRS):
                if p >= 4:
                    pe.wait_ge(v_done, p - 3)
                pe.wait_ge(u_cols_done, p + 1)
                for r in range(2):
                    for h in range(2):
                        last = nc.tensor.matmul(ps[p % 4][ST * h:ST * h + ST, NB * r:NB * r + NB],
                                                g.s5_b_cols[:, r, p, ST * h:ST * h + ST], u_cols[:, 2 * p + h],
                                                start=r == 0, stop=r == 1, skip_group_check=True)
                last.then_inc(v_psum, 1)
            pe.wait_ge(scan, 4 * NB)
            for q, (h, pair0) in enumerate(SETS):
                for s, (lo, hi, at) in enumerate(((0, NBP, 0), (NBP, NB, first_s))):
                    if q >= 2:
                        pe.wait_ge(y_done, 2 * (q - 2) + s + 1)
                    y = ps[4 + 2 * (q % 2) + s]
                    n = hi - lo
                    for a in range(4):
                        pair = pair0 + a
                        grp = 2 * pair + h
                        dst = y[0:n, P * a:P * a + P]
                        nc.tensor.matmul(dst, u_cols[:, grp, lo:hi], g.s5_toeplitz[:, grp].rearrange("p l c -> p (l c)"),
                                         start=a == 0, stop=False, skip_group_check=True)
                    for a in range(4):
                        pair = pair0 + a
                        dst = y[0:n, P * a:P * a + P]
                        rows = slice(ST * h, ST * h + ST)
                        for r in range(2):
                            last = nc.tensor.matmul(dst, before[rows, at:at + n, r, pair], g.s5_c_pow[rows, r, pair, 1:LB + 1, :],
                                                    start=False, stop=a == 3 and r == 1, skip_group_check=True)
                    last.then_inc(y_psum, 1)
            pe.wait_ge(y_done, 2 * len(SETS))
            n = 0
            for ct in range(KB):
                for q in range(3):
                    if n >= 4:
                        pe.wait_ge(y_cols_done, n - 3)
                    t = ps[n % 4]
                    if q < 2:
                        for a in range(4):
                            last = nc.tensor.transpose(t[:, P * a:P * a + P], blocks_p[:, 4 * q + a, P * ct:P * ct + P], g.ident[:])
                    else:
                        for a in range(LB):
                            last = nc.tensor.transpose(t[:, NBS * a:NBS * a + NBS], blocks_s[:, a, P * ct:P * ct + P],
                                                       g.ident[0:NBS, 0:NBS])
                    last.then_inc(y_turned, 1)
                    n += 1

        @block.scalar
        def _(act):
            for l in range(LB):
                act.wait_ge(u_psum, l + 1)
                nc.scalar.activation(u_p[:, :, l], ps[l % 4][:].rearrange("p (g c) -> p g c", c=GC), ACT.Copy).then_inc(u_out, 1)
            act.wait_ge(u_psum, LB + 1)
            nc.scalar.activation(u_rows_s[:], ps[0][0:DEC, :], ACT.Copy).then_inc(u_out, 1)
            for p in range(PAIRS):
                act.wait_ge(v_psum, p + 1)
                v = ps[p % 4][:, 0:2 * NB].rearrange("p (r n) -> p n r", r=2)
                nc.scalar.activation(before[:, 1:NBP + 1, :, p], v[:, 0:NBP], ACT.Copy)
                nc.scalar.activation(before[:, first_s + 1:first_s + 1 + NBS, :, p], v[:, NBP:NB], ACT.Copy).then_inc(v_done, 1)
            for q, (h, pair0) in enumerate(SETS):
                for s, (dst, n) in enumerate(((blocks_p, NBP), (blocks_s, NBS))):
                    act.wait_ge(y_psum, 2 * q + s + 1)
                    to = dst[0:n].rearrange("p l (g c) -> p g l c", c=GC)[:, groups_of(h, pair0)]
                    src = ps[4 + 2 * (q % 2) + s][0:n, :].rearrange("p (a l c) -> p a l c", a=4, c=GC)
                    for a in range(4):
                        last = nc.scalar.activation(to[:, a], src[:, a], ACT.Gelu_apprx_tanh)
                    last.then_inc(y_done, 1)

        @block.vector
        def _(dve):
            for q in range(GQ):
                dve.wait_ge(u_turned, q + 1)
                nc.vector.tensor_copy(u_cols[:, 2 * q:2 * q + 2],
                                      ps[4 + q % 4][:, 0:2 * NB].rearrange("p (a n) -> p a n", a=2)).then_inc(u_cols_done, 1)
            n = 0
            for ct in range(KB):
                for q in range(3):
                    dve.wait_ge(y_turned, n + 1)
                    t = ps[n % 4]
                    if q < 2:
                        to = g.s5_y[:, ct, 0:SEQ].rearrange("p (b l) -> p l b", l=LB)[:, 4 * q:4 * q + 4]
                        src = t[:].rearrange("p (l b) -> p l b", l=4)
                    else:
                        to = g.s5_y[:, ct, SEQ:TOK].rearrange("p (b l) -> p l b", l=LB)
                        src = t[:, 0:DEC].rearrange("p (l b) -> p l b", l=LB)
                    nc.vector.tensor_copy(to, src).then_inc(y_cols_done, 1)
                    n += 1

        @block.gpsimd
        def _(pool):
            pool.wait_ge(u_psum, LB + 1)
            nc.gpsimd.memset(before[:, 0], 0.0).then_inc(zero_state, 1)
            pool.wait_ge(zero_state, 1)
            pool.wait_ge(state_in, 32)
            pool.wait_ge(v_done, PAIRS)

            def ordered(count):
                pool.wait_ge(scan, count)
                pool.nop(nofuse=True)

            def advance(at, base, s):
                def h(n):
                    return before[:, bass.ds(n, 1)].rearrange("p o r a -> p (o r) a") if not isinstance(n, int) else before[:, n]
                now, nxt = h(at), h(at + 1)
                nc.gpsimd.tensor_tensor(prod[:, s, 0], now, g.s5_step[:, 0], ALU.mult).then_inc(scan, 1)
                nc.gpsimd.tensor_tensor(prod[:, s, 1, ::-1], now, g.s5_step[:, 1, ::-1], ALU.mult).then_inc(scan, 1)
                ordered(base + 2)
                nc.gpsimd.tensor_tensor(nxt, nxt, prod[:, s, 0], ALU.add).then_inc(scan, 1)
                ordered(base + 3)
                nc.gpsimd.tensor_tensor(nxt, nxt, prod[:, s, 1], ALU.add).then_inc(scan, 1)
                ordered(base + 4)

            for b in range(NBS):
                advance(first_s + b, 4 * b, 1)
            with pool.Fori(0, NBP // 4) as r:
                for b in range(4):
                    advance(r * 4 + b, r * 16 + (4 * b + 4 * NBS), 0)


def stage_glu(nc, g, d):
    with ExitStack() as ctx:
        w = ctx.enter_context(nc.sbuf_tensor("w_glu", [P, KB, BR], F32))
        bias = ctx.enter_context(nc.sbuf_tensor("b_glu", [P, KB], F32))
        gate = [ctx.enter_context(nc.sbuf_tensor(f"glu_gate{b}", [P, PW], F32)) for b in range(3)]
        loaded, psum, gate_done, used = (ctx.enter_context(nc.semaphore(f"glu_{n}")) for n in ("loaded", "psum", "gate_done", "used"))
        ps = [ctx.enter_context(nc.psum_tensor(f"glu_ps{b}", [P, 512], F32)) for b in range(3)]
        block = ctx.enter_context(nc.Block())
        jobs = [(j, n) for j in range(KB) for n in range(3)]

        @block.sync
        def _(sp):
            sp.dma_start(w[:], rows_view(d["w_glu"][0])).then_inc(loaded, 16)
            sp.dma_start(bias[:], d["b_glu"][0].rearrange("(k p) -> p k", p=P), allow_slow_non_contiguous=True).then_inc(loaded, 16)

        @block.tensor
        def _(pe):
            pe.wait_ge(loaded, 32)
            for q, (j, n) in enumerate(jobs):
                if q >= 3:
                    pe.wait_ge(gate_done, q - 2)
                at, width = PIECES[n]
                for k in range(KB):
                    last = nc.tensor.matmul(ps[n][:, 0:width], w[:, k, P * j:P * j + P], g.s5_y[:, k, at:at + width],
                                            start=k == 0, stop=k == KB - 1)
                last.then_inc(psum, 1)

        @block.scalar
        def _(act):
            act.wait_ge(loaded, 32)
            for q, (j, n) in enumerate(jobs):
                act.wait_ge(psum, q + 1)
                if q >= 3:
                    act.wait_ge(used, q - 2)
                width = PIECES[n][1]
                nc.scalar.activation(gate[n][:, 0:width], ps[n][:, 0:width], ACT.Sigmoid, bias=bias[:, j:j + 1]).then_inc(gate_done, 1)

        @block.vector
        def _(dve):
            for q, (j, n) in enumerate(jobs):
                dve.wait_ge(gate_done, q + 1)
                at, width = PIECES[n]
                nc.vector.tensor_tensor(g.branch[:, j, at:at + width], gate[n][:, 0:width], g.s5_y[:, j, at:at + width],
                                        ALU.mult).then_inc(used, 1)


def stage_merge(nc, g, d, name, index, first):
    with ExitStack() as ctx:
        w = [ctx.enter_context(nc.sbuf_tensor(f"{name}_merge_w{b}", [P, KD + KB, P], F32)) for b in range(2)]
        bias = ctx.enter_context(nc.sbuf_tensor(f"{name}_b_gate", [P, KD], F32))
        gate = [ctx.enter_context(nc.sbuf_tensor(f"{name}_gate{b}", [P, PW], F32)) for b in range(3)]

        def sem(what):
            return ctx.enter_context(nc.semaphore(f"{name}_{what}"))

        bias_loaded = sem("bias_loaded")
        w_loaded = [sem(f"merge_w_loaded{b}") for b in range(2)]
        gate_psum = sem("gate_psum")
        br_psum = sem("br_psum")
        gate_done = sem("gate_done")
        gated = sem("gated")
        added = sem("added")
        gate_ps = [ctx.enter_context(nc.psum_tensor(f"{name}_gate_ps{b}", [P, 512], F32)) for b in range(3)]
        br_ps = [ctx.enter_context(nc.psum_tensor(f"{name}_br_ps{b}", [P, 512], F32)) for b in range(3)]
        block = ctx.enter_context(nc.Block())
        w_gate = rows_view(d["w_gate"][0])
        w_br = rows_view(d[f"w_br_{name}"][0])

        def cols(j, base=0):
            return slice(base + P * j, base + P * j + P) if isinstance(j, int) else bass.ds(j * P + base, P)

        @block.sync
        def _(sp):
            sp.dma_start(bias[:], d["b_gate"][0].rearrange("(b k p) -> b p k", p=P, b=3)[index],
                         allow_slow_non_contiguous=True).then_inc(bias_loaded, 16)

            def load(j, b):
                sp.dma_start(w[b][:, 0:KD], w_gate[:, :, cols(j, D * index)]).then_inc(w_loaded[b], 16)
                sp.dma_start(w[b][:, KD:], w_br[:, :, cols(j)]).then_inc(w_loaded[b], 16)

            load(0, 0)
            load(1, 1)
            with sp.Fori(1, KD // 2) as r:
                for b in range(2):
                    sp.wait_ge(br_psum, r * 6 + (3 * b - 3))
                    load(r * 2 + b, b)

        @block.tensor
        def _(pe):
            def column(j, b, rounds, peeled):
                pe.wait_ge(w_loaded[b], rounds)
                for n, (at, width) in enumerate(PIECES):
                    if not peeled:
                        pe.wait_ge(gate_done, j * 3 + (n - 2))
                    for k in range(KD):
                        last = nc.tensor.matmul(gate_ps[n][:, 0:width], w[b][:, k], g.h[:, k, at:at + width],
                                                start=k == 0, stop=k == KD - 1)
                    last.then_inc(gate_psum, 1)
                    if not peeled:
                        pe.wait_ge(gated, j * 3 + (n - 2))
                    for k in range(KB):
                        last = nc.tensor.matmul(br_ps[n][:, 0:width], w[b][:, KD + k], g.branch[:, k, at:at + width],
                                                start=k == 0, stop=k == KB - 1)
                    last.then_inc(br_psum, 1)

            column(0, 0, 32, True)
            column(1, 1, 32, False)
            with pe.Fori(1, KD // 2) as r:
                for b in range(2):
                    column(r * 2 + b, b, r * 32 + 32, False)

        @block.scalar
        def _(act):
            act.wait_ge(bias_loaded, 16)
            for j in range(KD):
                for n, (at, width) in enumerate(PIECES):
                    act.wait_ge(gate_psum, 3 * j + n + 1)
                    if j:
                        act.wait_ge(gated, 3 * j + n - 2)
                    nc.scalar.activation(gate[n][:, 0:width], gate_ps[n][:, 0:width], ACT.Sigmoid,
                                         bias=bias[:, j:j + 1]).then_inc(gate_done, 1)

        @block.vector
        def _(dve):
            for j in range(KD):
                for n, (at, width) in enumerate(PIECES):
                    q = 3 * j + n
                    dve.wait_ge(gate_done, q + 1)
                    dve.wait_ge(br_psum, q + 1)
                    mix = g.mix[:, j, at:at + width]
                    if first:
                        nc.vector.tensor_tensor(mix, gate[n][:, 0:width], br_ps[n][:, 0:width], ALU.mult).then_inc(gated, 1)
                    else:
                        nc.vector.tensor_tensor(gate[n][:, 0:width], gate[n][:, 0:width], br_ps[n][:, 0:width], ALU.mult).then_inc(added, 1)
                        dve.wait_ge(added, q + 1)
                        nc.vector.tensor_tensor(mix, mix, gate[n][:, 0:width], ALU.add).then_inc(gated, 1)


def stage_gla_in(nc, g, d):
    with ExitStack() as ctx:
        w_qk = [ctx.enter_context(nc.sbuf_tensor(f"w_qk{b}", [P, KD, P], F32)) for b in range(4)]
        w_aa = ctx.enter_context(nc.sbuf_tensor("w_aa", [P, KD, LOWR], F32))
        w_vg = [ctx.enter_context(nc.sbuf_tensor(f"w_vg{b}", [P, KD, BR], F32)) for b in range(2)]
        loaded = [ctx.enter_context(nc.semaphore(f"gla_w_loaded{b}")) for b in range(7)]
        psum, out_done, pads = (ctx.enter_context(nc.semaphore(f"gla_in_{n}")) for n in ("psum", "out_done", "pads"))
        ps = [ctx.enter_context(nc.psum_tensor(f"gla_in_ps{b}", [P, 512], F32)) for b in range(4)]
        block = ctx.enter_context(nc.Block())
        w_in = rows_view(d["w_in"][0])
        jobs = [("t", j, n) for j in range(4) for n in range(3)] + [("a", 0, n) for n in range(3)] + \
               [("v", i, b) for b in range(2) for i in range(NT)]

        @block.sync
        def _(sp):
            for b in range(4):
                sp.dma_start(w_qk[b][:], w_in[:, :, P * b:P * b + P]).then_inc(loaded[b], 16)
            sp.dma_start(w_aa[:], w_in[:, :, COL["aa"]:COL["aa"] + LOWR]).then_inc(loaded[4], 16)
            for b, name in enumerate(("va", "ga")):
                sp.dma_start(w_vg[b][:], w_in[:, :, COL[name]:COL[name] + BR]).then_inc(loaded[5 + b], 16)

        @block.tensor
        def _(pe):
            for q, (kind, j, n) in enumerate(jobs):
                if q >= 4:
                    pe.wait_ge(out_done, q - 3)
                pe.wait_ge(loaded[{"t": j, "a": 4, "v": 5 + n}[kind]], 16)
                for k in range(KD):
                    if kind == "v":
                        out, lhs, rhs = ps[q % 4][:], g.h[:, k, P * j:P * j + P], w_vg[n][:, k]
                    else:
                        at, width = PIECES[n]
                        rows, lhs = (P, w_qk[j][:, k]) if kind == "t" else (LOWR, w_aa[:, k])
                        out, rhs = ps[q % 4][0:rows, 0:width], g.h[:, k, at:at + width]
                    last = nc.tensor.matmul(out, lhs, rhs, start=k == 0, stop=k == KD - 1)
                last.then_inc(psum, 1)

        @block.scalar
        def _(act):
            for q, (kind, j, n) in enumerate(jobs):
                act.wait_ge(psum, q + 1)
                if kind == "v":
                    dst, src = (g.gla_v, g.gla_gate)[n][:, j], ps[q % 4][:]
                else:
                    at, width = PIECES[n]
                    dst = g.gla_qk[:, j, at:at + width] if kind == "t" else g.gla_low[0:LOWR, at:at + width]
                    src = ps[q % 4][0:(P if kind == "t" else LOWR), 0:width]
                nc.scalar.activation(dst, src, ACT.Silu if kind == "v" and n else ACT.Copy).then_inc(out_done, 1)

        @block.gpsimd
        def _(pool):
            nc.gpsimd.memset(g.gla_qk[:, :, TOK:TP], 0.0).then_inc(pads, 1)


def stage_gla(nc, g, d, out):
    with ExitStack() as ctx:
        def sb(name, shape, dt=F32):
            return ctx.enter_context(nc.sbuf_tensor(name, shape, dt))

        def sem(name):
            return ctx.enter_context(nc.semaphore("gla_" + name))

        NCH = TP // CHUNK
        CHUNKS = SEQ // CHUNK + 1
        w_up = sb("w_alpha_up", [LOWR, 2 * P])
        b_alpha = sb("b_alpha", [P, 2])
        norm_col = sb("gla_norm_col", [P, 1])
        work = sb("gla_work", [P, 4 * TP])
        pre = work[:, 0:2 * TP].rearrange("p (a t) -> p a t", a=2)
        decay = work[:, 2 * TP:4 * TP].rearrange("p (a t) -> p a t", a=2)
        o_rows = work[:].rearrange("p (i c) -> p i c", i=NT)
        expo = sb("gla_expo", [P, 2, TP])
        resets = sb("gla_resets", [P, TP])
        gaps = sb("gla_gaps", [P, 2 * NCH])
        factors = sb("gla_factors", [P, 3, 2, NCH])
        k_rows = sb("gla_k_rows", [P, 2, 2 * P])
        att = sb("gla_att", [P, 2, HEADS, P])
        state = [sb(f"gla_state{b}", [P, 2, DV]) for b in range(2)]
        state_mid = sb("gla_state_mid", [P, 2, 2, DV])
        o_sq = sb("gla_o_sq", [P, DV])
        ssq = sb("gla_ssq", [P, NT * HEADS])
        std = sb("gla_std", [P, NT * HEADS])

        loaded, pads, pre_psum, pre_done, soft, rel_done, exp_done, q_done, k_done, factors_done = (sem(n) for n in (
            "loaded pads pre_psum pre_done soft rel_done exp_done q_done k_done factors_done").split())
        k_turned, k_rows_done, att_psum, att_done, ds_psum, mid_done, scaled, state_done = (sem(n) for n in (
            "k_turned k_rows_done att_psum att_done ds_psum mid_done scaled state_done").split())
        o_psum, o_done, ssq_done, std_done, rstd_done, gated, o_turned, branch_done, stored, step = (sem(n) for n in (
            "o_psum o_done ssq_done std_done rstd_done gated o_turned branch_done stored step").split())
        ps = [ctx.enter_context(nc.psum_tensor(f"gla_ps{b}", [P, 512], F32)) for b in range(8)]
        block = ctx.enter_context(nc.Block())
        q_all, k_all = g.gla_qk[:, 0:2], g.gla_qk[:, 2:4]
        PRE = [(j, n) for j in range(2) for n in range(3)]

        def chunked(t):
            return t.rearrange("p a (n c) -> p (a n) c", c=CHUNK)

        def flat(t):
            return t.rearrange("p a t -> p (a t)")

        def chunks_of(i):
            return (0, 1) if i < NT - 1 else (0,)

        def pair_of(bank):
            return bank[:, 0:2 * P].rearrange("p (a v) -> p a v", a=2)

        @block.sync
        def _(sp):
            sp.dma_start(w_up[:], d["w_alpha_up"][0]).then_inc(loaded, 16)
            sp.dma_start(b_alpha[:], d["b_alpha"][0].rearrange("(k p) -> p k", p=P), allow_slow_non_contiguous=True).then_inc(loaded, 16)
            sp.dma_start(norm_col[:], d["gla_norm_w"][0].rearrange("(p o) -> p o", o=1), allow_slow_non_contiguous=True).then_inc(loaded, 16)
            sp.dma_start(state[1][:], d["state_gla"][0, 0].rearrange("(a h) s v -> (h s) a v", h=2)).then_inc(loaded, 16)
            for who, chunks in enumerate((CHUNKS - 1, CHUNKS)):
                sp.wait_ge(state_done, chunks)
                sp.dma_start(out["gla"][who][0, 0].rearrange("(a h) s v -> (h s) a v", h=2), state[who][:]).then_inc(stored, 16)
            sp.wait_ge(stored, 32)

        @block.gpsimd
        def _(pool):
            nc.gpsimd.memset(resets[:], 1.0).then_inc(pads, 1)
            pool.wait_ge(pads, 1)
            nc.gpsimd.memset(resets[:, 0:TP:CHUNK], 0.0).then_inc(pads, 1)
            pool.wait_ge(pads, 2)
            nc.gpsimd.memset(pre[:, :, TOK:TP], 0.0).then_inc(pads, 1)
            pool.wait_ge(pads, 3)
            nc.gpsimd.memset(state[0][:], 0.0).then_inc(pads, 1)

        @block.scalar
        def _(act):
            act.wait_ge(loaded, 64)
            for q, (j, n) in enumerate(PRE):
                at, width = PIECES[n]
                act.wait_ge(pre_psum, q + 1)
                nc.scalar.activation(pre[:, j, at:at + width], ps[q][:, 0:width], ACT.Identity,
                                     bias=b_alpha[:, j:j + 1]).then_inc(pre_done, 1)
            act.wait_ge(pre_done, len(PRE))
            act.wait_ge(pads, 4)
            nc.scalar.activation(expo[:], pre, ACT.Abs).then_inc(soft, 1)
            act.wait_ge(soft, 1)
            nc.scalar.activation(expo[:], expo[:], ACT.Exp, scale=-1.0).then_inc(soft, 1)
            act.wait_ge(soft, 2)
            nc.scalar.activation(expo[:], expo[:], ACT.Ln, bias=1.0).then_inc(soft, 1)
            act.wait_ge(rel_done, 2)
            nc.scalar.activation(expo[:], pre, ACT.Exp, scale=1.0 / TAU).then_inc(exp_done, 1)
            for f, src in enumerate((chunked(decay)[:, :, 31], chunked(decay)[:, :, 63], gaps[:])):
                nc.scalar.activation(factors[:, f].rearrange("p a n -> p (a n)"), src, ACT.Exp, scale=1.0 / TAU).then_inc(factors_done, 1)
            act.wait_ge(q_done, 1)
            nc.scalar.activation(expo[:], pre, ACT.Exp, scale=-1.0 / TAU).then_inc(exp_done, 1)

            def unload_o(i):
                act.wait_ge(o_psum, i + 1)
                for half in range(2):
                    for a in range(2):
                        h = 2 * a + half
                        if i or half or a:
                            act.wait_ge(ssq_done, HEADS * i + 2 * half + a)
                        nc.scalar.activation(o_sq[:], ps[6 + half][:, DV * a:DV * a + DV], ACT.Square,
                                             accum_out=ssq[:, HEADS * i + h:HEADS * i + h + 1]).then_inc(ssq_done, 1)
                    nc.scalar.activation(o_rows[:, i].rearrange("p (a h v) -> p h a v", a=2, h=2)[:, half], pair_of(ps[6 + half]),
                                         ACT.Copy).then_inc(o_done, 1)

            for i in range(NT):
                act.wait_ge(k_turned, i + 1)
                if i >= 2:
                    act.wait_ge(ds_psum, 2 * (i - 1))
                nc.scalar.activation(k_rows[:, i % 2], ps[i % 2][:, 0:2 * P], ACT.Copy).then_inc(k_rows_done, 1)
                if i:
                    unload_o(i - 1)
            unload_o(NT - 1)
            act.wait_ge(ssq_done, NT * HEADS)
            nc.scalar.activation(std[:], ssq[:], ACT.Sqrt, scale=1.0 / DV, bias=g.eps[:]).then_inc(std_done, 1)
            for i in range(NT):
                n = P if i < NT - 1 else DEC
                act.wait_ge(o_turned, i + 1)
                nc.scalar.activation(g.branch[:, :, P * i:P * i + n], ps[i % 4][:].rearrange("p (h t) -> p h t", h=HEADS)[:, :, 0:n],
                                     ACT.Copy, scale=norm_col[:, 0:1]).then_inc(branch_done, 1)

        @block.vector
        def _(dve):
            dve.wait_ge(soft, 3)
            nc.vector.scalar_tensor_tensor(flat(pre), flat(pre), 0.0, flat(expo[:]), ALU.min, ALU.subtract).then_inc(step, 1)
            dve.wait_ge(step, 1)
            for a in range(2):
                nc.vector.tensor_tensor_scan(decay[:, a], resets[:], pre[:, a], 0.0, ALU.mult, ALU.add).then_inc(step, 1)
            dve.wait_ge(step, 3)
            mid = chunked(decay)[:, :, 31:32]
            nc.vector.tensor_tensor(chunked(pre), chunked(decay), mid.broadcast_to([P, 2 * NCH, CHUNK]), ALU.subtract).then_inc(rel_done, 1)
            nc.vector.tensor_tensor(gaps[:], chunked(decay)[:, :, 63], chunked(decay)[:, :, 31], ALU.subtract).then_inc(rel_done, 1)
            dve.wait_ge(exp_done, 1)
            nc.vector.scalar_tensor_tensor(flat(q_all), flat(q_all), GDK ** -0.5, flat(expo[:]), ALU.mult, ALU.mult).then_inc(q_done, 1)
            dve.wait_ge(exp_done, 2)
            nc.vector.tensor_tensor(flat(k_all), flat(k_all), flat(expo[:]), ALU.mult).then_inc(k_done, 1)
            dve.wait_ge(factors_done, 3)
            for i in range(NT):
                for half in range(2):
                    dve.wait_ge(att_psum, 2 * i + half + 1)
                    if i >= 2 and half == 0:
                        dve.wait_ge(o_psum, i - 1)
                    nc.vector.tensor_tensor(att[:, i % 2, half::2], pair_of(ps[2 + half]), g.upto[:].unsqueeze(1).broadcast_to([P, 2, P]),
                                            ALU.mult).then_inc(att_done, 1)
                for c in chunks_of(i):
                    n = 2 * i + c
                    s = state[0] if i < NT - 1 else state[1]
                    if i:
                        dve.wait_ge(o_psum, i)
                    if n:
                        dve.wait_ge(state_done, n)
                    for a in range(2):
                        last = nc.vector.tensor_scalar(state_mid[:, c, a], s[:, a], factors[:, 0, a, n:n + 1], None, ALU.mult)
                    last.then_inc(mid_done, 1)
                    dve.wait_ge(mid_done, n + 1)
                    for a in range(2):
                        last = nc.vector.tensor_scalar(s[:, a], s[:, a], factors[:, 1, a, n:n + 1], None, ALU.mult)
                    last.then_inc(scaled, 1)
                    dve.wait_ge(scaled, n + 1)
                    dve.wait_ge(ds_psum, n + 1)
                    for a in range(2):
                        last = nc.vector.scalar_tensor_tensor(s[:, a], ps[4 + c][:, DV * a:DV * a + DV], factors[:, 2, a, n:n + 1], s[:, a],
                                                              ALU.mult, ALU.add)
                    last.then_inc(state_done, 1)
            dve.wait_ge(std_done, 1)
            nc.vector.reciprocal(std[:], std[:]).then_inc(rstd_done, 1)
            dve.wait_ge(rstd_done, 1)
            dve.wait_ge(o_done, 2 * NT)
            for i in range(NT):
                for h in range(HEADS):
                    o = o_rows[:, i, DV * h:DV * h + DV]
                    last = nc.vector.scalar_tensor_tensor(o, o, std[:, HEADS * i + h:HEADS * i + h + 1], g.gla_gate[:, i, DV * h:DV * h + DV],
                                                          ALU.mult, ALU.mult)
                last.then_inc(gated, 1)

        @block.tensor
        def _(pe):
            pe.wait_ge(loaded, 64)
            for q, (j, n) in enumerate(PRE):
                at, width = PIECES[n]
                nc.tensor.matmul(ps[q][:, 0:width], w_up[:, P * j:P * j + P], g.gla_low[:, at:at + width],
                                 start=True, stop=True).then_inc(pre_psum, 1)
            pe.wait_ge(pre_done, len(PRE))
            pe.wait_ge(q_done, 1)
            pe.wait_ge(k_done, 1)
            for i in range(NT):
                b = i % 2
                tile = slice(P * i, P * i + P)
                if i >= 2:
                    pe.wait_ge(k_rows_done, i - 1)
                for a in range(2):
                    last = nc.tensor.transpose(ps[b][:, P * a:P * a + P], k_all[:, a, tile], g.ident[:])
                last.then_inc(k_turned, 1)
                if i:
                    pe.wait_ge(att_done, 2 * i)
                for half in range(2):
                    rows = slice(GDK * half, GDK * half + GDK)
                    for a in range(2):
                        last = nc.tensor.matmul(ps[2 + half][:, P * a:P * a + P], k_all[rows, a, tile], q_all[rows, a, tile],
                                                start=a == 0, stop=a == 1, skip_group_check=True)
                    last.then_inc(att_psum, 1)
                pe.wait_ge(k_rows_done, i + 1)
                for c in chunks_of(i):
                    if i:
                        pe.wait_ge(state_done, 2 * i + c - 1)
                    tok = slice(CHUNK * c, CHUNK * c + CHUNK)
                    for a in range(2):
                        for half in range(2):
                            h = 2 * a + half
                            last = nc.tensor.matmul(ps[4 + c][GDK * half:GDK * half + GDK, DV * a:DV * a + DV],
                                                    k_rows[tok, b, GDK * h:GDK * h + GDK], g.gla_v[tok, i, DV * h:DV * h + DV],
                                                    start=a == 0, stop=a == 1, skip_group_check=True)
                    last.then_inc(ds_psum, 1)
                pe.wait_ge(att_done, 2 * i + 2)
                if i:
                    pe.wait_ge(o_done, 2 * i)
                for h in range(HEADS):
                    a, half = h // 2, h % 2
                    nc.tensor.matmul(ps[6 + half][:, DV * a:DV * a + DV], att[:, b, h], g.gla_v[:, i, DV * h:DV * h + DV],
                                     start=a == 0, stop=False, skip_group_check=True)
                for c in chunks_of(i):
                    pe.wait_ge(mid_done, 2 * i + c + 1)
                    for h in range(HEADS):
                        a, half = h // 2, h % 2
                        rows = slice(GDK * half, GDK * half + GDK)
                        last = nc.tensor.matmul(ps[6 + half][CHUNK * c:CHUNK * c + CHUNK, DV * a:DV * a + DV],
                                                q_all[rows, a, P * i + CHUNK * c:P * i + CHUNK * c + CHUNK], state_mid[rows, c, a],
                                                start=False, stop=True, skip_group_check=True)
                last.then_inc(o_psum, 1)
            for i in range(NT):
                n = P if i < NT - 1 else DEC
                pe.wait_ge(gated, i + 1)
                if i >= 4:
                    pe.wait_ge(branch_done, i - 3)
                for h in range(HEADS):
                    last = nc.tensor.transpose(ps[i % 4][:, P * h:P * h + n], o_rows[0:n, i, DV * h:DV * h + DV], g.ident[0:n, 0:n])
                last.then_inc(o_turned, 1)


def stage_gdn_in(nc, g, d, out):
    with ExitStack() as ctx:
        def sb(name, shape, dt=F32):
            return ctx.enter_context(nc.sbuf_tensor("cv_" + name, shape, dt))

        def sem(name):
            return ctx.enter_context(nc.semaphore("cv_" + name))

        S0 = SEQ + 2 * (CW - 1)
        RAW = S0 + DEC
        RUN = RAW - (CW - 1)
        w = sb("w", [P, 2, KD, P])
        w_ba = sb("w_ba", [P, KD, 2 * HEADS])
        raw = sb("raw", [P, 2, RAW])
        acc = sb("acc", [P, 2, RUN])
        v_cols = sb("v_cols", [P, 2, TP])
        taps = sb("taps", [P, NCV, CW])
        history = sb("history", [P, NCV, CW - 1])
        tails = sb("tails", [P, NCV, 2, CW - 1])
        ba_cols = sb("ba_cols", [2 * HEADS, TP])
        squares = v_cols
        inv = acc

        loaded, ba_loaded, psum, raw_done, pads, edges, conv, silu_done, v_turned, v_done = (sem(n) for n in (
            "loaded ba_loaded psum raw_done pads edges conv silu_done v_turned v_done").split())
        w_loaded = [sem(f"w_loaded{b}") for b in range(2)]
        ba_psum, ba_out, ba_turned, ba_done, sq_done, sq_psum, root_done, inv_done, unit_done, stored, tails_done = (sem(n) for n in (
            "ba_psum ba_out ba_turned ba_done sq_done sq_psum root_done inv_done unit_done stored tails_done").split())
        ps = [ctx.enter_context(nc.psum_tensor(f"cv_ps{b}", [P, 512], F32)) for b in range(8)]
        block = ctx.enter_context(nc.Block())
        w_in = rows_view(d["w_in"][0])
        V0 = 2 * HEADS

        def root(act, j):
            for n, (at, width) in enumerate(PIECES):
                act.wait_ge(sq_psum, 3 * j + n + 1)
                if j >= 2:
                    act.wait_ge(unit_done, j - 1)
                nc.scalar.activation(inv[:, j % 2, at:at + width], ps[n][:, 0:width], ACT.Sqrt, bias=g.eps[:]).then_inc(root_done, 1)

        def out_v(dve, j):
            for q in range(3):
                dve.wait_ge(v_turned, 3 * (j - V0) + q + 1)
                h = j - V0
                nc.vector.tensor_copy(g.gdn_v[:, 3 * q:3 * q + 3, DV * h:DV * h + DV],
                                      ps[3 + q][:, 0:3 * P].rearrange("p (i v) -> p i v", i=3)).then_inc(v_done, 1)

        @block.sync
        def _(sp):
            for t in range(CW):
                sp.dma_start(taps[:, :, t], d["conv_w"][0, t].rearrange("(k p) -> p k", p=P), allow_slow_non_contiguous=True).then_inc(loaded, 16)
            for t in range(CW - 1):
                sp.dma_start(history[:, :, t], d["cache_gdn_conv"][0, 0, t].rearrange("(k p) -> p k", p=P),
                             allow_slow_non_contiguous=True).then_inc(loaded, 16)
            sp.dma_start(w_ba[:], w_in[:, :, COL["beta"]:COL["beta"] + 2 * HEADS]).then_inc(ba_loaded, 16)
            for j in range(NCV):
                if j >= 2:
                    sp.wait_ge(psum, 3 * (j - 1))
                sp.dma_start(w[:, j % 2], w_in[:, :, COL["qkv"] + P * j:COL["qkv"] + P * j + P]).then_inc(w_loaded[j % 2], 16)
            sp.wait_ge(tails_done, NCV)
            for who in range(2):
                for t in range(CW - 1):
                    sp.dma_start(out["conv"][who][0, 0, t].rearrange("(k p) -> p k", p=P), tails[:, :, who, t],
                                 allow_slow_non_contiguous=True).then_inc(stored, 16)
            sp.wait_ge(stored, 16 * 2 * (CW - 1))

        @block.gpsimd
        def _(pool):
            for n, t in enumerate((v_cols[:, :, TOK:TP], g.gdn_qk[:, :, TOK:TP], ba_cols[:, TOK:TP], raw[:, :, 0:CW - 1])):
                if n:
                    pool.wait_ge(pads, n)
                nc.gpsimd.memset(t, 0.0).then_inc(pads, 1)
            pool.wait_ge(pads, 4)
            pool.wait_ge(loaded, 16 * (2 * CW - 1))
            for j in range(NCV):
                if j >= 2:
                    pool.wait_ge(conv, CW * (j - 1))
                    pool.wait_ge(tails_done, j - 1)
                if j:
                    pool.wait_ge(edges, j)
                nc.gpsimd.tensor_copy(raw[:, j % 2, SEQ + CW - 1:S0], history[:, j]).then_inc(edges, 1)
                pool.wait_ge(raw_done, 4 * (j + 1))
                src = raw[:, j % 2, SEQ:SEQ + CW - 1]
                pool.wait_ge(edges, j + 1)
                nc.gpsimd.tensor_copy(tails[:, j, 0], src)
                nc.gpsimd.tensor_copy(tails[:, j, 1], raw[:, j % 2, RAW - CW + 1:RAW]).then_inc(tails_done, 1)

        @block.tensor
        def _(pe):
            def turn_v(j):
                pe.wait_ge(silu_done, 2 * (j + 1))
                if j == V0:
                    pe.wait_ge(pads, 4)
                for q in range(3):
                    n = 3 * (j - V0) + q
                    if n >= 3:
                        pe.wait_ge(v_done, n - 2)
                    for a in range(3):
                        i = 3 * q + a
                        last = nc.tensor.transpose(ps[3 + q][:, P * a:P * a + P], v_cols[:, j % 2, P * i:P * i + P], g.ident[:])
                    last.then_inc(v_turned, 1)

            for j in range(NCV):
                pe.wait_ge(w_loaded[j % 2], 16 * (j // 2 + 1))
                for n, (at, width) in enumerate(PIECES):
                    if j:
                        pe.wait_ge(raw_done, 4 * (j - 1) + n + (2 if n == 2 else 1))
                    for k in range(KD):
                        last = nc.tensor.matmul(ps[n][:, 0:width], w[:, j % 2, k], g.h[:, k, at:at + width], start=k == 0, stop=k == KD - 1)
                    last.then_inc(psum, 1)
                if j > V0:
                    turn_v(j - 1)
            pe.wait_ge(ba_loaded, 16)
            for n, (at, width) in enumerate(PIECES):
                pe.wait_ge(raw_done, 4 * (NCV - 1) + n + (2 if n == 2 else 1))
                for k in range(KD):
                    last = nc.tensor.matmul(ps[n][0:2 * HEADS, 0:width], w_ba[:, k], g.h[:, k, at:at + width], start=k == 0, stop=k == KD - 1)
                last.then_inc(ba_psum, 1)
            turn_v(NCV - 1)
            pe.wait_ge(ba_out, 3)
            for i in range(NT):
                last = nc.tensor.transpose(ps[7][:, 2 * HEADS * i:2 * HEADS * i + 2 * HEADS], ba_cols[:, P * i:P * i + P],
                                           g.ident[0:2 * HEADS, 0:2 * HEADS])
            last.then_inc(ba_turned, 1)
            for j in range(V0):
                pe.wait_ge(sq_done, j + 1)
                for n, (at, width) in enumerate(PIECES):
                    if j:
                        pe.wait_ge(root_done, 3 * (j - 1) + n + 1)
                    nc.tensor.matmul(ps[n][:, 0:width], g.ones[:], squares[:, j % 2, at:at + width], start=True, stop=True).then_inc(sq_psum, 1)

        @block.scalar
        def _(act):
            def silu(j):
                act.wait_ge(conv, CW * (j + 1))
                dst = g.gdn_qk[:, j] if j < V0 else v_cols[:, j % 2]
                if j >= V0 + 2:
                    act.wait_ge(v_turned, 3 * (j - 1 - V0))
                nc.scalar.activation(dst[:, 0:SEQ], acc[:, j % 2, 0:SEQ], ACT.Silu).then_inc(silu_done, 1)
                nc.scalar.activation(dst[:, SEQ:TOK], acc[:, j % 2, SEQ + CW - 1:RUN], ACT.Silu).then_inc(silu_done, 1)

            for j in range(NCV):
                if j >= 2:
                    act.wait_ge(conv, CW * (j - 1))
                    act.wait_ge(tails_done, j - 1)
                for n, (at, width) in enumerate(PIECES):
                    act.wait_ge(psum, 3 * j + n + 1)
                    end = min(at + width, SEQ)
                    nc.scalar.activation(raw[:, j % 2, CW - 1 + at:CW - 1 + end], ps[n][:, 0:end - at], ACT.Copy).then_inc(raw_done, 1)
                nc.scalar.activation(raw[:, j % 2, S0:RAW], ps[2][:, width - DEC:width], ACT.Copy).then_inc(raw_done, 1)
                if j:
                    silu(j - 1)
            silu(NCV - 1)
            for n, (at, width) in enumerate(PIECES):
                act.wait_ge(ba_psum, n + 1)
                nc.scalar.activation(ba_cols[:, at:at + width], ps[n][0:2 * HEADS, 0:width], ACT.Copy).then_inc(ba_out, 1)
            act.wait_ge(v_turned, 12)
            for j in range(V0):
                if j >= 2:
                    act.wait_ge(sq_psum, 3 * (j - 1))
                nc.scalar.activation(squares[:, j % 2, 0:TOK], g.gdn_qk[:, j, 0:TOK], ACT.Square).then_inc(sq_done, 1)
                if j >= 1:
                    root(act, j - 1)
            root(act, V0 - 1)

        @block.vector
        def _(dve):
            for j in range(NCV):
                dve.wait_ge(raw_done, 4 * (j + 1))
                dve.wait_ge(edges, j + 1)
                dve.wait_ge(pads, 4)
                if j >= 2:
                    dve.wait_ge(silu_done, 2 * (j - 1))
                a = acc[:, j % 2]
                nc.vector.tensor_scalar(a, raw[:, j % 2, 0:RUN], taps[:, j, 0:1], None, ALU.mult).then_inc(conv, 1)
                for t in range(1, CW):
                    dve.wait_ge(conv, CW * j + t)
                    nc.vector.scalar_tensor_tensor(a, raw[:, j % 2, t:t + RUN], taps[:, j, t:t + 1], a, ALU.mult, ALU.add).then_inc(conv, 1)
                if j > V0:
                    out_v(dve, j - 1)
            out_v(dve, NCV - 1)
            dve.wait_ge(ba_turned, 1)
            nc.vector.tensor_copy(g.gdn_ba[:], ps[7][:, 0:NT * 2 * HEADS].rearrange("p (i c) -> p i c", i=NT)).then_inc(ba_done, 1)
            for j in range(V0):
                dve.wait_ge(root_done, 3 * (j + 1))
                r = inv[:, j % 2, 0:TOK]
                nc.vector.reciprocal(r, r).then_inc(inv_done, 1)
                dve.wait_ge(inv_done, j + 1)
                x = g.gdn_qk[:, j, 0:TOK]
                nc.vector.scalar_tensor_tensor(x, x, DV ** -0.5 if j < HEADS else 1.0, r, ALU.mult, ALU.mult).then_inc(unit_done, 1)


def stage_gdn(nc, g, d, out):
    with ExitStack() as ctx:
        def sb(name, shape=(P, HEADS, P)):
            return ctx.enter_context(nc.sbuf_tensor("gd_" + name, list(shape), F32))

        def sem(name):
            return ctx.enter_context(nc.semaphore("gd_" + name))

        NG_ = NT * HEADS
        blocks = sb("blocks", [P, 4, P])
        rate = sb("rate", [P, HEADS])
        dt_bias = sb("dt_bias", [P, HEADS])
        beta = sb("beta", [P, NT, HEADS])
        log_g = sb("log_g", [P, NT, HEADS])
        soft = sb("soft", [P, NT, HEADS])
        grow = sb("grow", [P, 4, NT, HEADS])
        beta_grow = sb("beta_grow", [P, NT, HEADS])
        k_in = sb("k_in")
        k_out = [sb(f"k_out{b}") for b in range(2)]
        v_in = [sb(f"v_in{b}") for b in range(2)]
        att = [sb(f"att{b}") for b in range(2)]
        solve_t = [sb(f"solve_t{b}") for b in range(2)]
        wk = [sb(f"wk{b}") for b in range(2)]
        slot = [sb(f"slot{b}") for b in range(4)]
        steps, power2 = slot[0], slot[0]
        decay_t, power2_t = slot[1], slot[1]
        decay, power4 = slot[2], slot[2]
        a_mat, joint = slot[3], slot[3]
        x = [sb(f"x{b}") for b in range(2)]
        xt = [sb(f"xt{b}") for b in range(2)]
        between = [sb(f"between{b}") for b in range(3)]
        u = sb("u")
        q_state = sb("q_state")
        state = [sb(f"state{b}") for b in range(2)]

        names = ("loaded masks rate_done sig_done soft_done step g_done pre_psum grow_done bg_done "
                 "kt_psum k_in k_out v_in steps dec_psum dec_exp dec_mask kk_psum qk_psum a att at_psum dt between d x1 x1t "
                 "p2_psum p2 p4_psum p4 x2_psum x2 x3_psum x3 p16_psum p16 x4_psum x4 p32_psum p32 x5_psum x5 p64_psum p64 x6_psum x6 "
                 "wk_psum wk u_psum qs_psum u_out ds_psum state o_psum qs_out o_out stored state_in").split()
        S = {n: sem(n) for n in names}
        ps = [ctx.enter_context(nc.psum_tensor(f"gd_ps{b}", [P, HEADS, P], F32)) for b in range(8)]
        block = ctx.enter_context(nc.Block())
        q_all, k_all = g.gdn_qk[:, 0:HEADS], g.gdn_qk[:, HEADS:2 * HEADS]

        def heads(mask):
            return mask.unsqueeze(1).broadcast_to([P, HEADS, P])

        def per_head(cols, n=P):
            return cols.unsqueeze(2).broadcast_to([n, HEADS, P])

        def tile(i):
            return slice(P * i, P * i + P)

        def chunks_of(i):
            return (0, 1) if i < NT - 1 else (0,)

        def rows(c):
            return slice(CHUNK * c, CHUNK * c + CHUNK)

        @block.sync
        def _(sp):
            sp.dma_start(rate[:], d["gdn_a_log"].broadcast_to([P, HEADS]), allow_slow_non_contiguous=True).then_inc(S["loaded"], 16)
            sp.dma_start(dt_bias[:], d["gdn_dt_bias"].broadcast_to([P, HEADS]), allow_slow_non_contiguous=True).then_inc(S["loaded"], 16)
            sp.wait_ge(S["state"], 16)
            sp.dma_start(out["gdn"][0][0, 0].rearrange("h k v -> k h v"), state[0][:]).then_inc(S["stored"], 16)
            sp.wait_ge(S["stored"], 16)
            sp.dma_start(state[0][:], d["state_gdn"][0, 0].rearrange("h k v -> k h v")).then_inc(S["state_in"], 16)
            sp.wait_ge(S["state"], 17)
            sp.dma_start(out["gdn"][1][0, 0].rearrange("h k v -> k h v"), state[1][:]).then_inc(S["stored"], 16)
            sp.wait_ge(S["stored"], 32)

        @block.gpsimd
        def _(pool):
            n = 0

            def done(ins):
                nonlocal n
                ins.then_inc(S["masks"], 1)
                n += 1
                pool.wait_ge(S["masks"], n)

            done(nc.gpsimd.memset(blocks[:], 1.0))
            for m in range(4):
                size = 8 << m
                view = blocks[:, m].rearrange("p (a b) -> p a b", b=size)
                for base, step, cm in ((0, -size, 1), (size - 1, size, -1)):
                    done(nc.gpsimd.affine_select(out=view, in_=view, compare_op=ALU.is_ge, fill=0.0, base=base,
                                                 pattern=[[step, P // size], [0, size]], channel_multiplier=cm))
            for m in (3, 2, 1):
                done(nc.gpsimd.tensor_tensor(blocks[:, m], blocks[:, m], blocks[:, m - 1], ALU.subtract))
            done(nc.gpsimd.memset(state[0][:], 0.0))
            pool.wait_ge(S["g_done"], 1)
            for i in range(NT):
                b = i % 2
                if i >= 2:
                    pool.wait_ge(S["u_psum"], 2 * (i - 1))
                nc.gpsimd.tensor_tensor(v_in[b][:], g.gdn_v[:, i].rearrange("p (h v) -> p h v", h=HEADS), per_head(beta[:, i]),
                                        ALU.mult).then_inc(S["v_in"], 1)
                if i:
                    pool.wait_ge(S["x3_psum"], 2 * i)
                nc.gpsimd.tensor_tensor(steps[:], heads(g.after[:]), per_head(log_g[:, i]), ALU.mult).then_inc(S["steps"], 1)
                pool.wait_ge(S["dec_exp"], 2 * i + 1)
                nc.gpsimd.tensor_tensor(decay_t[:], decay_t[:], heads(g.upto[:]), ALU.mult).then_inc(S["dec_mask"], 1)
                pool.wait_ge(S["dec_exp"], 2 * i + 2)
                nc.gpsimd.tensor_tensor(decay[:], decay[:], heads(g.after[:]), ALU.mult).then_inc(S["dec_mask"], 1)
                pool.wait_ge(S["a"], i + 1)
                nc.gpsimd.tensor_tensor(x[1][:], a_mat[:], heads(blocks[:, 0]), ALU.mult).then_inc(S["d"], 1)
                pool.wait_ge(S["d"], i + 1)
                nc.gpsimd.tensor_tensor(x[0][:], heads(g.ident[:]), x[1][:], ALU.subtract).then_inc(S["x1"], 1)

        @block.scalar
        def _(act):
            act.wait_ge(S["loaded"], 32)
            nc.scalar.activation(rate[:], rate[:], ACT.Exp).then_inc(S["rate_done"], 1)
            nc.scalar.activation(beta[:], g.gdn_ba[:, :, 0:HEADS], ACT.Sigmoid).then_inc(S["sig_done"], 1)
            act.wait_ge(S["step"], 1)
            nc.scalar.activation(soft[:], log_g[:], ACT.Abs).then_inc(S["soft_done"], 1)
            act.wait_ge(S["soft_done"], 1)
            nc.scalar.activation(soft[:], soft[:], ACT.Exp, scale=-1.0).then_inc(S["soft_done"], 1)
            act.wait_ge(S["soft_done"], 2)
            nc.scalar.activation(soft[:], soft[:], ACT.Ln, bias=1.0).then_inc(S["soft_done"], 1)
            act.wait_ge(S["pre_psum"], 1)
            nc.scalar.activation(grow[:].rearrange("p a i h -> p (a i h)"), ps[0][:].rearrange("p h t -> p (h t)")[:, 0:4 * NG_],
                                 ACT.Exp).then_inc(S["grow_done"], 1)
            for i in range(NT):
                b = i % 2
                act.wait_ge(S["dec_psum"], 2 * i + 1)
                if i:
                    act.wait_ge(S["x2_psum"], 2 * i)
                nc.scalar.activation(decay_t[:], ps[1][:], ACT.Exp).then_inc(S["dec_exp"], 1)
                act.wait_ge(S["dec_psum"], 2 * i + 2)
                if i:
                    act.wait_ge(S["x3_psum"], 2 * i)
                nc.scalar.activation(decay[:], ps[2][:], ACT.Exp).then_inc(S["dec_exp"], 1)
                for r, (to, bank) in enumerate(((power2, 2), (power2_t, 3))):
                    act.wait_ge(S["p2_psum"], 2 * i + r + 1)
                    nc.scalar.activation(to[:], ps[bank][:], ACT.Copy).then_inc(S["p2"], 1)
                act.wait_ge(S["p4_psum"], i + 1)
                nc.scalar.activation(power4[:], ps[0][:], ACT.Copy).then_inc(S["p4"], 1)
                for name, bank in (("p16", 1), ("p32", 0), ("p64", 3)):
                    act.wait_ge(S[name + "_psum"], i + 1)
                    nc.scalar.activation(joint[:], ps[bank][:], ACT.Copy).then_inc(S[name], 1)
                act.wait_ge(S["wk_psum"], i + 1)
                nc.scalar.activation(wk[b][:], ps[1][:], ACT.Copy, scale=-1.0).then_inc(S["wk"], 1)

        @block.vector
        def _(dve):
            dve.wait_ge(S["loaded"], 32)
            nc.vector.tensor_tensor(log_g[:], g.gdn_ba[:, :, HEADS:], dt_bias[:].unsqueeze(1).broadcast_to([P, NT, HEADS]),
                                    ALU.add).then_inc(S["step"], 1)
            dve.wait_ge(S["soft_done"], 3)
            nc.vector.scalar_tensor_tensor(log_g[:], log_g[:], 0.0, soft[:], ALU.max, ALU.add).then_inc(S["step"], 1)
            dve.wait_ge(S["step"], 2)
            dve.wait_ge(S["rate_done"], 1)
            nc.vector.scalar_tensor_tensor(log_g[:], log_g[:], -1.0, rate[:].unsqueeze(1).broadcast_to([P, NT, HEADS]),
                                           ALU.mult, ALU.mult).then_inc(S["g_done"], 1)
            dve.wait_ge(S["grow_done"], 1)
            dve.wait_ge(S["sig_done"], 1)
            nc.vector.tensor_tensor(beta_grow[:], beta[:], grow[:, 0], ALU.mult).then_inc(S["bg_done"], 1)
            dve.wait_ge(S["bg_done"], 1)
            dve.wait_ge(S["masks"], 13)

            def prepare(i):
                b = i % 2
                dve.wait_ge(S["kt_psum"], i + 1)
                if i:
                    dve.wait_ge(S["wk_psum"], i)
                nc.vector.tensor_tensor(k_in[:], ps[0][:], per_head(beta_grow[:, i]), ALU.mult).then_inc(S["k_in"], 1)
                nc.vector.tensor_tensor(k_out[b][:], ps[0][:], per_head(grow[:, 1, i]), ALU.mult).then_inc(S["k_out"], 1)
                dve.wait_ge(S["kk_psum"], i + 1)
                dve.wait_ge(S["dec_mask"], 2 * i + 2)
                for h in range(HEADS):
                    last = nc.vector.scalar_tensor_tensor(a_mat[:, h], ps[3][:, h], beta[:, i, h:h + 1], decay[:, h], ALU.mult, ALU.mult)
                last.then_inc(S["a"], 1)
                dve.wait_ge(S["qk_psum"], i + 1)
                nc.vector.tensor_tensor(att[b][:], ps[0][:], decay_t[:], ALU.mult).then_inc(S["att"], 1)
                dve.wait_ge(S["at_psum"], i + 1)
                nc.vector.tensor_tensor(xt[1][:], ps[1][:], heads(blocks[:, 0]), ALU.mult).then_inc(S["dt"], 1)
                dve.wait_ge(S["dt"], i + 1)
                nc.vector.tensor_tensor(xt[0][:], heads(g.ident[:]), xt[1][:], ALU.subtract).then_inc(S["x1t"], 1)
                for m in range(3):
                    nc.vector.tensor_tensor(between[m][:], ps[1][:], heads(blocks[:, m + 1]), ALU.mult).then_inc(S["between"], 1)

                def join(name, banks, op, src, dst):
                    for r, (bank, old, new) in enumerate(zip(banks, src, dst)):
                        dve.wait_ge(S[name + "_psum"], 2 * i + r + 1)
                        nc.vector.tensor_tensor(new[:], old[:], ps[bank][:], op).then_inc(S[name], 1)

                dve.wait_ge(S["x1"], i + 1)
                dve.wait_ge(S["x1t"], i + 1)
                join("x2", (1, 2), ALU.add, (x[0], xt[0]), (x[1], xt[1]))
                dve.wait_ge(S["x2"], 2 * i + 2)
                join("x3", (3, 0), ALU.add, (x[1], xt[1]), (x[0], xt[0]))
                dve.wait_ge(S["x3"], 2 * i + 2)
                join("x4", (2, 3), ALU.subtract, (x[0], xt[0]), (x[1], xt[1]))
                dve.wait_ge(S["x4"], 2 * i + 2)
                join("x5", (1, 2), ALU.subtract, (x[1], xt[1]), (x[0], xt[0]))
                dve.wait_ge(S["x5"], 2 * i + 2)
                dve.wait_ge(S["x6_psum"], i + 1)
                nc.vector.tensor_tensor(solve_t[b][:], xt[0][:], ps[0][:], ALU.subtract).then_inc(S["x6"], 1)

            def recur(i):
                for c in chunks_of(i):
                    n = 2 * i + c
                    dve.wait_ge(S["u_psum"], n + 1)
                    if c == 0 and i:
                        dve.wait_ge(S["o_psum"], i)
                    nc.vector.tensor_copy(u[rows(c)], ps[4][rows(c)]).then_inc(S["u_out"], 1)
                    dve.wait_ge(S["ds_psum"], n + 1)
                    old, new = state[n % 2], state[(n + 1) % 2]
                    if n:
                        dve.wait_ge(S["state"], n)
                        dve.wait_ge(S["qs_psum"], n)
                    if n == 16:
                        dve.wait_ge(S["state_in"], 16)
                    for h in range(HEADS):
                        last = nc.vector.scalar_tensor_tensor(new[:, h], old[:, h], grow[:, 2 + c, i, h:h + 1], ps[6 + c][:, h],
                                                              ALU.mult, ALU.add)
                    last.then_inc(S["state"], 1)
                nc_rows = slice(0, P) if i < NT - 1 else rows(0)
                m = P if i < NT - 1 else CHUNK
                dve.wait_ge(S["qs_psum"], n + 1)
                if i:
                    dve.wait_ge(S["o_out"], i)
                nc.vector.tensor_tensor(q_state[nc_rows], ps[5][nc_rows], per_head(grow[nc_rows, 0, i], m), ALU.mult).then_inc(S["qs_out"], 1)
                dve.wait_ge(S["qs_out"], i + 1)
                dve.wait_ge(S["o_psum"], i + 1)
                dve.wait_ge(S["v_in"], i + 1)
                nc.vector.tensor_tensor(g.gdn_v[nc_rows, i].rearrange("p (h v) -> p h v", h=HEADS), q_state[nc_rows], ps[6][nc_rows],
                                        ALU.add).then_inc(S["o_out"], 1)

            for i in range(NT):
                prepare(i)
                recur(i)

        @block.tensor
        def _(pe):
            def product(bank, lhs, rhs, done, rowsl=slice(0, P), start=True):
                for h in range(HEADS):
                    last = nc.tensor.matmul(ps[bank][rowsl, h], lhs(h), rhs(h), start=start and h == 0, stop=h == HEADS - 1,
                                            skip_group_check=True)
                if done:
                    last.then_inc(S[done], 1)

            def of(t):
                return lambda h: t[:, h]

            pe.wait_ge(S["g_done"], 1)
            flat_g = log_g[:].rearrange("p i h -> p (i h)")
            for q, m in enumerate((g.upto[:], g.after[:], g.row_sel[:, 0:P], g.row_sel[:, P:2 * P])):
                last = nc.tensor.matmul(ps[0][:].rearrange("p h t -> p (h t)")[:, NG_ * q:NG_ * q + NG_], m, flat_g,
                                        start=q == 0, stop=q == 3, skip_group_check=True)
            last.then_inc(S["pre_psum"], 1)
            pe.wait_ge(S["grow_done"], 1)

            def prepare(i):
                b = i % 2
                k, q = (lambda h: k_all[:, h, tile(i)]), (lambda h: q_all[:, h, tile(i)])
                if i:
                    pe.wait_ge(S["x6"], i)
                for h in range(HEADS):
                    last = nc.tensor.transpose(ps[0][:, h], k(h), g.ident[:])
                last.then_inc(S["kt_psum"], 1)
                pe.wait_ge(S["steps"], i + 1)
                if i:
                    pe.wait_ge(S["wk"], i)
                product(1, of(steps), lambda h: g.upto[:], "dec_psum")
                nc.tensor.matmul(ps[2][:].rearrange("p h t -> p (h t)"), g.upto[:], steps[:].rearrange("p h t -> p (h t)"),
                                 start=True, stop=True).then_inc(S["dec_psum"], 1)
                product(3, k, k, "kk_psum")
                pe.wait_ge(S["k_out"], i + 1)
                product(0, k, q, "qk_psum")
                pe.wait_ge(S["a"], i + 1)
                pe.wait_ge(S["dec_exp"], 2 * i + 1)
                for h in range(HEADS):
                    last = nc.tensor.transpose(ps[1][:, h], a_mat[:, h], g.ident[:])
                last.then_inc(S["at_psum"], 1)
                pe.wait_ge(S["dt"], i + 1)
                pe.wait_ge(S["d"], i + 1)
                product(2, of(xt[1]), of(x[1]), "p2_psum")
                product(3, of(x[1]), of(xt[1]), "p2_psum")
                pe.wait_ge(S["p2"], 2 * i + 2)
                pe.wait_ge(S["att"], i + 1)
                product(0, of(power2_t), of(power2), "p4_psum")
                pe.wait_ge(S["x1"], i + 1)
                pe.wait_ge(S["x1t"], i + 1)
                pe.wait_ge(S["between"], 3 * i + 3)
                product(1, of(xt[0]), of(power2), "x2_psum")
                product(2, of(power2), of(xt[0]), "x2_psum")
                pe.wait_ge(S["p4"], i + 1)
                pe.wait_ge(S["x2"], 2 * i + 2)
                product(3, of(xt[1]), of(power4), "x3_psum")
                product(0, of(power4), of(xt[1]), "x3_psum")
                pe.wait_ge(S["x3"], 2 * i + 2)
                product(1, of(between[0]), of(x[0]), "p16_psum")
                pe.wait_ge(S["p16"], i + 1)
                product(2, of(xt[0]), of(joint), "x4_psum")
                product(3, of(joint), of(xt[0]), "x4_psum")
                pe.wait_ge(S["x4"], 2 * i + 2)
                product(0, of(between[1]), of(x[1]), "p32_psum")
                pe.wait_ge(S["p32"], i + 1)
                product(1, of(xt[1]), of(joint), "x5_psum")
                product(2, of(joint), of(xt[1]), "x5_psum")
                pe.wait_ge(S["x5"], 2 * i + 2)
                product(3, of(between[2]), of(x[0]), "p64_psum")
                pe.wait_ge(S["p64"], i + 1)
                product(0, of(joint), of(xt[0]), "x6_psum")
                pe.wait_ge(S["x6"], i + 1)
                product(1, of(k_in), of(solve_t[b]), "wk_psum")

            def recur(i):
                b = i % 2
                pe.wait_ge(S["v_in"], i + 1)
                if i:
                    pe.wait_ge(S["u_out"], 2 * i)
                product(4, of(solve_t[b]), of(v_in[b]), None)
                pe.wait_ge(S["wk"], i + 1)
                for c in chunks_of(i):
                    n = 2 * i + c
                    s = state[n % 2]
                    if n:
                        pe.wait_ge(S["state"], n)
                    if n == 0:
                        pe.wait_ge(S["masks"], 13)
                    if n == 16:
                        pe.wait_ge(S["state_in"], 16)
                    product(4, lambda h: wk[b][:, h, rows(c)], of(s), "u_psum", rows(c), start=False)
                    if i:
                        pe.wait_ge(S["qs_out"], i)
                    product(5, lambda h: q_all[:, h, P * i + CHUNK * c:P * i + CHUNK * c + CHUNK], of(s), "qs_psum", rows(c))
                    pe.wait_ge(S["u_out"], n + 1)
                    if c == 0 and i:
                        pe.wait_ge(S["o_out"], i)
                    product(6 + c, lambda h: k_out[b][rows(c), h], lambda h: u[rows(c), h], "ds_psum")
                pe.wait_ge(S["state"], 2 * i + 1)
                if i < NT - 1:
                    product(6, of(att[b]), of(u), "o_psum")
                else:
                    product(6, lambda h: att[b][rows(0), h, rows(0)], lambda h: u[rows(0), h], "o_psum", rows(0))

            for i in range(NT):
                prepare(i)
                recur(i)


def stage_gdn_out(nc, g, d):
    with ExitStack() as ctx:
        def sb(name, shape):
            return ctx.enter_context(nc.sbuf_tensor("go_" + name, shape, F32))

        def sem(name):
            return ctx.enter_context(nc.semaphore("go_" + name))

        w = sb("w", [P, KD, BR])
        gate = sb("gate", [P, NT, BR])
        square = sb("square", [P, DV])
        ssq = sb("ssq", [P, NT * HEADS])
        std = sb("std", [P, NT * HEADS])
        norm_col = sb("norm_col", [P, 1])
        loaded, psum, gate_done, ssq_done, std_done, rstd_done, gated, turned, done, pads = (sem(n) for n in (
            "loaded psum gate_done ssq_done std_done rstd_done gated turned done pads").split())
        ps = [ctx.enter_context(nc.psum_tensor(f"go_ps{b}", [P, 512], F32)) for b in range(8)]
        block = ctx.enter_context(nc.Block())

        @block.sync
        def _(sp):
            sp.dma_start(w[:], rows_view(d["w_in"][0])[:, :, COL["gb"]:COL["gb"] + BR]).then_inc(loaded, 16)
            sp.dma_start(norm_col[:], d["gdn_norm_w"][0].rearrange("(p o) -> p o", o=1), allow_slow_non_contiguous=True).then_inc(loaded, 16)

        @block.tensor
        def _(pe):
            pe.wait_ge(loaded, 32)
            for i in range(NT):
                if i >= 4:
                    pe.wait_ge(gate_done, i - 3)
                for k in range(KD):
                    last = nc.tensor.matmul(ps[i % 4][:], g.h[:, k, P * i:P * i + P], w[:, k], start=k == 0, stop=k == KD - 1)
                last.then_inc(psum, 1)
            for i in range(NT):
                n = P if i < NT - 1 else DEC
                pe.wait_ge(gated, i + 1)
                if i >= 4:
                    pe.wait_ge(done, i - 3)
                for h in range(HEADS):
                    last = nc.tensor.transpose(ps[4 + i % 4][:, P * h:P * h + n], g.gdn_v[0:n, i, DV * h:DV * h + DV], g.ident[0:n, 0:n])
                last.then_inc(turned, 1)

        @block.scalar
        def _(act):
            for i in range(NT):
                n = P if i < NT - 1 else DEC
                for h in range(HEADS):
                    q = HEADS * i + h
                    if q:
                        act.wait_ge(ssq_done, q)
                    nc.scalar.activation(square[0:n], g.gdn_v[0:n, i, DV * h:DV * h + DV], ACT.Square,
                                         accum_out=ssq[0:n, q:q + 1]).then_inc(ssq_done, 1)
            act.wait_ge(ssq_done, NT * HEADS)
            act.wait_ge(pads, 1)
            nc.scalar.activation(std[:], ssq[:], ACT.Sqrt, scale=1.0 / DV, bias=g.eps[:]).then_inc(std_done, 1)
            for i in range(NT):
                act.wait_ge(psum, i + 1)
                nc.scalar.activation(gate[:, i], ps[i % 4][:], ACT.Silu).then_inc(gate_done, 1)
            act.wait_ge(loaded, 32)
            for i in range(NT):
                n = P if i < NT - 1 else DEC
                act.wait_ge(turned, i + 1)
                nc.scalar.activation(g.branch[:, :, P * i:P * i + n], ps[4 + i % 4][:].rearrange("p (h t) -> p h t", h=HEADS)[:, :, 0:n],
                                     ACT.Copy, scale=norm_col[:, 0:1]).then_inc(done, 1)

        @block.vector
        def _(dve):
            nc.vector.memset(ssq[DEC:P, HEADS * (NT - 1):], 1.0).then_inc(pads, 1)
            dve.wait_ge(std_done, 1)
            nc.vector.reciprocal(std[:], std[:]).then_inc(rstd_done, 1)
            dve.wait_ge(rstd_done, 1)
            for i in range(NT):
                n = P if i < NT - 1 else DEC
                dve.wait_ge(gate_done, i + 1)
                for h in range(HEADS):
                    o = g.gdn_v[0:n, i, DV * h:DV * h + DV]
                    last = nc.vector.scalar_tensor_tensor(o, o, std[0:n, HEADS * i + h:HEADS * i + h + 1], gate[0:n, i, DV * h:DV * h + DV],
                                                          ALU.mult, ALU.mult)
                last.then_inc(gated, 1)


XS = MT * P
NL = NG + NE


def tiles_of(t):
    return t[:].rearrange("p k t -> p (k t)").rearrange("p (i c) -> p i c", i=NT)


def stage_project(nc, g, d):
    with ExitStack() as ctx:
        def sb(name, shape):
            return ctx.enter_context(nc.sbuf_tensor("pj_" + name, shape, F32))

        def sem(name):
            return (g.kept if name in SOFTWARE_DMA else ctx).enter_context(nc.semaphore("pj_" + name))

        w = sb("w_out", [P, KD, D])
        rows = sb("rows", [P, 3, 2, D])
        norm_row = sb("norm_row", [P, D])
        w_route = sb("w_route", [P, KD, NL])
        b_route = sb("b_route", [NL, 1])
        h2 = sb("h2", [P, 3, D])
        h2t = sb("h2t", [P, 2, KD, P])
        branch_sum = sb("branch_sum", [P, 2, D])
        square = sb("square", [P, D])
        ssq = sb("ssq", [P, NT])
        std = sb("std", [P, NT])
        rstd = sb("rstd", [P, NT])
        logits = sb("logits", [NL, 2, P])
        S = {n: sem(n) for n in ("w_loaded x_loaded rows_loaded route_loaded pads scale added ssq std rstd scaled h2 stored0 stored1 stored2 "
                                 "proj_psum gated turned h2t logit_psum logit_out logit_turned").split()}
        stored = [S["stored0"], S["stored1"], S["stored2"]]
        ps = [ctx.enter_context(nc.psum_tensor(f"pj_ps{b}", [P, 512], F32)) for b in range(8)]
        block = ctx.enter_context(nc.Block())
        x1 = tiles_of(g.h)

        @block.sync
        def _(sp):
            for q in range(2):
                sp.dma_start(w[:, 4 * q:4 * q + 4], rows_view(d["w_out"][0])[:, 4 * q:4 * q + 4]).then_inc(S["w_loaded"], 16)
            sp.dma_start(x1[:, 0:8, :], d["x_prompt"][0].rearrange("(i p) c -> p i c", p=P)).then_inc(S["x_loaded"], 16)
            sp.dma_start(x1[0:64, 8, :], d["x_sample"][0]).then_inc(S["x_loaded"], 16)
            for i in range(NT):
                n = P if i < NT - 1 else DEC
                sp.wait_ge(S["h2"], i + 1)
                sp.dma_start(g.h2_dram[P * i:P * i + n, :], h2[0:n, i % 3]).then_inc(stored[i % 3], 16)
            for s in stored:
                sp.wait_ge(s, 48)

        @block.gpsimd
        def _(pool):
            for j, chunk in enumerate((2, 4, 3)):
                for who in range(2):
                    pool.dma_start(rows[:, j, who], g.mod_dram[who:who + 1, D * chunk:D * chunk + D].broadcast_to([P, D])).then_inc(S["rows_loaded"], 16)
            pool.dma_start(norm_row[:], d["norm2_w"].broadcast_to([P, D])).then_inc(S["rows_loaded"], 16)
            pool.dma_start(w_route[:, :, 0:NG], rows_view(d["w_route_group"][0])).then_inc(S["route_loaded"], 16)
            pool.dma_start(w_route[:, :, NG:], rows_view(d["w_route_expert"][0])).then_inc(S["route_loaded"], 16)
            pool.dma_start(b_route[0:NG], d["b_route_group"][0].rearrange("(e o) -> e o", o=1)).then_inc(S["route_loaded"], 16)
            pool.dma_start(b_route[NG:], d["b_route_expert"][0].rearrange("(e o) -> e o", o=1)).then_inc(S["route_loaded"], 16)

        @block.tensor
        def _(pe):
            def project(i):
                n = P if i < NT - 1 else DEC
                for c in range(2):
                    for k in range(KD):
                        last = nc.tensor.matmul(ps[2 * (i % 2) + c][0:n], g.mix[:, k, P * i:P * i + n], w[:, k, 512 * c:512 * c + 512],
                                                start=k == 0, stop=k == KD - 1)
                    last.then_inc(S["proj_psum"], 1)

            pe.wait_ge(S["w_loaded"], 32)
            project(0)
            project(1)
            pe.wait_ge(S["route_loaded"], 64)
            for i in range(NT):
                pe.wait_ge(S["h2"], i + 1)
                if i:
                    pe.wait_ge(S["h2t"], 2 * i)
                for k in range(KD):
                    last = nc.tensor.transpose(ps[4 + k // 4][:, P * (k % 4):P * (k % 4) + P], h2[:, i % 3, P * k:P * k + P], g.ident[:])
                last.then_inc(S["turned"], 1)
                if i + 2 < NT:
                    project(i + 2)
                pe.wait_ge(S["h2t"], 2 * i + 2)
                if i:
                    pe.wait_ge(S["logit_out"], i)
                for k in range(KD):
                    last = nc.tensor.matmul(ps[6][0:NL, 0:P], w_route[:, k], h2t[:, i % 2, k], start=k == 0, stop=k == KD - 1)
                last.then_inc(S["logit_psum"], 1)
                if i:
                    nc.tensor.transpose(ps[7][:, NL * (i - 1):NL * i], logits[:, (i - 1) % 2], g.ident[0:NL, 0:NL])
            pe.wait_ge(S["logit_out"], NT)
            nc.tensor.transpose(ps[7][:, NL * (NT - 1):NL * NT], logits[:, (NT - 1) % 2], g.ident[0:NL, 0:NL]).then_inc(S["logit_turned"], 1)

        @block.vector
        def _(dve):
            nc.vector.memset(x1[64:128, 8, :], 0.0).then_inc(S["pads"], 1)
            dve.wait_ge(S["rows_loaded"], 112)
            for who in range(2):
                nc.vector.scalar_tensor_tensor(rows[:, 1, who], rows[:, 1, who], 1.0, norm_row[:], ALU.add, ALU.mult).then_inc(S["scale"], 1)
            dve.wait_ge(S["x_loaded"], 32)
            dve.wait_ge(S["pads"], 1)

            def logit(i):
                dve.wait_ge(S["logit_psum"], i + 1)
                nc.vector.tensor_scalar(logits[:, i % 2], ps[6][0:NL, 0:P], b_route[:, 0:1], None, ALU.add).then_inc(S["logit_out"], 1)

            dve.wait_ge(S["route_loaded"], 64)

            def add_branches(i):
                n, who = (P, 0) if i < NT - 1 else (DEC, 1)
                for c in range(2):
                    half = slice(512 * c, 512 * c + 512)
                    dve.wait_ge(S["proj_psum"], 2 * i + c + 1)
                    nc.vector.tensor_tensor(branch_sum[0:n, i % 2, half], ps[2 * (i % 2) + c][0:n], rows[0:n, 0, who, half], ALU.mult).then_inc(S["gated"], 1)
                dve.wait_ge(S["gated"], 2 * i + 2)
                nc.vector.tensor_tensor(x1[0:n, i], x1[0:n, i], branch_sum[0:n, i % 2], ALU.add).then_inc(S["added"], 1)

            add_branches(0)
            for i in range(NT):
                who = 0 if i < NT - 1 else 1
                dve.wait_ge(S["std"], i + 1)
                nc.vector.reciprocal(rstd[:, i:i + 1], std[:, i:i + 1]).then_inc(S["rstd"], 1)
                dve.wait_ge(S["rstd"], i + 1)
                dve.wait_ge(S["scale"], 2)
                if i >= 3:
                    dve.wait_ge(stored[i % 3], 16 * (i // 3))
                    dve.wait_ge(S["turned"], i - 2)
                nc.vector.scalar_tensor_tensor(h2[:, i % 3], x1[:, i], rstd[:, i:i + 1], rows[:, 1, who], ALU.mult, ALU.mult).then_inc(S["scaled"], 1)
                dve.wait_ge(S["scaled"], i + 1)
                nc.vector.tensor_tensor(h2[:, i % 3], h2[:, i % 3], rows[:, 2, who], ALU.add).then_inc(S["h2"], 1)
                if i >= 1:
                    logit(i - 1)
                if i + 1 < NT:
                    add_branches(i + 1)
            logit(NT - 1)
            dve.wait_ge(S["logit_turned"], 1)
            nc.vector.tensor_copy(g.logits[:].rearrange("p i e -> p (i e)"), ps[7][:, 0:NT * NL])

        @block.scalar
        def _(act):
            def unload(i):
                for c in range(2):
                    act.wait_ge(S["turned"], i + 1)
                    if i >= 2:
                        act.wait_ge(S["logit_psum"], i - 1)
                    nc.scalar.activation(h2t[:, i % 2, 4 * c:4 * c + 4], ps[4 + c][:].rearrange("p (k t) -> p k t", k=4), ACT.Copy).then_inc(S["h2t"], 1)

            for i in range(NT):
                act.wait_ge(S["added"], i + 1)
                nc.scalar.activation(square[:], x1[:, i], ACT.Square, accum_out=ssq[:, i:i + 1]).then_inc(S["ssq"], 1)
                act.wait_ge(S["ssq"], i + 1)
                nc.scalar.activation(std[:, i:i + 1], ssq[:, i:i + 1], ACT.Sqrt, scale=1.0 / D, bias=g.eps[:]).then_inc(S["std"], 1)
                if i:
                    unload(i - 1)
            unload(NT - 1)


LOGIT_STEP, BOTH_STEP, RATIO_STEP, SLOT_STEP = 5, 24, 25, 58


def stage_route(nc, g, d):
    with ExitStack() as ctx:
        def sb(name, shape, dt=F32):
            return ctx.enter_context(nc.sbuf_tensor("rt_" + name, shape, dt))

        def sem(name):
            return (g.kept if name in SOFTWARE_DMA else ctx).enter_context(nc.semaphore("rt_" + name))

        before = sb("before", [P, P])
        token = sb("token", [P, NT])
        token_i = sb("token_i", [P, NT], I32)
        no_tokens = sb("no_tokens", [MT, P])
        count = sb("count", [P, MT])
        rank = sb("rank", [P, NE])
        g_max = sb("g_max", [P, NT])
        g_exp = sb("g_exp", [P, NT, NG])
        p_group = sb("p_group", [P, NT])
        g_hot = sb("g_hot", [P, NT, NG])
        inside = sb("inside", [P, NT, NE])
        cand = sb("cand", [P, NT, NE])
        best = sb("best", [P, NT])
        top = sb("top", [P, 2, NT])
        hot = sb("hot", [P, 2, NT, NE])
        both = sb("both", [P, NT, NE])
        ratio = sb("ratio", [P, NT])
        slot = sb("slot", [P, NT, NE])
        total = sb("total", [P, NT + 1, NE])
        tiles = sb("tiles", [P, 2, NE])
        ends = sb("ends", [P, NE])
        slot_f = sb("slot_f", [P, 2, NT])
        passed = sb("passed", [P, MT, NE])
        owner = sb("owner", [P, MT])
        slot_rows = sb("slot_rows", [MT, P])
        S = {n: sem(n) for n in "step made zero_stored exp_done psum scattered slot_rows turned".split()}
        ps = [ctx.enter_context(nc.psum_tensor(f"rt_ps{b}", [P, 512], F32)) for b in range(3)]
        block = ctx.enter_context(nc.Block())

        @block.gpsimd
        def _(pool):
            nc.gpsimd.memset(before[:], 1.0).then_inc(S["made"], 1)
            pool.wait_ge(S["made"], 1)
            nc.gpsimd.affine_select(out=before[:], in_=before[:], compare_op=ALU.is_gt, fill=0.0, base=0,
                                    pattern=[[1, P]], channel_multiplier=-1).then_inc(S["made"], 1)
            pool.wait_ge(S["made"], 2)
            nc.gpsimd.memset(no_tokens[:], 0.0).then_inc(S["made"], 1)
            pool.wait_ge(S["made"], 3)
            nc.gpsimd.iota(token_i[:], pattern=[[P, NT]], base=0, channel_multiplier=1).then_inc(S["made"], 1)
            pool.wait_ge(S["step"], SLOT_STEP)
            pool.wait_ge(S["zero_stored"], 16)
            for k in range(2):
                for i in range(NT):
                    n = P if i < NT - 1 else DEC
                    nc.gpsimd.indirect_dma_start(g.token_dram, bass.IndirectOffsetOnAxis(ap=g.slot_i[0:n, k, i:i + 1], axis=0),
                                                 token[0:n, i:i + 1], None).then_inc(S["scattered"], 16)
            pool.wait_ge(S["scattered"], 16 * 2 * NT)

        @block.sync
        def _(sp):
            sp.wait_ge(S["made"], 3)
            sp.dma_start(g.token_dram.rearrange("(t r) o -> t (r o)", t=MT), no_tokens[:]).then_inc(S["zero_stored"], 16)
            sp.wait_ge(S["zero_stored"], 16)
            sp.wait_ge(S["scattered"], 16 * 2 * NT)
            sp.dma_start(slot_rows[:], g.token_dram.rearrange("(t r) o -> t (r o)", t=MT)).then_inc(S["slot_rows"], 16)

        @block.scalar
        def _(act):
            act.wait_ge(S["step"], LOGIT_STEP)
            nc.scalar.activation(g_exp[:], g_exp[:], ACT.Exp).then_inc(S["exp_done"], 1)
            act.wait_ge(S["step"], RATIO_STEP)
            nc.scalar.activation(ratio[:], ratio[:], ACT.Exp).then_inc(S["exp_done"], 1)

        @block.tensor
        def _(pe):
            pe.wait_ge(S["made"], 2)
            pe.wait_ge(S["step"], BOTH_STEP)
            flat = both[:].rearrange("p i e -> p (i e)")
            nc.tensor.matmul(ps[0][:, 0:NT * NE], before[:], flat, start=True, stop=True)
            nc.tensor.matmul(ps[1][:, 0:NT * NE], g.ones[:], flat, start=True, stop=True).then_inc(S["psum"], 1)
            pe.wait_ge(S["slot_rows"], 16)
            nc.tensor.transpose(ps[2][:, 0:MT], slot_rows[:], g.ident[0:MT, 0:MT]).then_inc(S["turned"], 1)

        @block.vector
        def _(dve):
            done = 0

            def then(instruction):
                nonlocal done
                instruction.then_inc(S["step"], 1)
                done += 1
                dve.wait_ge(S["step"], done)

            def wide(t, n):
                return t.unsqueeze(2).broadcast_to([P, NT, n])

            def first(values, maxima, out, n):
                then(nc.vector.tensor_tensor(cand[:, :, 0:n], values, wide(maxima, n), ALU.is_equal))
                then(nc.vector.tensor_tensor(cand[:, :, 0:n], cand[:, :, 0:n], rank[:, 0:n].unsqueeze(1).broadcast_to([P, NT, n]), ALU.mult))
                then(nc.vector.tensor_reduce(best[:], cand[:, :, 0:n], AX.X, ALU.max))
                then(nc.vector.tensor_tensor(out, cand[:, :, 0:n], wide(best[:], n), ALU.is_equal))

            groups, experts = g.logits[:, :, 0:NG], g.logits[:, :, NG:]
            then(nc.vector.tensor_tensor_scan(count[:], g.ones[:, 0:MT], g.ones[:, 0:MT], 0.0, ALU.mult, ALU.add))
            then(nc.vector.tensor_scalar(rank[:], count[:, 0:NE], -1.0, NE + 1.0, ALU.mult, ALU.add))
            dve.wait_ge(S["made"], 4)
            then(nc.vector.tensor_copy(token[:], token_i[:]))
            then(nc.vector.tensor_reduce(g_max[:], groups, AX.X, ALU.max))
            then(nc.vector.tensor_tensor(g_exp[:], groups, wide(g_max[:], NG), ALU.subtract))
            assert done == LOGIT_STEP
            first(groups, g_max[:], g_hot[:], NG)
            then(nc.vector.tensor_scalar(g_hot[:], g_hot[:], 1e30, -1e30, ALU.mult, ALU.add))
            then(nc.vector.tensor_tensor(inside[:].rearrange("p i (a b) -> p i a b", a=NG), experts.rearrange("p i (a b) -> p i a b", a=NG),
                                         g_hot[:].unsqueeze(3).broadcast_to([P, NT, NG, NE // NG]), ALU.add))
            then(nc.vector.tensor_reduce(top[:, 0], inside[:], AX.X, ALU.max))
            first(inside[:], top[:, 0], hot[:, 0], NE)
            then(nc.vector.scalar_tensor_tensor(inside[:], hot[:, 0], -1e30, inside[:], ALU.mult, ALU.add))
            then(nc.vector.tensor_reduce(top[:, 1], inside[:], AX.X, ALU.max))
            first(inside[:], top[:, 1], hot[:, 1], NE)
            then(nc.vector.memset(hot[DEC:P, :, NT - 1, :], 0.0))
            then(nc.vector.tensor_tensor(both[:], hot[:, 0], hot[:, 1], ALU.add))
            assert done == BOTH_STEP
            then(nc.vector.tensor_tensor(ratio[:], top[:, 1], top[:, 0], ALU.subtract))
            assert done == RATIO_STEP
            dve.wait_ge(S["exp_done"], 1)
            then(nc.vector.tensor_reduce(p_group[:], g_exp[:], AX.X, ALU.add))
            dve.wait_ge(S["exp_done"], 2)
            then(nc.vector.tensor_scalar(best[:], ratio[:], 1.0, None, ALU.add))
            then(nc.vector.tensor_tensor(p_group[:], p_group[:], best[:], ALU.mult))
            then(nc.vector.reciprocal(g.choice_w[:, 0], p_group[:]))
            then(nc.vector.tensor_tensor(g.choice_w[:, 1], g.choice_w[:, 0], ratio[:], ALU.mult))
            then(nc.vector.memset(total[:, 0], 0.0))
            dve.wait_ge(S["psum"], 1)
            for i in range(NT):
                then(nc.vector.tensor_tensor(total[:, i + 1], total[:, i], ps[1][:, NE * i:NE * i + NE], ALU.add))
            then(nc.vector.tensor_scalar(tiles[:, 0], total[:, NT], 0.0, None, ALU.is_gt))
            for j in range(1, NT):
                then(nc.vector.scalar_tensor_tensor(tiles[:, j % 2], total[:, NT], float(P * j), tiles[:, (j - 1) % 2], ALU.is_gt, ALU.add))
            last = (NT - 1) % 2
            then(nc.vector.tensor_tensor_scan(ends[:], g.ones[:, 0:NE], tiles[:, last], 0.0, ALU.mult, ALU.add))
            then(nc.vector.tensor_tensor(tiles[:, last], ends[:], tiles[:, last], ALU.subtract))
            then(nc.vector.tensor_tensor(slot[:].rearrange("p i e -> p (i e)"), total[:, 0:NT].rearrange("p i e -> p (i e)"), ps[0][:, 0:NT * NE], ALU.add))
            then(nc.vector.scalar_tensor_tensor(slot[:], tiles[:, last].unsqueeze(1).broadcast_to([P, NT, NE]), float(P), slot[:], ALU.mult, ALU.add))
            for k in range(2):
                then(nc.vector.tensor_tensor(hot[:, k], hot[:, k], slot[:], ALU.mult))
                then(nc.vector.tensor_reduce(slot_f[:, k], hot[:, k], AX.X, ALU.add))
            then(nc.vector.tensor_copy(g.slot_i[:], slot_f[:]))
            assert done == SLOT_STEP
            then(nc.vector.tensor_tensor(passed[:], ends[:].unsqueeze(1).broadcast_to([P, MT, NE]), count[:].unsqueeze(2).broadcast_to([P, MT, NE]), ALU.is_lt))
            then(nc.vector.tensor_reduce(owner[:], passed[:], AX.X, ALU.add))
            then(nc.vector.tensor_scalar(owner[:], owner[:], float(NE - 1), None, ALU.min))
            then(nc.vector.tensor_copy(g.owner_i[:], owner[:]))
            dve.wait_ge(S["turned"], 1)
            nc.vector.tensor_copy(g.row_token[:], ps[2][:, 0:MT])


def stage_experts(nc, g, d):
    with ExitStack() as ctx:
        def sb(name, shape):
            return ctx.enter_context(nc.sbuf_tensor("ex_" + name, shape, F32))

        def sem(name):
            return (g.kept if name in SOFTWARE_DMA else ctx).enter_context(nc.semaphore("ex_" + name))

        w_in = sb("w_in", [P, 2, 2, KD, FF])
        w_down = sb("w_down", [P, 2, FF // P, D])
        x = sb("x", [P, 2, D])
        xt = sb("xt", [P, 2, KD, P])
        silu = sb("silu", [P, 2, 2 * P])
        hid = sb("hid", [P, 2, FF // P, P])
        y = sb("y", [P, 2, D])
        S = {n: sem(n) for n in "in_loaded0 in_loaded1 down_loaded0 down_loaded1 x_loaded0 x_loaded1 turned xt_out gu_psum silu hid down_psum y_out stored0 stored1".split()}
        pair = lambda name: (S[name + "0"], S[name + "1"])
        in_loaded, down_loaded, x_loaded, stored = pair("in_loaded"), pair("down_loaded"), pair("x_loaded"), pair("stored")
        ps = [ctx.enter_context(nc.psum_tensor(f"ex_ps{b}", [P, 512], F32)) for b in range(8)]
        block = ctx.enter_context(nc.Block())
        gate_view = d["w_exp_gate"][0].rearrange("e (k p) n -> p (e k) n", p=P)
        up_view = d["w_exp_up"][0].rearrange("e (k p) n -> p (e k) n", p=P)
        down_view = d["w_exp_down"][0].rearrange("e (k p) n -> p (e k) n", p=P)
        ys_view = g.ys_dram.rearrange("(t p) c -> p t c", p=P)

        @block.sync
        def _(sp):
            def load(t, b, rounds):
                if rounds is not None:
                    sp.wait_ge(S["gu_psum"], rounds)
                e = sp.value_load(g.owner_i[0:1, bass.ds(t, 1)], min_val=0, max_val=NE - 1)
                sp.dma_start(w_in[:, b, 0], gate_view[:, bass.ds(e * KD, KD), :]).then_inc(in_loaded[b], 16)
                sp.dma_start(w_in[:, b, 1], up_view[:, bass.ds(e * KD, KD), :]).then_inc(in_loaded[b], 16)
                if rounds is not None:
                    sp.wait_ge(S["down_psum"], rounds * 2)
                sp.dma_start(w_down[:, b], down_view[:, bass.ds(e * (FF // P), FF // P), :]).then_inc(down_loaded[b], 16)

            def store(t, b, count):
                sp.wait_ge(S["y_out"], count)
                sp.dma_start(ys_view[:, bass.ds(t, 1), :], y[:, b:b + 1]).then_inc(stored[b], 16)

            load(0, 0, None)
            load(1, 1, None)
            with sp.Fori(1, MT // 2) as r:
                for b in range(2):
                    load(r * 2 + b, b, r * 2 + (b - 1))
                    store(r * 2 + (b - 2), b, r * 4 + (2 * b - 2))
            for b in range(2):
                store(MT - 2 + b, b, 2 * MT - 2 + 2 * b)
            for b in range(2):
                sp.wait_ge(stored[b], 8 * MT)

        @block.gpsimd
        def _(pool):
            for t in range(MT):
                if t >= 2:
                    pool.wait_ge(S["turned"], t - 1)
                nc.gpsimd.indirect_dma_start(x[:, t % 2], None, g.h2_dram,
                                             bass.IndirectOffsetOnAxis(ap=g.row_token[:, t:t + 1], axis=0)).then_inc(x_loaded[t % 2], 16)

        @block.tensor
        def _(pe):
            def turn(t, b, rounds, freed):
                pe.wait_ge(x_loaded[b], rounds)
                if freed is not None:
                    pe.wait_ge(S["xt_out"], freed)
                for k in range(KD):
                    last = nc.tensor.transpose(ps[k // 4][:, P * (k % 4):P * (k % 4) + P], x[:, b, P * k:P * k + P], g.ident[:])
                last.then_inc(S["turned"], 1)

            def gate_up(t, b, rounds, freed):
                pe.wait_ge(in_loaded[b], rounds)
                pe.wait_ge(S["xt_out"], t * 2 + 2)
                if freed is not None:
                    pe.wait_ge(S["hid"], freed)
                for m in range(4):
                    for k in range(KD):
                        last = nc.tensor.matmul(ps[2 + b][:, P * m:P * m + P], w_in[:, b, m // 2, k, P * (m % 2):P * (m % 2) + P], xt[:, b, k],
                                                start=m == 0 and k == 0, stop=m == 3 and k == KD - 1, skip_group_check=True)
                last.then_inc(S["gu_psum"], 1)

            def down(t, b, rounds, freed):
                pe.wait_ge(down_loaded[b], rounds)
                pe.wait_ge(S["hid"], t + 1)
                if freed is not None:
                    pe.wait_ge(S["y_out"], freed)
                for c in range(2):
                    for k in range(FF // P):
                        last = nc.tensor.matmul(ps[4 + 2 * b + c][:], hid[:, b, k], w_down[:, b, k, 512 * c:512 * c + 512],
                                                start=k == 0, stop=k == FF // P - 1)
                    last.then_inc(S["down_psum"], 1)

            turn(0, 0, 16, None)
            gate_up(0, 0, 32, None)
            turn(1, 1, 16, 2)
            down(0, 0, 16, None)
            gate_up(1, 1, 32, None)
            turn(2, 0, 32, 4)
            down(1, 1, 16, None)
            with pe.Fori(1, MT // 2 - 1) as r:
                for b in range(2):
                    gate_up(r * 2 + b, b, r * 32 + 32, r * 2 + (b - 1))
                    turn(r * 2 + (b + 1), 1 - b, r * 16 + (16 + 16 * b), r * 4 + (2 * b + 2))
                    down(r * 2 + b, b, r * 16 + 16, r * 4 + (2 * b - 2))
            t = MT - 2
            gate_up(t, 0, 16 * MT, t - 1)
            turn(t + 1, 1, 8 * MT, 2 * t + 2)
            down(t, 0, 8 * MT, 2 * t - 2)
            gate_up(t + 1, 1, 16 * MT, t)
            down(t + 1, 1, 8 * MT, 2 * t)

        @block.scalar
        def _(act):
            def unload(t, b, freed):
                act.wait_ge(S["turned"], t + 1)
                if freed is not None:
                    act.wait_ge(S["gu_psum"], freed)
                nc.scalar.activation(xt[:, b, 0:4], ps[0][:].rearrange("p (k t) -> p k t", k=4), ACT.Copy).then_inc(S["xt_out"], 1)

            def silu_of(t, b, freed):
                act.wait_ge(S["gu_psum"], t + 1)
                if freed is not None:
                    act.wait_ge(S["hid"], freed)
                nc.scalar.activation(silu[:, b], ps[2 + b][:, 0:2 * P], ACT.Silu).then_inc(S["silu"], 1)

            def store_half(t, b, freed):
                act.wait_ge(S["down_psum"], t * 2 + 1)
                if freed is not None:
                    act.wait_ge(stored[b], freed)
                nc.scalar.activation(y[:, b, 0:512], ps[4 + 2 * b][:], ACT.Copy).then_inc(S["y_out"], 1)

            act.preload_act_table(ACT.Silu)
            unload(0, 0, None)
            silu_of(0, 0, None)
            unload(1, 1, None)
            store_half(0, 0, None)
            silu_of(1, 1, None)
            unload(2, 0, 1)
            store_half(1, 1, None)
            with act.Fori(1, MT // 2 - 1) as r:
                for b in range(2):
                    silu_of(r * 2 + b, b, r * 2 + (b - 1))
                    unload(r * 2 + (b + 1), 1 - b, r * 2 + b)
                    store_half(r * 2 + b, b, r * 16)
            t = MT - 2
            silu_of(t, 0, t - 1)
            unload(t + 1, 1, t)
            store_half(t, 0, 8 * t)
            silu_of(t + 1, 1, t)
            store_half(t + 1, 1, 8 * t)

        @block.vector
        def _(dve):
            def unload(t, b, freed):
                dve.wait_ge(S["turned"], t + 1)
                if freed is not None:
                    dve.wait_ge(S["gu_psum"], freed)
                nc.vector.tensor_copy(xt[:, b, 4:8], ps[1][:].rearrange("p (k t) -> p k t", k=4)).then_inc(S["xt_out"], 1)

            def hidden(t, b, freed):
                dve.wait_ge(S["silu"], t + 1)
                if freed is not None:
                    dve.wait_ge(S["down_psum"], freed)
                nc.vector.tensor_tensor(hid[:, b].rearrange("p k t -> p (k t)"), silu[:, b], ps[2 + b][:, 2 * P:], ALU.mult).then_inc(S["hid"], 1)

            def store_half(t, b, freed):
                dve.wait_ge(S["down_psum"], t * 2 + 2)
                if freed is not None:
                    dve.wait_ge(stored[b], freed)
                nc.vector.tensor_copy(y[:, b, 512:], ps[5 + 2 * b][:]).then_inc(S["y_out"], 1)

            unload(0, 0, None)
            hidden(0, 0, None)
            unload(1, 1, None)
            store_half(0, 0, None)
            hidden(1, 1, None)
            unload(2, 0, 1)
            store_half(1, 1, None)
            with dve.Fori(1, MT // 2 - 1) as r:
                for b in range(2):
                    hidden(r * 2 + b, b, r * 4 + (2 * b - 2))
                    unload(r * 2 + (b + 1), 1 - b, r * 2 + b)
                    store_half(r * 2 + b, b, r * 16)
            t = MT - 2
            hidden(t, 0, 2 * t - 2)
            unload(t + 1, 1, t)
            store_half(t, 0, 8 * t)
            hidden(t + 1, 1, 2 * t)
            store_half(t + 1, 1, 8 * t)



def stage_combine(nc, g, d, out):
    with ExitStack() as ctx:
        def sb(name, shape):
            return ctx.enter_context(nc.sbuf_tensor("co_" + name, shape, F32))

        def sem(name):
            return (g.kept if name in SOFTWARE_DMA else ctx).enter_context(nc.semaphore("co_" + name))

        rows = sb("rows", [P, 3, 2, D])
        gain = sb("gain", [P, 2, D])
        final_w = sb("final_w", [P, D])
        square = sb("square", [P, D])
        ssq = sb("ssq", [P, NT])
        std = sb("std", [P, NT])
        rstd = sb("rstd", [P, NT])
        S = {n: sem(n) for n in "gathered0 gathered1 gathered2 gains_loaded weighted summed gated added ssq std rstd y stored".split()}
        gathered = [S[f"gathered{b}"] for b in range(3)]
        block = ctx.enter_context(nc.Block())
        x1 = tiles_of(g.h)

        @block.gpsimd
        def _(pool):
            for i in range(NT):
                n = P if i < NT - 1 else DEC
                for k in range(2):
                    if i >= 3:
                        pool.wait_ge(S["added"], i - 2)
                    nc.gpsimd.indirect_dma_start(rows[0:n, i % 3, k], None, g.ys_dram,
                                                 bass.IndirectOffsetOnAxis(ap=g.slot_i[0:n, k, i:i + 1], axis=0)).then_inc(gathered[i % 3], 16)

        @block.sync
        def _(sp):
            for who in range(2):
                sp.dma_start(gain[:, who], g.mod_dram[who:who + 1, 5 * D:6 * D].broadcast_to([P, D])).then_inc(S["gains_loaded"], 16)
            sp.dma_start(final_w[:], d["final_norm_w"].rearrange("(o c) -> o c", o=1).broadcast_to([P, D])).then_inc(S["gains_loaded"], 16)
            for i in range(NT):
                sp.wait_ge(S["y"], i + 1)
                if i < NT - 1:
                    sp.dma_start(out["y"][0][0, P * i:P * i + P, :], x1[:, i]).then_inc(S["stored"], 16)
                else:
                    sp.dma_start(out["y"][1][0], x1[0:DEC, i]).then_inc(S["stored"], 16)
            sp.wait_ge(S["stored"], 16 * NT)

        @block.scalar
        def _(act):
            def root(i):
                n = P if i < NT - 1 else DEC
                act.wait_ge(S["added"], i + 1)
                nc.scalar.activation(square[0:n], x1[0:n, i], ACT.Square, accum_out=ssq[0:n, i:i + 1]).then_inc(S["ssq"], 1)
                act.wait_ge(S["ssq"], i + 1)
                nc.scalar.activation(std[0:n, i:i + 1], ssq[0:n, i:i + 1], ACT.Sqrt, scale=1.0 / D, bias=g.eps[0:n]).then_inc(S["std"], 1)

            for i in range(NT):
                n = P if i < NT - 1 else DEC
                act.wait_ge(gathered[i % 3], 32 * (i // 3 + 1))
                nc.scalar.activation(rows[0:n, i % 3, 0], rows[0:n, i % 3, 0], ACT.Copy, scale=g.choice_w[0:n, 0, i:i + 1]).then_inc(S["weighted"], 1)
                if i:
                    root(i - 1)
            root(NT - 1)

        @block.vector
        def _(dve):
            dve.wait_ge(S["gains_loaded"], 48)

            def finish(i):
                n = P if i < NT - 1 else DEC
                dve.wait_ge(S["std"], i + 1)
                nc.vector.reciprocal(rstd[0:n, i:i + 1], std[0:n, i:i + 1]).then_inc(S["rstd"], 1)
                dve.wait_ge(S["rstd"], i + 1)
                nc.vector.scalar_tensor_tensor(x1[0:n, i], x1[0:n, i], rstd[0:n, i:i + 1], final_w[0:n], ALU.mult, ALU.mult).then_inc(S["y"], 1)

            for i in range(NT):
                n, who = (P, 0) if i < NT - 1 else (DEC, 1)
                dve.wait_ge(S["weighted"], i + 1)
                nc.vector.scalar_tensor_tensor(rows[0:n, i % 3, 0], rows[0:n, i % 3, 1], g.choice_w[0:n, 1, i:i + 1], rows[0:n, i % 3, 0],
                                               ALU.mult, ALU.add).then_inc(S["summed"], 1)
                dve.wait_ge(S["summed"], i + 1)
                nc.vector.tensor_tensor(rows[0:n, i % 3, 0], rows[0:n, i % 3, 0], gain[0:n, who], ALU.mult).then_inc(S["gated"], 1)
                dve.wait_ge(S["gated"], i + 1)
                nc.vector.tensor_tensor(x1[0:n, i], x1[0:n, i], rows[0:n, i % 3, 0], ALU.add).then_inc(S["added"], 1)
                if i:
                    finish(i - 1)
            finish(NT - 1)


def reuse_semaphores(nc):
    left = sorted(nc.released_uncleared_semaphores)
    while left:
        run = next((n for n in range(1, len(left)) if left[n] != left[0] + n), len(left))
        nc.gpsimd.sem_clear(range(left[0], left[0] + run))
        left = left[run:]
    nc.all_engine_barrier()


OUT_SHAPES = [(1, SEQ, D), (1, DEC, D)] + 2 * [(1, 1, HEADS, GDK, DV), (1, 1, HEADS, DV, DV), (1, 1, CW - 1, CONVCH),
                                               (1, 1, GROUPS, ST), (1, 1, GROUPS, ST)]


def build(nc, d, out):
    g = Shared()
    out = dict(y=out[0:2], gla=(out[2], out[7]), gdn=(out[3], out[8]), conv=(out[4], out[9]), s5=(out[5:7], out[10:12]))
    with ExitStack() as ctx:
        g.kept = ctx.enter_context(ExitStack())

        def sb(name, shape, stack=ctx):
            return stack.enter_context(nc.sbuf_tensor(name, shape, F32))

        g.mod_dram = nc.dram_tensor("mod_dram", [2, 6 * D], F32, kind="Internal").ap()
        g.ident = sb("ident", [P, P])
        g.upto = sb("upto", [P, P])
        g.after = sb("after", [P, P])
        g.ones = sb("ones", [P, P])
        g.row_sel = sb("row_sel", [P, 2 * P])
        g.eps = sb("eps", [P, 1])
        g.mod_cols = sb("mod_cols", [P, 48, 2])
        g.h = sb("h", [P, KD, TP])
        g.h2_dram = nc.dram_tensor("h2_dram", [TOK, D], F32, kind="Internal").ap()
        g.ys_dram = nc.dram_tensor("ys_dram", [XS, D], F32, kind="Internal").ap()
        g.token_dram = nc.dram_tensor("token_dram", [XS, 1], F32, kind="Internal").ap()
        stage_start(nc, g, d)
        g.mix = sb("mix", [P, KD, TOK])
        g.s5_y = g.mix[:, 0:KB]
        with ExitStack() as tables:
            g.s5_toeplitz = sb("s5_toeplitz", [P, GROUPS, LB, GC], tables)
            g.s5_b_cols = sb("s5_b_cols", [P, 2, PAIRS, P], tables)
            g.s5_c_pow = sb("s5_c_pow", [P, 2, PAIRS, LB + 1, GC], tables)
            g.s5_step = sb("s5_step_mul", [P, 2, 2, PAIRS], tables)
            stage_s5_tables(nc, g, d)
            stage_s5(nc, g, d, out)
        reuse_semaphores(nc)
        branches = ctx.enter_context(ExitStack())
        g.branch = sb("branch", [P, KB, TOK], branches)
        stage_glu(nc, g, d)
        stage_merge(nc, g, d, "c", 2, True)
        with ExitStack() as inner:
            g.gla_qk = sb("gla_qk", [P, 4, TP], inner)
            g.gla_low = sb("gla_low", [LOWR, TOK], inner)
            g.gla_v = sb("gla_v", [P, NT, BR], inner)
            g.gla_gate = sb("gla_gate", [P, NT, BR], inner)
            stage_gla_in(nc, g, d)
            stage_gla(nc, g, d, out)
        stage_merge(nc, g, d, "a", 0, False)
        reuse_semaphores(nc)
        with ExitStack() as inner:
            g.gdn_qk = sb("gdn_qk", [P, 2 * HEADS, TP], inner)
            g.gdn_v = sb("gdn_v", [P, NT, BR], inner)
            g.gdn_ba = sb("gdn_ba", [P, NT, 2 * HEADS], inner)
            stage_gdn_in(nc, g, d, out)
            stage_gdn(nc, g, d, out)
            stage_gdn_out(nc, g, d)
        stage_merge(nc, g, d, "b", 1, False)

        branches.close()
        finish(nc, g, d, out)


def finish(nc, g, d, out):
    with ExitStack() as ctx:
        def sb(name, shape, dt=F32):
            return ctx.enter_context(nc.sbuf_tensor(name, shape, dt))

        g.logits = sb("route_logits", [P, NT, NL])
        g.choice_w = sb("choice_w", [P, 2, NT])
        g.slot_i = sb("slot_i", [P, 2, NT], U32)
        g.row_token = sb("row_token", [P, MT], U32)
        g.owner_i = sb("owner_i", [P, MT], I32)
        reuse_semaphores(nc)
        stage_project(nc, g, d)
        stage_route(nc, g, d)
        stage_experts(nc, g, d)
        stage_combine(nc, g, d, out)


INS = """x_prompt x_sample c_prompt c_sample state_gla state_gdn cache_gdn_conv state_s5_re state_s5_im
norm1_w norm2_w final_norm_w w_ada b_ada w_in w_alpha_up b_alpha gla_norm_w conv_w gdn_a_log gdn_dt_bias gdn_norm_w
s5_a_re s5_a_im s5_log_dt s5_b_re s5_b_im s5_c_re s5_c_im s5_d w_glu b_glu w_br_a w_br_b w_br_c w_gate b_gate w_out
w_route_group b_route_group w_route_expert b_route_expert w_exp_gate w_exp_up w_exp_down""".split()


def kernel(**inputs):
    import concourse.bacc as _bacc
    from concourse.bass_utils import run_bass_kernel_spmd as _run

    nc = _bacc.Bacc("TRN2", target_bir_lowering=False, num_devices=1)
    arrays, d = {}, {}
    for name in INS:
        arrays["in_" + name] = np.ascontiguousarray(inputs[name])
        d[name] = nc.dram_tensor("in_" + name, arrays["in_" + name].shape, F32, kind="ExternalInput").ap()
    out = [nc.dram_tensor(f"out_{i}", shape, F32, kind="ExternalOutput").ap() for i, shape in enumerate(OUT_SHAPES)]
    build(nc, d, out)
    result = _run(nc, [arrays], core_ids=[0])
    return tuple(result.results[0][f"out_{i}"] for i in range(len(OUT_SHAPES)))
```

```python
from contextlib import ExitStack

import numpy as np
import concourse.bass as bass
import concourse.mybir as mybir

F32 = mybir.dt.float32
I32 = mybir.dt.int32
U32 = mybir.dt.uint32
ALU = mybir.AluOpType
ACT = mybir.ActivationFunctionType
AX = mybir.AxisListType

P = 128
D = 1024
KD = D // P
SEQ = 1024
DEC = 64
TOK = SEQ + DEC
NT = 9
TP = NT * P
CHUNK = 64
EPS = 1e-6
BR = D // 2
KB = BR // P
HEADS = 4
GDK = 64
DV = 128
LOWR = 16
TAU = 16.0
CONVCH = 3 * BR
NCV = CONVCH // P
CW = 4
GROUPS = 32
GC = 16
ST = 64
PAIRS = GROUPS // 2
LB = 8
NBP = SEQ // LB
NBS = DEC // LB
NB = NBP + NBS
NE = 16
NG = 4
FF = D // 4
MT = 32
COL = dict(qa=0, ka=256, va=512, ga=1024, aa=1536, qkv=1552, beta=3088, a=3092, gb=3096, u=3608)
PIECES = [(0, 364), (364, 364), (728, 360)]
PW = 364


SOFTWARE_DMA = ("bias_loaded", "norm_loaded", "rows_loaded", "route_loaded", "scattered", "x_loaded0", "x_loaded1",
                "gathered0", "gathered1", "gathered2")


class Shared:
    pass


def rows_view(w):
    return w.rearrange("(k p) n -> p k n", p=P)


def stage_start(nc, g, d):
    with ExitStack() as ctx:
        def sb(name, shape, dt=F32):
            return ctx.enter_context(nc.sbuf_tensor(name, shape, dt))

        def sem(name):
            return (g.kept if name in SOFTWARE_DMA else ctx).enter_context(nc.semaphore(name))

        x_tiles = sb("x_tiles", [P, NT, D])
        x_sq = sb("x_sq", [P, D])
        x_ssq = sb("x_ssq", [P, NT])
        x_std = sb("x_std", [P, NT])
        x_rstd = sb("x_rstd", [P, NT])
        x_hat = sb("x_hat", [P, 2, D])
        c_cols = sb("c_cols", [P, KD, 2])
        c_silu = sb("c_silu", [P, KD, 2])
        ada_w = sb("ada_w", [P, 3, KD, 512])
        mod_rows = sb("mod_rows", [2, 6 * D])
        bias_rows = sb("bias_rows", [2, 6 * D])
        norm_cols = sb("norm_cols", [P, 2, KD])
        norm_scale = sb("norm_scale", [P, KD, 2])

        x_loaded = sem("x_loaded")
        c_loaded = sem("c_loaded")
        bias_loaded = sem("bias_loaded")
        norm_loaded = sem("norm_loaded")
        ada_loaded = [sem(f"ada_loaded{b}") for b in range(3)]
        masks_done = sem("masks_done")
        pad_zero = sem("pad_zero")
        ssq_done = sem("ssq_done")
        std_done = sem("std_done")
        rstd_done = sem("rstd_done")
        hat_done = sem("hat_done")
        turned = sem("turned")
        h_raw = sem("h_raw")
        silu_done = sem("silu_done")
        mod_psum = sem("mod_psum")
        mod_done = sem("mod_done")
        mod_stored = sem("mod_stored")
        mod_turned = sem("mod_turned")
        mod_cols_done = sem("mod_cols_done")
        scale_done = sem("scale_done")
        h_done = sem("h_done")

        turn_ps = [ctx.enter_context(nc.psum_tensor(f"turn_ps{b}", [P, 512], F32)) for b in range(4)]
        mod_ps = [ctx.enter_context(nc.psum_tensor(f"mod_ps{b}", [2, 512], F32)) for b in range(2)]
        cols_ps = ctx.enter_context(nc.psum_tensor("cols_ps", [P, 48, 2], F32))
        block = ctx.enter_context(nc.Block())
        ada_view = rows_view(d["w_ada"][0])

        @block.sync
        def _(sp):
            sp.dma_start(c_cols[:, :, 0], d["c_prompt"][0].rearrange("(k p) -> p k", p=P),
                         allow_slow_non_contiguous=True).then_inc(c_loaded, 16)
            sp.dma_start(c_cols[:, :, 1], d["c_sample"][0].rearrange("(k p) -> p k", p=P),
                         allow_slow_non_contiguous=True).then_inc(c_loaded, 16)
            sp.dma_start(x_tiles[:, 0:8, :], d["x_prompt"][0].rearrange("(i p) c -> p i c", p=P)).then_inc(x_loaded, 16)
            sp.dma_start(x_tiles[0:64, 8, :], d["x_sample"][0]).then_inc(x_loaded, 16)
            for b in range(3):
                sp.dma_start(ada_w[:, b], ada_view[:, :, 512 * b:512 * b + 512]).then_inc(ada_loaded[b], 16)
            with sp.Fori(1, 4) as r:
                for b in range(3):
                    sp.wait_ge(mod_psum, r * 3 + (b - 2))
                    sp.dma_start(ada_w[:, b], ada_view[:, :, bass.ds(r * 1536 + 512 * b, 512)]).then_inc(ada_loaded[b], 16)
            sp.wait_ge(mod_done, 12)
            sp.dma_start(g.mod_dram, mod_rows[:]).then_inc(mod_stored, 16)
            sp.wait_ge(mod_stored, 16)

        @block.gpsimd
        def _(pool):
            steps = [(t, slice(0, P), slice(0, P), 1.0) for t in (g.ident, g.upto, g.after, g.ones)]
            steps += [(g.eps, slice(0, P), slice(0, 1), EPS), (g.row_sel, slice(0, P), slice(0, 2 * P), 0.0)]
            steps += [(g.row_sel, slice(0, 64), slice(0, P), 1.0), (g.row_sel, slice(64, P), slice(P, 2 * P), 1.0)]
            n = 0
            for t, rows, cols, value in steps:
                if n:
                    pool.wait_ge(masks_done, n)
                nc.gpsimd.memset(t[rows, cols], value).then_inc(masks_done, 1)
                n += 1
            for t, op, step, cm in ((g.ident, ALU.is_equal, 1, -1), (g.upto, ALU.is_ge, 1, -1), (g.after, ALU.is_gt, -1, 1)):
                pool.wait_ge(masks_done, n)
                nc.gpsimd.affine_select(out=t[:], in_=t[:], compare_op=op, fill=0.0, base=0,
                                        pattern=[[step, P]], channel_multiplier=cm).then_inc(masks_done, 1)
                n += 1
            pool.wait_ge(masks_done, n)
            nc.gpsimd.memset(g.upto[0:64, 64:128], 0.0).then_inc(masks_done, 1)
            pool.wait_ge(masks_done, n + 1)
            nc.gpsimd.memset(g.after[64:128, 0:64], 0.0).then_inc(masks_done, 1)
            pool.dma_start(bias_rows[:], d["b_ada"].broadcast_to([2, 6 * D])).then_inc(bias_loaded, 16)
            pool.dma_start(norm_cols[:, 0], d["norm1_w"][0].rearrange("(k p) -> p k", p=P),
                           allow_slow_non_contiguous=True).then_inc(norm_loaded, 16)
            pool.dma_start(norm_cols[:, 1], d["norm2_w"][0].rearrange("(k p) -> p k", p=P),
                           allow_slow_non_contiguous=True).then_inc(norm_loaded, 16)

        @block.vector
        def _(dve):
            nc.vector.memset(x_tiles[64:128, 8, :], 0.0).then_inc(pad_zero, 1)
            dve.wait_ge(std_done, 1)
            nc.vector.reciprocal(x_rstd[:], x_std[:]).then_inc(rstd_done, 1)
            dve.wait_ge(rstd_done, 1)

            def normalise(i, b, freed):
                if freed is not None:
                    dve.wait_ge(turned, freed)
                nc.vector.tensor_scalar(x_hat[:, b], x_tiles[:, i] if isinstance(i, int) else x_tiles[:, bass.ds(i, 1)].rearrange("p o c -> p (o c)"),
                                        x_rstd[:, i:i + 1] if isinstance(i, int) else x_rstd[:, bass.ds(i, 1)],
                                        None, ALU.mult).then_inc(hat_done, 1)

            normalise(0, 0, None)
            normalise(1, 1, None)
            with dve.Fori(1, 4) as r:
                for b in range(2):
                    normalise(r * 2 + b, b, r * 2 + (b - 1))
            normalise(8, 0, 7)
            dve.wait_ge(bias_loaded, 16)
            with dve.Fori(0, 6) as r:
                for b in range(2):
                    dve.wait_ge(mod_psum, r * 2 + (b + 1))
                    sl = bass.ds(r * 1024 + 512 * b, 512)
                    nc.vector.tensor_tensor(mod_rows[:, sl], mod_ps[b][:], bias_rows[:, sl], ALU.add).then_inc(mod_done, 1)
            dve.wait_ge(mod_turned, 1)
            nc.vector.tensor_copy(g.mod_cols[:], cols_ps[:]).then_inc(mod_cols_done, 1)
            dve.wait_ge(mod_cols_done, 1)
            dve.wait_ge(norm_loaded, 32)
            nc.vector.tensor_scalar(norm_scale[:], g.mod_cols[:, KD:2 * KD, :], 1.0, None, ALU.add).then_inc(scale_done, 1)
            dve.wait_ge(scale_done, 1)
            nc.vector.tensor_tensor(norm_scale[:], norm_scale[:], norm_cols[:, 0, :].unsqueeze(2).broadcast_to([P, KD, 2]),
                                    ALU.mult).then_inc(scale_done, 1)
            dve.wait_ge(scale_done, 2)
            dve.wait_ge(h_raw, 2 * NT)
            for k in range(KD):
                for who, (a, b) in enumerate(((0, SEQ), (SEQ, TOK))):
                    nc.vector.tensor_scalar(g.h[:, k, a:b], g.h[:, k, a:b], norm_scale[:, k, who:who + 1],
                                            g.mod_cols[:, k, who:who + 1], ALU.mult, ALU.add).then_inc(h_done, 1)

        @block.scalar
        def _(act):
            act.wait_ge(c_loaded, 32)
            nc.scalar.activation(c_silu[:], c_cols[:], ACT.Silu).then_inc(silu_done, 1)
            act.wait_ge(x_loaded, 32)
            act.wait_ge(pad_zero, 1)
            for i in range(NT):
                if i:
                    act.wait_ge(ssq_done, i)
                nc.scalar.activation(x_sq[:], x_tiles[:, i], ACT.Square, accum_out=x_ssq[:, i:i + 1]).then_inc(ssq_done, 1)
            act.wait_ge(ssq_done, NT)
            act.wait_ge(masks_done, 13)
            nc.scalar.activation(x_std[:], x_ssq[:], ACT.Sqrt, scale=1.0 / D, bias=g.eps[:]).then_inc(std_done, 1)

            def unload(i, b):
                for q in range(2):
                    act.wait_ge(turned, i + 1)
                    dst = g.h[:, 4 * q:4 * q + 4, bass.ds(i * P, P)] if not isinstance(i, int) else g.h[:, 4 * q:4 * q + 4, i * P:i * P + P]
                    nc.scalar.activation(dst, turn_ps[2 * b + q][:].rearrange("p (k t) -> p k t", k=4), ACT.Copy).then_inc(h_raw, 1)

            with act.Fori(0, 4) as r:
                for b in range(2):
                    unload(r * 2 + b, b)
            unload(8, 0)

        @block.tensor
        def _(pe):
            pe.wait_ge(masks_done, 13)

            def turn(i, b, freed):
                pe.wait_ge(hat_done, i + 1)
                if freed is not None:
                    pe.wait_ge(h_raw, freed)
                for k in range(KD):
                    last = nc.tensor.transpose(turn_ps[2 * b + k // 4][:, P * (k % 4):P * (k % 4) + P],
                                               x_hat[:, b, P * k:P * k + P], g.ident[:])
                last.then_inc(turned, 1)

            turn(0, 0, None)
            turn(1, 1, None)
            with pe.Fori(1, 4) as r:
                for b in range(2):
                    turn(r * 2 + b, b, r * 4 + (2 * b - 2))
            turn(8, 0, 14)
            pe.wait_ge(silu_done, 1)

            def ada(s, b, q, rounds, freed):
                pe.wait_ge(ada_loaded[b], rounds)
                if freed is not None:
                    pe.wait_ge(mod_done, freed)
                for k in range(KD):
                    last = nc.tensor.matmul(mod_ps[q][:], c_silu[:, k], ada_w[:, b, k], start=k == 0, stop=k == KD - 1)
                last.then_inc(mod_psum, 1)

            ada(0, 0, 0, 16, None)
            ada(1, 1, 1, 16, None)
            for s in range(2, 12):
                ada(s, s % 3, s % 2, 16 * (s // 3 + 1), s - 1)
            pe.wait_ge(mod_done, 12)
            for j in range(48):
                last = nc.tensor.transpose(cols_ps[:, j, :], mod_rows[0:2, P * j:P * j + P], g.ident[0:2, 0:2])
            last.then_inc(mod_turned, 1)



TWO_PI_HI = 6.28125
TWO_PI_LO = 2 * float(np.pi) - TWO_PI_HI
PI_IN = 3.1415925


def stage_s5_tables(nc, g, d):
    with ExitStack() as ctx:
        def sb(name, shape, dt=F32):
            return ctx.enter_context(nc.sbuf_tensor(name, shape, dt))

        def sem(name):
            return ctx.enter_context(nc.semaphore(name))

        a_re, a_im, log_dt, dt, z_re, z_im, mag, turns, sin_z, sin_half, cos_z, num, den, t_a, t_b = (
            sb(f"s5_{n}", [P, PAIRS]) for n in
            "a_re a_im log_dt dt z_re z_im mag turns sin_z sin_half cos_z num den t_a t_b".split())
        whole = sb("s5_whole_turns", [P, PAIRS], I32)
        coef = sb("s5_coef", [P, 2, PAIRS])
        b_in = sb("s5_b_in", [P, 2, PAIRS, GC])
        c_rows = sb("s5_c_rows", [P, 2, 2, P])
        powers = sb("s5_powers", [P, 4, 3, PAIRS])
        b_pow = sb("s5_b_pow", [P, 2, PAIRS, LB, GC])
        tmp = sb("s5_tmp", [P, 2, 2, PAIRS, 4 * GC])
        lags = sb("s5_lags", [GC, GROUPS, LB, GC])
        d_cols = sb("s5_d_cols", [GC, GROUPS])
        d_diag = sb("s5_d_diag", [GC, GROUPS, GC])

        mix_space = g.mix[:].rearrange("p k t -> p (k t)")
        w_u = mix_space[:, 0:KD * BR].rearrange("p (k c) -> p k c", k=KD)
        space_s = mix_space[0:NBS, 0:LB * BR]
        space_p = mix_space[:, LB * BR:2 * LB * BR]
        u_rows_s = mix_space[0:DEC, 2 * LB * BR:2 * LB * BR + BR]
        u_p, u_s = (x.rearrange("b (g l c) -> b g l c", l=LB, c=GC) for x in (space_p, space_s))
        u_cols = g.branch[:].rearrange("p k t -> p (k t)").rearrange("p (g b) -> p g b", b=NB)
        GQ = GROUPS // 2

        w_loaded = sem("w_u_loaded")
        u_psum = sem("u_psum")
        u_out = sem("u_out")
        u_rows_in = sem("u_rows_in")
        u_turned = sem("u_turned")
        u_cols_done = sem("u_cols_done")
        loaded = sem("s5_loaded")
        b_loaded = sem("s5_b_loaded")
        c_loaded = sem("s5_c_loaded")
        step = sem("s5_step")
        acts = sem("s5_acts")
        dt_ready = sem("s5_dt_ready")
        z_ready = sem("s5_z_ready")
        reduced = sem("s5_reduced")
        c_turned = sem("s5_c_turned")
        b_ready = sem("s5_b_ready")
        q_ready = sem("s5_q_ready")
        b_turned = sem("s5_b_turned")
        b_cols_done = sem("s5_b_cols_done")
        lag_psum = sem("s5_lag_psum")
        lag_out = sem("s5_lag_out")
        lags_done = sem("s5_lags_done")
        zeroed = sem("s5_zeroed")
        placed = sem("s5_placed")
        turn_ps = [ctx.enter_context(nc.psum_tensor(f"s5_turn_ps{b}", [P, 512], F32)) for b in range(4)]
        lag_ps = [ctx.enter_context(nc.psum_tensor(f"s5_lag_ps{b}", [GC, 4, LB, GC], F32)) for b in range(2)]
        u_ps = [ctx.enter_context(nc.psum_tensor(f"u_ps{b}", [P, 512], F32)) for b in range(2)]
        block = ctx.enter_context(nc.Block())

        @block.sync
        def _(sp):
            sp.dma_start(w_u, rows_view(d["w_in"][0])[:, :, COL["u"]:COL["u"] + BR]).then_inc(w_loaded, 16)
            sp.dma_start(a_re[:], d["s5_a_re"][0].rearrange("(p h) s -> (h s) p", h=2),
                         allow_slow_non_contiguous=True).then_inc(loaded, 16)
            sp.dma_start(a_im[:], d["s5_a_im"][0].rearrange("(p h) s -> (h s) p", h=2),
                         allow_slow_non_contiguous=True).then_inc(loaded, 16)
            for h in range(2):
                src = d["s5_log_dt"][0].rearrange("(p h) -> h p", h=2)[h:h + 1, :].broadcast_to([ST, PAIRS])
                sp.dma_start(log_dt[ST * h:ST * h + ST, :], src, allow_slow_non_contiguous=True).then_inc(loaded, 16)
            for r, name in enumerate(("s5_b_re", "s5_b_im")):
                sp.dma_start(b_in[:, r], d[name][0].rearrange("(p h) s c -> (h s) p c", h=2)).then_inc(b_loaded, 16)
            for r, name in enumerate(("s5_c_re", "s5_c_im")):
                for p in range(PAIRS):
                    src = d[name][0, 2 * p:2 * p + 2].rearrange("h c s -> c h s")
                    sp.dma_start(c_rows[GC * (p % 8):GC * (p % 8) + GC, r, p // 8].rearrange("c (h s) -> c h s", h=2),
                                 src).then_inc(c_loaded, 16)
            sp.dma_start(d_cols[:], d["s5_d"][0].rearrange("(g c) -> c g", c=GC),
                         allow_slow_non_contiguous=True).then_inc(loaded, 16)
            sp.wait_ge(u_psum, LB + 1)
            sp.wait_ge(u_out, LB + 1)
            for l in range(LB):
                sp.dma_start(u_s[:, :, l], u_rows_s[l:DEC:LB].rearrange("b (g c) -> b g c", c=GC)).then_inc(u_rows_in, 16)
            sp.wait_ge(lags_done, 1)
            sp.wait_ge(zeroed, 1)
            for l in range(LB):
                sp.dma_start(g.s5_toeplitz[GC * l:GC * l + GC, :, l:, :], lags[:, :, 0:LB - l, :]).then_inc(placed, 16)
            sp.wait_ge(placed, 16 * LB)

        @block.gpsimd
        def _(pool):
            nc.gpsimd.memset(g.s5_toeplitz[:], 0.0).then_inc(zeroed, 1)

        @block.scalar
        def _(act):
            act.wait_ge(loaded, 80)
            nc.scalar.activation(dt[:], log_dt[:], ACT.Exp).then_inc(dt_ready, 1)
            act.wait_ge(z_ready, 1)
            nc.scalar.activation(mag[:], z_re[:], ACT.Exp).then_inc(acts, 1)
            act.wait_ge(reduced, 1)
            nc.scalar.activation(sin_z[:], turns[:], ACT.Sin).then_inc(acts, 1)
            nc.scalar.activation(sin_half[:], turns[:], ACT.Sin, scale=0.5).then_inc(acts, 1)
            for l in range(LB):
                act.wait_ge(u_psum, l + 1)
                nc.scalar.activation(u_p[:, :, l], u_ps[l % 2][:].rearrange("p (g c) -> p g c", c=GC), ACT.Copy).then_inc(u_out, 1)
            act.wait_ge(u_psum, LB + 1)
            nc.scalar.activation(u_rows_s, u_ps[0][0:DEC, :], ACT.Copy).then_inc(u_out, 1)
            for q in range(GQ):
                act.wait_ge(u_turned, q + 1)
                nc.scalar.activation(u_cols[:, 2 * q:2 * q + 2], u_ps[q % 2][:, 0:2 * NB].rearrange("p (a n) -> p a n", a=2),
                                     ACT.Copy).then_inc(u_cols_done, 1)
            for q in range(8):
                act.wait_ge(b_turned, q + 1)
                r, p = q // 4, 4 * (q % 4)
                nc.scalar.activation(g.s5_b_cols[:, r, p:p + 4, :], turn_ps[q % 4][:].rearrange("p (a s) -> p a s", a=4),
                                     ACT.Copy).then_inc(b_cols_done, 1)

        @block.vector
        def _(dve):
            n = [0]

            def link(ins):
                n[0] += 1
                ins.then_inc(step, 1)
                dve.wait_ge(step, n[0])

            def tt(out, a, b, op):
                link(nc.vector.tensor_tensor(out, a, b, op))

            def ts(out, a, s1, s2, op0, op1=None):
                link(nc.vector.tensor_scalar(out, a, s1, s2, op0, op1) if op1 is not None else
                     nc.vector.tensor_scalar(out, a, s1, None, op0))

            dve.wait_ge(loaded, 80)
            dve.wait_ge(dt_ready, 1)
            tt(z_re[:], a_re[:], dt[:], ALU.mult)
            tt(z_im[:], a_im[:], dt[:], ALU.mult)
            ts(turns[:], z_im[:], 1.0 / (TWO_PI_HI + TWO_PI_LO), None, ALU.mult)
            link(nc.vector.tensor_copy(whole[:], turns[:]))
            nc.vector.tensor_copy(t_a[:], whole[:]).then_inc(z_ready, 1)
            dve.wait_ge(z_ready, 1)
            link(nc.vector.scalar_tensor_tensor(turns[:], t_a[:], -TWO_PI_HI, z_im[:], ALU.mult, ALU.add))
            link(nc.vector.scalar_tensor_tensor(turns[:], t_a[:], -TWO_PI_LO, turns[:], ALU.mult, ALU.add))
            nc.vector.tensor_scalar(turns[:], turns[:], -PI_IN, PI_IN, ALU.max, ALU.min).then_inc(reduced, 1)
            dve.wait_ge(acts, 3)
            tt(t_a[:], sin_half[:], sin_half[:], ALU.mult)
            ts(cos_z[:], t_a[:], -2.0, 1.0, ALU.mult, ALU.add)
            tt(powers[:, 0, 0], mag[:], cos_z[:], ALU.mult)
            tt(powers[:, 0, 1], mag[:], sin_z[:], ALU.mult)
            for q in range(4):
                ts(powers[:, q, 2], powers[:, q, 1], -1.0, None, ALU.mult)
                if q == 3:
                    break
                tt(t_a[:], powers[:, q, 0], powers[:, q, 1], ALU.subtract)
                tt(t_b[:], powers[:, q, 0], powers[:, q, 1], ALU.add)
                tt(powers[:, q + 1, 0], t_a[:], t_b[:], ALU.mult)
                link(nc.vector.scalar_tensor_tensor(powers[:, q + 1, 1], powers[:, q, 0], 2.0, powers[:, q, 1],
                                                    ALU.mult, ALU.mult))
            link(nc.vector.tensor_copy(g.s5_step[:, 0, 0], powers[:, 3, 0]))
            link(nc.vector.tensor_copy(g.s5_step[:, 0, 1], powers[:, 3, 0]))
            link(nc.vector.tensor_copy(g.s5_step[:, 1, 0], powers[:, 3, 1]))
            link(nc.vector.tensor_copy(g.s5_step[:, 1, 1], powers[:, 3, 2]))
            ts(num[:], powers[:, 0, 0], -1.0, None, ALU.add)
            tt(t_a[:], a_re[:], a_re[:], ALU.mult)
            tt(t_b[:], a_im[:], a_im[:], ALU.mult)
            tt(den[:], t_a[:], t_b[:], ALU.add)
            link(nc.vector.reciprocal(den[:], den[:]))
            tt(t_a[:], num[:], a_re[:], ALU.mult)
            tt(t_b[:], powers[:, 0, 1], a_im[:], ALU.mult)
            tt(t_a[:], t_a[:], t_b[:], ALU.add)
            tt(coef[:, 0], t_a[:], den[:], ALU.mult)
            tt(t_a[:], powers[:, 0, 1], a_re[:], ALU.mult)
            tt(t_b[:], num[:], a_im[:], ALU.mult)
            tt(t_a[:], t_a[:], t_b[:], ALU.subtract)
            tt(coef[:, 1], t_a[:], den[:], ALU.mult)
            ts(t_a[:], coef[:, 1], -1.0, None, ALU.mult)
            dve.wait_ge(b_loaded, 32)

            def times(out, a, w_re, w_a, w_b, width):
                def wide(w):
                    return w.unsqueeze(2).broadcast_to([P, PAIRS, width])
                for r in range(2):
                    tt(tmp[:, 0, r, :, 0:width], a[r], wide(w_re), ALU.mult)
                tt(tmp[:, 1, 0, :, 0:width], a[1], wide(w_a), ALU.mult)
                tt(tmp[:, 1, 1, :, 0:width], a[0], wide(w_b), ALU.mult)
                for r in range(2):
                    tt(out[r], tmp[:, 0, r, :, 0:width], tmp[:, 1, r, :, 0:width], ALU.add)

            def b_at(lo, hi):
                return [b_pow[:, r, :, lo:hi, :].rearrange("p a l c -> p a (l c)") for r in range(2)]

            def q_at(lo, hi):
                return [g.s5_c_pow[:, r, :, lo:hi, :].rearrange("p a l c -> p a (l c)") for r in range(2)]

            times(b_at(7, 8), [b_in[:, 0], b_in[:, 1]], coef[:, 0], t_a[:], coef[:, 1], GC)
            times(b_at(6, 7), b_at(7, 8), powers[:, 0, 0], powers[:, 0, 2], powers[:, 0, 1], GC)
            times(b_at(4, 6), b_at(6, 8), powers[:, 1, 0], powers[:, 1, 2], powers[:, 1, 1], 2 * GC)
            times(b_at(0, 4), b_at(4, 8), powers[:, 2, 0], powers[:, 2, 2], powers[:, 2, 1], 4 * GC)
            nc.vector.tensor_copy(t_b[:], t_a[:]).then_inc(b_ready, 1)
            dve.wait_ge(c_turned, 1)
            for r in range(2):
                for half in range(2):
                    src = turn_ps[2 * r + half][:, 0:P].rearrange("p (a c) -> p a c", c=GC)
                    ts(g.s5_c_pow[:, r, 8 * half:8 * half + 8, 0, :], src, -1.0 if r else 1.0, None, ALU.mult)
            times(q_at(1, 2), q_at(0, 1), powers[:, 0, 0], powers[:, 0, 1], powers[:, 0, 2], GC)
            times(q_at(2, 4), q_at(0, 2), powers[:, 1, 0], powers[:, 1, 1], powers[:, 1, 2], 2 * GC)
            times(q_at(4, 8), q_at(0, 4), powers[:, 2, 0], powers[:, 2, 1], powers[:, 2, 2], 4 * GC)
            times(q_at(8, 9), q_at(0, 1), powers[:, 3, 0], powers[:, 3, 1], powers[:, 3, 2], GC)
            nc.vector.tensor_copy(t_b[:], t_a[:]).then_inc(q_ready, 1)
            for q in range(8):
                dve.wait_ge(lag_psum, q + 1)
                first = 8 * (q // 2) + q % 2
                nc.vector.tensor_copy(lags[:, first:first + 7:2], lag_ps[q % 2][:]).then_inc(lag_out, 1)
            tt(d_diag[:], g.ident[0:GC, 0:GC].unsqueeze(1).broadcast_to([GC, GROUPS, GC]),
               d_cols[:].unsqueeze(2).broadcast_to([GC, GROUPS, GC]), ALU.mult)
            dve.wait_ge(lag_out, 8)
            nc.vector.tensor_tensor(lags[:, :, 0, :], lags[:, :, 0, :], d_diag[:], ALU.add).then_inc(lags_done, 1)

        @block.tensor
        def _(pe):
            def u_of(l):
                if l >= 2:
                    pe.wait_ge(u_out, l - 1)
                for k in range(KD):
                    last = nc.tensor.matmul(u_ps[l % 2][:], g.h[:, k, l:SEQ:LB], w_u[:, k], start=k == 0, stop=k == KD - 1)
                last.then_inc(u_psum, 1)

            pe.wait_ge(w_loaded, 16)
            u_of(0)
            u_of(1)
            pe.wait_ge(c_loaded, 32 * PAIRS)
            for r in range(2):
                for half in range(2):
                    last = nc.tensor.transpose(turn_ps[2 * r + half][:, 0:P], c_rows[:, r, half], g.ident[:])
            last.then_inc(c_turned, 1)
            for l in range(2, LB):
                u_of(l)
            pe.wait_ge(u_out, LB - 1)
            for k in range(KD):
                last = nc.tensor.matmul(u_ps[0][0:DEC, :], g.h[:, k, SEQ:TOK], w_u[:, k], start=k == 0, stop=k == KD - 1)
            last.then_inc(u_psum, 1)
            pe.wait_ge(u_out, LB + 1)
            pe.wait_ge(u_rows_in, 16 * LB)
            for q in range(GQ):
                if q >= 2:
                    pe.wait_ge(u_cols_done, q - 1)
                for a in range(2):
                    grp = 2 * q + a
                    nc.tensor.transpose(u_ps[q % 2][:, NB * a:NB * a + NBP], space_p[:, P * grp:P * grp + P], g.ident[:])
                    last = nc.tensor.transpose(u_ps[q % 2][:, NB * a + NBP:NB * a + NB], space_s[:, P * grp:P * grp + P],
                                               g.ident[0:NBS, 0:NBS])
                last.then_inc(u_turned, 1)
            pe.wait_ge(q_ready, 1)
            for q in range(8):
                if q >= 4:
                    pe.wait_ge(b_cols_done, q - 3)
                r, p = q // 4, 4 * (q % 4)
                for a in range(4):
                    last = nc.tensor.transpose(turn_ps[q % 4][:, P * a:P * a + P],
                                               b_pow[:, r, p + a].rearrange("p l c -> p (l c)"), g.ident[:])
                last.then_inc(b_turned, 1)
            for q in range(8):
                if q >= 2:
                    pe.wait_ge(lag_out, q - 1)
                for a in range(4):
                    pair, h = 4 * (q // 2) + a, q % 2
                    rows = slice(ST * h, ST * h + ST)
                    for r in range(2):
                        last = nc.tensor.matmul(lag_ps[q % 2][:, a], b_pow[rows, r, pair, LB - 1, :],
                                                g.s5_c_pow[rows, r, pair, 0:LB, :], start=a == 0 and r == 0,
                                                stop=a == 3 and r == 1, skip_group_check=True)
                last.then_inc(lag_psum, 1)


def stage_s5(nc, g, d, out):
    with ExitStack() as ctx:
        def sb(name, shape, dt=F32):
            return ctx.enter_context(nc.sbuf_tensor(name, shape, dt))

        def sem(name):
            return ctx.enter_context(nc.semaphore(name))

        space_p = sb("s5_blocks_p", [P, LB * BR])
        space_s = sb("s5_blocks_s", [NBS, LB * BR])
        blocks_p, blocks_s = (x[:].rearrange("b (l c) -> b l c", l=LB) for x in (space_p, space_s))
        u_cols = g.branch[:].rearrange("p k t -> p (k t)").rearrange("p (g b) -> p g b", b=NB)
        before_space = sb("s5_before", [P, (NB + 2) * 2 * PAIRS])
        before = before_space[:].rearrange("p (n r a) -> p n r a", r=2, a=PAIRS)
        first_s = NBP + 1
        prod = sb("s5_prod", [P, 2, 2, PAIRS])
        w_gate = sb("s5_w_gate", [P, 2, KD, P])
        b_gate = sb("s5_b_gate", [P, KD])

        state_in = sem("s5_state_in")
        zero_state = sem("s5_zero_state")
        v_psum = sem("s5_v_psum")
        v_done = sem("s5_v_done")
        scan = sem("s5_scan")
        gate_loaded = [sem(f"s5_gate_loaded{b}") for b in range(2)]
        bias_loaded = sem("s5_bias_loaded")
        gate_psum = sem("s5_gate_psum")
        gate_done = sem("s5_gate_done")
        y_psum = sem("s5_y_psum")
        y_done = sem("s5_y_done")
        y_turned = sem("s5_y_turned")
        y_cols_done = sem("s5_y_cols_done")
        stored = sem("s5_stored")
        ps = [ctx.enter_context(nc.psum_tensor(f"s5_ps{b}", [P, 512], F32)) for b in range(8)]
        block = ctx.enter_context(nc.Block())
        SETS = [(h, 4 * q) for q in range(PAIRS // 4) for h in range(2)]

        def groups_of(h, pair0):
            return slice(2 * pair0 + h, 2 * pair0 + h + 7, 2)

        @block.sync
        def _(sp):
            gate_view = rows_view(d["w_gate"][0])
            sp.dma_start(b_gate[:], d["b_gate"][0].rearrange("(b k p) -> b p k", p=P, b=3)[2],
                         allow_slow_non_contiguous=True).then_inc(bias_loaded, 16)
            for j in range(2):
                sp.dma_start(w_gate[:, j], gate_view[:, :, 2 * D + P * j:2 * D + P * j + P]).then_inc(gate_loaded[j], 16)
            for r, name in enumerate(("state_s5_re", "state_s5_im")):
                sp.dma_start(before[:, first_s, r], d[name][0, 0].rearrange("(p h) s -> (h s) p", h=2),
                             allow_slow_non_contiguous=True).then_inc(state_in, 16)
            with sp.Fori(1, KD // 2) as r:
                for b in range(2):
                    sp.wait_ge(gate_psum, r * 6 + (3 * b - 3))
                    sp.dma_start(w_gate[:, b], gate_view[:, :, bass.ds(r * (2 * P) + (2 * D + P * b), P)]).then_inc(gate_loaded[b], 16)
            sp.wait_ge(scan, 3 * NB)
            n = 0
            for where, at in ((0, NBP), (1, first_s + NBS)):
                for r in range(2):
                    sp.dma_start(out["s5"][where][r][0, 0].rearrange("(p h) s -> (h s) p", h=2), before[:, at, r],
                                 allow_slow_non_contiguous=True).then_inc(stored, 16)
                    n += 1
            sp.wait_ge(stored, 16 * n)

        @block.tensor
        def _(pe):
            for p in range(PAIRS):
                if p >= 4:
                    pe.wait_ge(v_done, p - 3)
                for r in range(2):
                    for h in range(2):
                        last = nc.tensor.matmul(ps[p % 4][ST * h:ST * h + ST, NB * r:NB * r + NB],
                                                g.s5_b_cols[:, r, p, ST * h:ST * h + ST], u_cols[:, 2 * p + h],
                                                start=r == 0, stop=r == 1, skip_group_check=True)
                last.then_inc(v_psum, 1)
            for j in range(KD):
                pe.wait_ge(gate_loaded[j % 2], 16 * (j // 2 + 1))
                for n, (at, width) in enumerate(PIECES):
                    if j:
                        pe.wait_ge(gate_done, 3 * j + n - 2)
                    else:
                        pe.wait_ge(v_done, PAIRS)
                    for k in range(KD):
                        last = nc.tensor.matmul(ps[n][:, 0:width], w_gate[:, j % 2, k], g.h[:, k, at:at + width],
                                                start=k == 0, stop=k == KD - 1)
                    last.then_inc(gate_psum, 1)
            pe.wait_ge(scan, 3 * NB)
            for q, (h, pair0) in enumerate(SETS):
                for s, (lo, hi, at) in enumerate(((0, NBP, 0), (NBP, NB, first_s))):
                    if q >= 2:
                        pe.wait_ge(y_done, 2 * (q - 2) + s + 1)
                    y = ps[4 + 2 * (q % 2) + s]
                    n = hi - lo
                    for a in range(4):
                        pair = pair0 + a
                        grp = 2 * pair + h
                        dst = y[0:n, P * a:P * a + P]
                        nc.tensor.matmul(dst, u_cols[:, grp, lo:hi], g.s5_toeplitz[:, grp].rearrange("p l c -> p (l c)"),
                                         start=a == 0, stop=False, skip_group_check=True)
                    for a in range(4):
                        pair = pair0 + a
                        dst = y[0:n, P * a:P * a + P]
                        rows = slice(ST * h, ST * h + ST)
                        for r in range(2):
                            last = nc.tensor.matmul(dst, before[rows, at:at + n, r, pair], g.s5_c_pow[rows, r, pair, 1:LB + 1, :],
                                                    start=False, stop=a == 3 and r == 1, skip_group_check=True)
                    last.then_inc(y_psum, 1)
            pe.wait_ge(y_done, 2 * len(SETS))
            pe.wait_ge(gate_done, 3 * KD)
            n = 0
            for ct in range(KB):
                for q in range(3):
                    if n >= 4:
                        pe.wait_ge(y_cols_done, n - 3)
                    t = ps[n % 4]
                    if q < 2:
                        for a in range(4):
                            last = nc.tensor.transpose(t[:, P * a:P * a + P], blocks_p[:, 4 * q + a, P * ct:P * ct + P], g.ident[:])
                    else:
                        for a in range(LB):
                            last = nc.tensor.transpose(t[:, NBS * a:NBS * a + NBS], blocks_s[:, a, P * ct:P * ct + P],
                                                       g.ident[0:NBS, 0:NBS])
                    last.then_inc(y_turned, 1)
                    n += 1

        @block.scalar
        def _(act):
            for p in range(PAIRS):
                act.wait_ge(v_psum, p + 1)
                v = ps[p % 4][:, 0:2 * NB].rearrange("p (r n) -> p n r", r=2)
                nc.scalar.activation(before[:, 1:NBP + 1, :, p], v[:, 0:NBP], ACT.Copy)
                nc.scalar.activation(before[:, first_s + 1:first_s + 1 + NBS, :, p], v[:, NBP:NB], ACT.Copy).then_inc(v_done, 1)
            act.wait_ge(bias_loaded, 16)
            for j in range(KD):
                for n, (at, width) in enumerate(PIECES):
                    act.wait_ge(gate_psum, 3 * j + n + 1)
                    nc.scalar.activation(g.mix[:, j, at:at + width], ps[n][:, 0:width], ACT.Sigmoid,
                                         bias=b_gate[:, j:j + 1]).then_inc(gate_done, 1)
            for q, (h, pair0) in enumerate(SETS):
                for s, (dst, n) in enumerate(((blocks_p, NBP), (blocks_s, NBS))):
                    act.wait_ge(y_psum, 2 * q + s + 1)
                    to = dst[0:n].rearrange("p l (g c) -> p g l c", c=GC)[:, groups_of(h, pair0)]
                    src = ps[4 + 2 * (q % 2) + s][0:n, :].rearrange("p (a l c) -> p a l c", a=4, c=GC)
                    for a in range(4):
                        last = nc.scalar.activation(to[:, a], src[:, a], ACT.Gelu_apprx_tanh)
                    last.then_inc(y_done, 1)

        @block.vector
        def _(dve):
            nc.vector.memset(before[:, 0], 0.0).then_inc(zero_state, 1)
            dve.wait_ge(zero_state, 1)
            dve.wait_ge(state_in, 32)
            dve.wait_ge(v_done, PAIRS)

            def advance(at, base):
                def h(n):
                    return before[:, bass.ds(n, 1)].rearrange("p o r a -> p (o r) a") if not isinstance(n, int) else before[:, n]
                now, nxt = h(at), h(at + 1)
                nc.vector.tensor_tensor(prod[:], now.unsqueeze(1).broadcast_to([P, 2, 2, PAIRS]), g.s5_step[:], ALU.mult).then_inc(scan, 1)
                dve.wait_ge(scan, base + 1)
                nc.vector.tensor_tensor(nxt, nxt, prod[:, 0], ALU.add).then_inc(scan, 1)
                dve.wait_ge(scan, base + 2)
                nc.vector.tensor_tensor(nxt, nxt, prod[:, 1, ::-1], ALU.add).then_inc(scan, 1)
                dve.wait_ge(scan, base + 3)

            for b in range(NBS):
                advance(first_s + b, 3 * b)
            with dve.Fori(0, NBP // 4) as r:
                for b in range(4):
                    advance(r * 4 + b, r * 12 + (3 * b + 3 * NBS))
            n = 0
            for ct in range(KB):
                for q in range(3):
                    dve.wait_ge(y_turned, n + 1)
                    t = ps[n % 4]
                    if q < 2:
                        to = g.branch[:, ct, 0:SEQ].rearrange("p (b l) -> p l b", l=LB)[:, 4 * q:4 * q + 4]
                        src = t[:].rearrange("p (l b) -> p l b", l=4)
                    else:
                        to = g.branch[:, ct, SEQ:TOK].rearrange("p (b l) -> p l b", l=LB)
                        src = t[:, 0:DEC].rearrange("p (l b) -> p l b", l=LB)
                    nc.vector.tensor_copy(to, src).then_inc(y_cols_done, 1)
                    n += 1


def stage_glu(nc, g, d):
    with ExitStack() as ctx:
        def sb(name, shape):
            return ctx.enter_context(nc.sbuf_tensor("glu_" + name, shape, F32))

        w = sb("w", [P, KB, BR])
        w_br = sb("w_br", [P, KB, D])
        bias = sb("bias", [P, KB])
        gate = sb("gate", [P, KB, PW])
        loaded, br_loaded, psum, gate_done, done, br_psum, mixed = (ctx.enter_context(nc.semaphore(f"glu_{n}")) for n in (
            "loaded", "br_loaded", "psum", "gate_done", "done", "br_psum", "mixed"))
        ps = [ctx.enter_context(nc.psum_tensor(f"glu_ps{b}", [P, 512], F32)) for b in range(8)]
        block = ctx.enter_context(nc.Block())

        @block.sync
        def _(sp):
            sp.dma_start(w[:], rows_view(d["w_glu"][0])).then_inc(loaded, 16)
            sp.dma_start(bias[:], d["b_glu"][0].rearrange("(k p) -> p k", p=P), allow_slow_non_contiguous=True).then_inc(loaded, 16)
            sp.dma_start(w_br[:], rows_view(d["w_br_c"][0])).then_inc(br_loaded, 16)

        @block.tensor
        def _(pe):
            def gates(n):
                at, width = PIECES[n]
                for j in range(KB):
                    if n:
                        pe.wait_ge(gate_done, KB * (n - 1) + j + 1)
                    for k in range(KB):
                        last = nc.tensor.matmul(ps[j][:, 0:width], w[:, k, P * j:P * j + P], g.branch[:, k, at:at + width],
                                                start=k == 0, stop=k == KB - 1)
                    last.then_inc(psum, 1)

            def project(n):
                at, width = PIECES[n]
                pe.wait_ge(done, KB * (n + 1))
                for j in range(KD):
                    q = KD * n + j
                    if q >= 4:
                        pe.wait_ge(mixed, q - 3)
                    for k in range(KB):
                        last = nc.tensor.matmul(ps[4 + q % 4][:, 0:width], w_br[:, k, P * j:P * j + P], g.branch[:, k, at:at + width],
                                                start=k == 0, stop=k == KB - 1)
                    last.then_inc(br_psum, 1)

            pe.wait_ge(loaded, 32)
            gates(0)
            gates(1)
            pe.wait_ge(br_loaded, 16)
            project(0)
            gates(2)
            project(1)
            project(2)

        @block.scalar
        def _(act):
            act.wait_ge(loaded, 32)
            for n, (at, width) in enumerate(PIECES):
                for j in range(KB):
                    act.wait_ge(psum, KB * n + j + 1)
                    if n:
                        act.wait_ge(done, KB * (n - 1) + j + 1)
                    nc.scalar.activation(gate[:, j, 0:width], ps[j][:, 0:width], ACT.Sigmoid, bias=bias[:, j:j + 1]).then_inc(gate_done, 1)

        @block.vector
        def _(dve):
            def glu(n):
                at, width = PIECES[n]
                dve.wait_ge(psum, KB * (n + 1))
                for j in range(KB):
                    dve.wait_ge(gate_done, KB * n + j + 1)
                    y = g.branch[:, j, at:at + width]
                    nc.vector.tensor_tensor(y, gate[:, j, 0:width], y, ALU.mult).then_inc(done, 1)

            def mix(n):
                at, width = PIECES[n]
                for j in range(KD):
                    q = KD * n + j
                    dve.wait_ge(br_psum, q + 1)
                    to = g.mix[:, j, at:at + width]
                    nc.vector.tensor_tensor(to, to, ps[4 + q % 4][:, 0:width], ALU.mult).then_inc(mixed, 1)

            glu(0)
            glu(1)
            mix(0)
            glu(2)
            mix(1)
            mix(2)


def stage_merge(nc, g, d, name, index, first):
    with ExitStack() as ctx:
        w = [ctx.enter_context(nc.sbuf_tensor(f"{name}_merge_w{b}", [P, KD + KB, P], F32)) for b in range(2)]
        bias = ctx.enter_context(nc.sbuf_tensor(f"{name}_b_gate", [P, KD], F32))
        gate = [ctx.enter_context(nc.sbuf_tensor(f"{name}_gate{b}", [P, PW], F32)) for b in range(3)]

        def sem(what):
            return ctx.enter_context(nc.semaphore(f"{name}_{what}"))

        bias_loaded = sem("bias_loaded")
        w_loaded = [sem(f"merge_w_loaded{b}") for b in range(2)]
        gate_psum = sem("gate_psum")
        br_psum = sem("br_psum")
        gate_done = sem("gate_done")
        gated = sem("gated")
        added = sem("added")
        gate_ps = [ctx.enter_context(nc.psum_tensor(f"{name}_gate_ps{b}", [P, 512], F32)) for b in range(3)]
        br_ps = [ctx.enter_context(nc.psum_tensor(f"{name}_br_ps{b}", [P, 512], F32)) for b in range(3)]
        block = ctx.enter_context(nc.Block())
        w_gate = rows_view(d["w_gate"][0])
        w_br = rows_view(d[f"w_br_{name}"][0])

        def cols(j, base=0):
            return slice(base + P * j, base + P * j + P) if isinstance(j, int) else bass.ds(j * P + base, P)

        @block.sync
        def _(sp):
            sp.dma_start(bias[:], d["b_gate"][0].rearrange("(b k p) -> b p k", p=P, b=3)[index],
                         allow_slow_non_contiguous=True).then_inc(bias_loaded, 16)

            def load(j, b):
                sp.dma_start(w[b][:, 0:KD], w_gate[:, :, cols(j, D * index)]).then_inc(w_loaded[b], 16)
                sp.dma_start(w[b][:, KD:], w_br[:, :, cols(j)]).then_inc(w_loaded[b], 16)

            load(0, 0)
            load(1, 1)
            with sp.Fori(1, KD // 2) as r:
                for b in range(2):
                    sp.wait_ge(br_psum, r * 6 + (3 * b - 3))
                    load(r * 2 + b, b)

        @block.tensor
        def _(pe):
            def column(j, b, rounds, peeled):
                pe.wait_ge(w_loaded[b], rounds)
                for n, (at, width) in enumerate(PIECES):
                    if not peeled:
                        pe.wait_ge(gate_done, j * 3 + (n - 2))
                    for k in range(KD):
                        last = nc.tensor.matmul(gate_ps[n][:, 0:width], w[b][:, k], g.h[:, k, at:at + width],
                                                start=k == 0, stop=k == KD - 1)
                    last.then_inc(gate_psum, 1)
                    if not peeled:
                        pe.wait_ge(gated, j * 3 + (n - 2))
                    for k in range(KB):
                        last = nc.tensor.matmul(br_ps[n][:, 0:width], w[b][:, KD + k], g.branch[:, k, at:at + width],
                                                start=k == 0, stop=k == KB - 1)
                    last.then_inc(br_psum, 1)

            column(0, 0, 32, True)
            column(1, 1, 32, False)
            with pe.Fori(1, KD // 2) as r:
                for b in range(2):
                    column(r * 2 + b, b, r * 32 + 32, False)

        @block.scalar
        def _(act):
            act.wait_ge(bias_loaded, 16)
            for j in range(KD):
                for n, (at, width) in enumerate(PIECES):
                    act.wait_ge(gate_psum, 3 * j + n + 1)
                    if j:
                        act.wait_ge(gated, 3 * j + n - 2)
                    nc.scalar.activation(gate[n][:, 0:width], gate_ps[n][:, 0:width], ACT.Sigmoid,
                                         bias=bias[:, j:j + 1]).then_inc(gate_done, 1)

        @block.vector
        def _(dve):
            for j in range(KD):
                for n, (at, width) in enumerate(PIECES):
                    q = 3 * j + n
                    dve.wait_ge(gate_done, q + 1)
                    dve.wait_ge(br_psum, q + 1)
                    mix = g.mix[:, j, at:at + width]
                    if first:
                        nc.vector.tensor_tensor(mix, gate[n][:, 0:width], br_ps[n][:, 0:width], ALU.mult).then_inc(gated, 1)
                    else:
                        nc.vector.tensor_tensor(gate[n][:, 0:width], gate[n][:, 0:width], br_ps[n][:, 0:width], ALU.mult).then_inc(added, 1)
                        dve.wait_ge(added, q + 1)
                        nc.vector.tensor_tensor(mix, mix, gate[n][:, 0:width], ALU.add).then_inc(gated, 1)


def stage_gla(nc, g, d, out):
    with ExitStack() as ctx:
        def sb(name, shape, dt=F32):
            return ctx.enter_context(nc.sbuf_tensor(name, shape, dt))

        def sem(name):
            return ctx.enter_context(nc.semaphore("gla_" + name))

        NCH = TP // CHUNK
        CHUNKS = SEQ // CHUNK + 1
        w_up = sb("w_alpha_up", [LOWR, 2 * P])
        b_alpha = sb("b_alpha", [P, 2])
        norm_col = sb("gla_norm_col", [P, 1])
        w_aa = sb("w_aa", [P, KD, LOWR])
        branch_space = g.branch[:].rearrange("p k t -> p (k t)")[:, 0:KD * BR]
        w_qk = branch_space.rearrange("p (b k c) -> p b k c", b=4, k=KD)
        w_vg = [sb("w_va", [P, KD, BR]), branch_space.rearrange("p (k c) -> p k c", k=KD)]
        work = sb("gla_work", [P, 4 * TP])
        pre = work[:, 0:2 * TP].rearrange("p (a t) -> p a t", a=2)
        decay = work[:, 2 * TP:4 * TP].rearrange("p (a t) -> p a t", a=2)
        o_rows = work[:].rearrange("p (i c) -> p i c", i=NT)
        expo = sb("gla_expo", [P, 2, TP])
        resets = sb("gla_resets", [P, TP])
        gaps = sb("gla_gaps", [P, 2 * NCH])
        factors = sb("gla_factors", [P, 3, 2, NCH])
        k_rows = sb("gla_k_rows", [P, 2, 2 * P])
        att = sb("gla_att", [P, 2, HEADS, P])
        state = [sb(f"gla_state{b}", [P, 2, DV]) for b in range(2)]
        state_mid = resets[:, 0:4 * DV].rearrange("p (c a v) -> p c a v", c=2, a=2)
        o_sq = sb("gla_o_sq", [P, DV])
        ssq = sb("gla_ssq", [P, NT * HEADS])
        std = sb("gla_std", [P, NT * HEADS])

        in_loaded = [sem(f"in_loaded{b}") for b in range(7)]
        in_psum, in_done = sem("in_psum"), sem("in_done")
        loaded, pads, pre_psum, pre_done, soft, rel_done, exp_done, q_done, k_done, factors_done = (sem(n) for n in (
            "loaded pads pre_psum pre_done soft rel_done exp_done q_done k_done factors_done").split())
        k_turned, k_rows_done, att_psum, att_done, ds_psum, mid_done, scaled, state_done = (sem(n) for n in (
            "k_turned k_rows_done att_psum att_done ds_psum mid_done scaled state_done").split())
        o_psum, o_done, ssq_done, std_done, rstd_done, gated, o_turned, branch_done, stored, step = (sem(n) for n in (
            "o_psum o_done ssq_done std_done rstd_done gated o_turned branch_done stored step").split())
        ps = [ctx.enter_context(nc.psum_tensor(f"gla_ps{b}", [P, 512], F32)) for b in range(8)]
        block = ctx.enter_context(nc.Block())
        q_all, k_all = g.gla_qk[:, 0:2], g.gla_qk[:, 2:4]
        PRE = [(j, n) for j in range(2) for n in range(3)]
        w_in = rows_view(d["w_in"][0])
        COLS = [("t", j, n) for j in range(4) for n in range(3)] + [("a", 0, n) for n in range(3)]
        ROWS = [("v", i, b) for b in range(2) for i in range(NT)]

        def chunked(t):
            return t.rearrange("p a (n c) -> p (a n) c", c=CHUNK)

        def flat(t):
            return t.rearrange("p a t -> p (a t)")

        def chunks_of(i):
            return (0, 1) if i < NT - 1 else (0,)

        def pair_of(bank):
            return bank[:, 0:2 * P].rearrange("p (a v) -> p a v", a=2)

        @block.sync
        def _(sp):
            for b in range(4):
                sp.dma_start(w_qk[:, b], w_in[:, :, P * b:P * b + P]).then_inc(in_loaded[b], 16)
            sp.dma_start(w_aa[:], w_in[:, :, COL["aa"]:COL["aa"] + LOWR]).then_inc(in_loaded[4], 16)
            sp.dma_start(w_vg[0][:], w_in[:, :, COL["va"]:COL["va"] + BR]).then_inc(in_loaded[5], 16)
            sp.dma_start(w_up[:], d["w_alpha_up"][0]).then_inc(loaded, 16)
            sp.dma_start(b_alpha[:], d["b_alpha"][0].rearrange("(k p) -> p k", p=P), allow_slow_non_contiguous=True).then_inc(loaded, 16)
            sp.dma_start(norm_col[:], d["gla_norm_w"][0].rearrange("(p o) -> p o", o=1), allow_slow_non_contiguous=True).then_inc(loaded, 16)
            sp.dma_start(state[1][:], d["state_gla"][0, 0].rearrange("(a h) s v -> (h s) a v", h=2)).then_inc(loaded, 16)
            sp.wait_ge(in_psum, 12)
            sp.dma_start(w_vg[1], w_in[:, :, COL["ga"]:COL["ga"] + BR]).then_inc(in_loaded[6], 16)
            for who, chunks in enumerate((CHUNKS - 1, CHUNKS)):
                sp.wait_ge(state_done, chunks)
                sp.dma_start(out["gla"][who][0, 0].rearrange("(a h) s v -> (h s) a v", h=2), state[who][:]).then_inc(stored, 16)
            sp.wait_ge(stored, 32)

        @block.gpsimd
        def _(pool):
            nc.gpsimd.memset(resets[:], 1.0).then_inc(pads, 1)
            pool.wait_ge(pads, 1)
            nc.gpsimd.memset(g.gla_qk[:, :, TOK:TP], 0.0).then_inc(pads, 1)
            pool.wait_ge(pads, 2)
            nc.gpsimd.memset(resets[:, 0:TP:CHUNK], 0.0).then_inc(pads, 1)
            pool.wait_ge(pads, 3)
            nc.gpsimd.memset(pre[:, :, TOK:TP], 0.0).then_inc(pads, 1)
            pool.wait_ge(pads, 4)
            nc.gpsimd.memset(state[0][:], 0.0).then_inc(pads, 1)

        @block.scalar
        def _(act):
            def unload_in(q):
                kind, j, n = (COLS + ROWS)[q]
                act.wait_ge(in_psum, q + 1)
                if kind == "v":
                    dst, src = (g.gla_v, g.gla_gate)[n][:, j], ps[q % 4][:]
                else:
                    at, width = PIECES[n]
                    dst = g.gla_qk[:, j, at:at + width] if kind == "t" else g.gla_low[0:LOWR, at:at + width]
                    src = ps[q % 4][0:(P if kind == "t" else LOWR), 0:width]
                nc.scalar.activation(dst, src, ACT.Silu if kind == "v" and n else ACT.Copy).then_inc(in_done, 1)

            nc_ = len(COLS)
            for q in range(nc_):
                unload_in(q)
            act.wait_ge(loaded, 64)
            for q, (j, n) in enumerate(PRE):
                at, width = PIECES[n]
                act.wait_ge(pre_psum, q + 1)
                nc.scalar.activation(pre[:, j, at:at + width], ps[4 + q % 4][:, 0:width], ACT.Identity,
                                     bias=b_alpha[:, j:j + 1]).then_inc(pre_done, 1)
            unload_in(nc_)
            act.wait_ge(pre_done, len(PRE))
            act.wait_ge(pads, 5)
            nc.scalar.activation(expo[:], pre, ACT.Abs).then_inc(soft, 1)
            act.wait_ge(soft, 1)
            nc.scalar.activation(expo[:], expo[:], ACT.Exp, scale=-1.0).then_inc(soft, 1)
            act.wait_ge(soft, 2)
            nc.scalar.activation(expo[:], expo[:], ACT.Ln, bias=1.0).then_inc(soft, 1)
            for q in range(nc_ + 1, nc_ + 4):
                unload_in(q)
            act.wait_ge(rel_done, 2)
            nc.scalar.activation(expo[:], pre, ACT.Exp, scale=1.0 / TAU).then_inc(exp_done, 1)
            for f, src in enumerate((chunked(decay)[:, :, 31], chunked(decay)[:, :, 63], gaps[:])):
                nc.scalar.activation(factors[:, f].rearrange("p a n -> p (a n)"), src, ACT.Exp, scale=1.0 / TAU).then_inc(factors_done, 1)
            for q in range(nc_ + 4, nc_ + 6):
                unload_in(q)
            act.wait_ge(q_done, 1)
            nc.scalar.activation(expo[:], pre, ACT.Exp, scale=-1.0 / TAU).then_inc(exp_done, 1)
            for q in range(nc_ + 6, nc_ + len(ROWS)):
                unload_in(q)

            def unload_o(i):
                act.wait_ge(o_psum, i + 1)
                for half in range(2):
                    for a in range(2):
                        h = 2 * a + half
                        if i or half or a:
                            act.wait_ge(ssq_done, HEADS * i + 2 * half + a)
                        nc.scalar.activation(o_sq[:], ps[6 + half][:, DV * a:DV * a + DV], ACT.Square,
                                             accum_out=ssq[:, HEADS * i + h:HEADS * i + h + 1]).then_inc(ssq_done, 1)
                    nc.scalar.activation(o_rows[:, i].rearrange("p (a h v) -> p h a v", a=2, h=2)[:, half], pair_of(ps[6 + half]),
                                         ACT.Copy).then_inc(o_done, 1)

            for i in range(NT):
                act.wait_ge(k_turned, i + 1)
                if i >= 2:
                    act.wait_ge(ds_psum, 2 * (i - 1))
                nc.scalar.activation(k_rows[:, i % 2], ps[i % 2][:, 0:2 * P], ACT.Copy).then_inc(k_rows_done, 1)
                if i:
                    unload_o(i - 1)
            unload_o(NT - 1)
            act.wait_ge(ssq_done, NT * HEADS)
            nc.scalar.activation(std[:], ssq[:], ACT.Sqrt, scale=1.0 / DV, bias=g.eps[:]).then_inc(std_done, 1)
            for i in range(NT):
                n = P if i < NT - 1 else DEC
                act.wait_ge(o_turned, i + 1)
                nc.scalar.activation(g.branch[:, :, P * i:P * i + n], ps[i % 4][:].rearrange("p (h t) -> p h t", h=HEADS)[:, :, 0:n],
                                     ACT.Copy, scale=norm_col[:, 0:1]).then_inc(branch_done, 1)

        @block.vector
        def _(dve):
            dve.wait_ge(soft, 3)
            nc.vector.scalar_tensor_tensor(flat(pre), flat(pre), 0.0, flat(expo[:]), ALU.min, ALU.subtract).then_inc(step, 1)
            dve.wait_ge(step, 1)
            for a in range(2):
                nc.vector.tensor_tensor_scan(decay[:, a], resets[:], pre[:, a], 0.0, ALU.mult, ALU.add).then_inc(step, 1)
            dve.wait_ge(step, 3)
            mid = chunked(decay)[:, :, 31:32]
            nc.vector.tensor_tensor(chunked(pre), chunked(decay), mid.broadcast_to([P, 2 * NCH, CHUNK]), ALU.subtract).then_inc(rel_done, 1)
            nc.vector.tensor_tensor(gaps[:], chunked(decay)[:, :, 63], chunked(decay)[:, :, 31], ALU.subtract).then_inc(rel_done, 1)
            dve.wait_ge(exp_done, 1)
            nc.vector.scalar_tensor_tensor(flat(q_all), flat(q_all), GDK ** -0.5, flat(expo[:]), ALU.mult, ALU.mult).then_inc(q_done, 1)
            dve.wait_ge(exp_done, 2)
            nc.vector.tensor_tensor(flat(k_all), flat(k_all), flat(expo[:]), ALU.mult).then_inc(k_done, 1)
            dve.wait_ge(factors_done, 3)
            for i in range(NT):
                for half in range(2):
                    dve.wait_ge(att_psum, 2 * i + half + 1)
                    if i >= 2 and half == 0:
                        dve.wait_ge(o_psum, i - 1)
                    nc.vector.tensor_tensor(att[:, i % 2, half::2], pair_of(ps[2 + half]), g.upto[:].unsqueeze(1).broadcast_to([P, 2, P]),
                                            ALU.mult).then_inc(att_done, 1)
                for c in chunks_of(i):
                    n = 2 * i + c
                    s = state[0] if i < NT - 1 else state[1]
                    if i:
                        dve.wait_ge(o_psum, i)
                    if n:
                        dve.wait_ge(state_done, n)
                    for a in range(2):
                        last = nc.vector.tensor_scalar(state_mid[:, c, a], s[:, a], factors[:, 0, a, n:n + 1], None, ALU.mult)
                    last.then_inc(mid_done, 1)
                    dve.wait_ge(mid_done, n + 1)
                    for a in range(2):
                        last = nc.vector.tensor_scalar(s[:, a], s[:, a], factors[:, 1, a, n:n + 1], None, ALU.mult)
                    last.then_inc(scaled, 1)
                    dve.wait_ge(scaled, n + 1)
                    dve.wait_ge(ds_psum, n + 1)
                    for a in range(2):
                        last = nc.vector.scalar_tensor_tensor(s[:, a], ps[4 + c][:, DV * a:DV * a + DV], factors[:, 2, a, n:n + 1], s[:, a],
                                                              ALU.mult, ALU.add)
                    last.then_inc(state_done, 1)
            dve.wait_ge(std_done, 1)
            nc.vector.reciprocal(std[:], std[:]).then_inc(rstd_done, 1)
            dve.wait_ge(rstd_done, 1)
            dve.wait_ge(o_done, 2 * NT)
            for i in range(NT):
                for h in range(HEADS):
                    o = o_rows[:, i, DV * h:DV * h + DV]
                    last = nc.vector.scalar_tensor_tensor(o, o, std[:, HEADS * i + h:HEADS * i + h + 1], g.gla_gate[:, i, DV * h:DV * h + DV],
                                                          ALU.mult, ALU.mult)
                last.then_inc(gated, 1)

        @block.tensor
        def _(pe):
            def product(q):
                kind, j, n = (COLS + ROWS)[q]
                if q >= 4:
                    pe.wait_ge(in_done, q - 3)
                pe.wait_ge(in_loaded[{"t": j, "a": 4, "v": 5 + n}[kind]], 16)
                for k in range(KD):
                    if kind == "v":
                        to, lhs, rhs = ps[q % 4][:], g.h[:, k, P * j:P * j + P], w_vg[n][:, k]
                    else:
                        at, width = PIECES[n]
                        rows, lhs = (P, w_qk[:, j, k]) if kind == "t" else (LOWR, w_aa[:, k])
                        to, rhs = ps[q % 4][0:rows, 0:width], g.h[:, k, at:at + width]
                    last = nc.tensor.matmul(to, lhs, rhs, start=k == 0, stop=k == KD - 1)
                last.then_inc(in_psum, 1)

            for q in range(len(COLS) + 1):
                product(q)
            pe.wait_ge(in_done, len(COLS))
            pe.wait_ge(loaded, 64)
            for q, (j, n) in enumerate(PRE):
                at, width = PIECES[n]
                if q >= 4:
                    pe.wait_ge(pre_done, q - 3)
                nc.tensor.matmul(ps[4 + q % 4][:, 0:width], w_up[:, P * j:P * j + P], g.gla_low[:, at:at + width],
                                 start=True, stop=True).then_inc(pre_psum, 1)
            for q in range(len(COLS) + 1, len(COLS) + len(ROWS)):
                product(q)
            pe.wait_ge(in_done, len(COLS) + len(ROWS))
            pe.wait_ge(pre_done, len(PRE))
            pe.wait_ge(q_done, 1)
            pe.wait_ge(k_done, 1)
            for i in range(NT):
                b = i % 2
                tile = slice(P * i, P * i + P)
                if i >= 2:
                    pe.wait_ge(k_rows_done, i - 1)
                for a in range(2):
                    last = nc.tensor.transpose(ps[b][:, P * a:P * a + P], k_all[:, a, tile], g.ident[:])
                last.then_inc(k_turned, 1)
                if i:
                    pe.wait_ge(att_done, 2 * i)
                for half in range(2):
                    rows = slice(GDK * half, GDK * half + GDK)
                    for a in range(2):
                        last = nc.tensor.matmul(ps[2 + half][:, P * a:P * a + P], k_all[rows, a, tile], q_all[rows, a, tile],
                                                start=a == 0, stop=a == 1, skip_group_check=True)
                    last.then_inc(att_psum, 1)
                pe.wait_ge(k_rows_done, i + 1)
                for c in chunks_of(i):
                    if i:
                        pe.wait_ge(state_done, 2 * i + c - 1)
                    tok = slice(CHUNK * c, CHUNK * c + CHUNK)
                    for a in range(2):
                        for half in range(2):
                            h = 2 * a + half
                            last = nc.tensor.matmul(ps[4 + c][GDK * half:GDK * half + GDK, DV * a:DV * a + DV],
                                                    k_rows[tok, b, GDK * h:GDK * h + GDK], g.gla_v[tok, i, DV * h:DV * h + DV],
                                                    start=a == 0, stop=a == 1, skip_group_check=True)
                    last.then_inc(ds_psum, 1)
                pe.wait_ge(att_done, 2 * i + 2)
                if i:
                    pe.wait_ge(o_done, 2 * i)
                for h in range(HEADS):
                    a, half = h // 2, h % 2
                    nc.tensor.matmul(ps[6 + half][:, DV * a:DV * a + DV], att[:, b, h], g.gla_v[:, i, DV * h:DV * h + DV],
                                     start=a == 0, stop=False, skip_group_check=True)
                for c in chunks_of(i):
                    pe.wait_ge(mid_done, 2 * i + c + 1)
                    for h in range(HEADS):
                        a, half = h // 2, h % 2
                        rows = slice(GDK * half, GDK * half + GDK)
                        last = nc.tensor.matmul(ps[6 + half][CHUNK * c:CHUNK * c + CHUNK, DV * a:DV * a + DV],
                                                q_all[rows, a, P * i + CHUNK * c:P * i + CHUNK * c + CHUNK], state_mid[rows, c, a],
                                                start=False, stop=True, skip_group_check=True)
                last.then_inc(o_psum, 1)
            for i in range(NT):
                n = P if i < NT - 1 else DEC
                pe.wait_ge(gated, i + 1)
                if i >= 4:
                    pe.wait_ge(branch_done, i - 3)
                for h in range(HEADS):
                    last = nc.tensor.transpose(ps[i % 4][:, P * h:P * h + n], o_rows[0:n, i, DV * h:DV * h + DV], g.ident[0:n, 0:n])
                last.then_inc(o_turned, 1)


def stage_gdn_in(nc, g, d, out):
    with ExitStack() as ctx:
        def sb(name, shape, dt=F32):
            return ctx.enter_context(nc.sbuf_tensor("cv_" + name, shape, dt))

        def sem(name):
            return ctx.enter_context(nc.semaphore("cv_" + name))

        S0 = SEQ + 2 * (CW - 1)
        RAW = S0 + DEC
        RUN = RAW - (CW - 1)
        w = sb("w", [P, 2, KD, P])
        w_ba = sb("w_ba", [P, KD, 2 * HEADS])
        raw = sb("raw", [P, 2, RAW])
        acc = sb("acc", [P, 2, RUN])
        v_cols = sb("v_cols", [P, 2, TP])
        taps = sb("taps", [P, NCV, CW])
        history = sb("history", [P, NCV, CW - 1])
        tails = sb("tails", [P, NCV, 2, CW - 1])
        ba_cols = sb("ba_cols", [2 * HEADS, TP])
        squares = v_cols
        inv = acc

        loaded, ba_loaded, psum, raw_done, pads, edges, conv, silu_done, v_turned, v_done = (sem(n) for n in (
            "loaded ba_loaded psum raw_done pads edges conv silu_done v_turned v_done").split())
        w_loaded = [sem(f"w_loaded{b}") for b in range(2)]
        ba_psum, ba_out, ba_turned, ba_done, sq_done, sq_psum, root_done, inv_done, unit_done, stored, tails_done = (sem(n) for n in (
            "ba_psum ba_out ba_turned ba_done sq_done sq_psum root_done inv_done unit_done stored tails_done").split())
        ps = [ctx.enter_context(nc.psum_tensor(f"cv_ps{b}", [P, 512], F32)) for b in range(8)]
        block = ctx.enter_context(nc.Block())
        w_in = rows_view(d["w_in"][0])
        V0 = 2 * HEADS

        def root(act, j):
            for n, (at, width) in enumerate(PIECES):
                act.wait_ge(sq_psum, 3 * j + n + 1)
                if j >= 2:
                    act.wait_ge(unit_done, j - 1)
                nc.scalar.activation(inv[:, j % 2, at:at + width], ps[n][:, 0:width], ACT.Sqrt, bias=g.eps[:]).then_inc(root_done, 1)

        def out_v(dve, j):
            for q in range(3):
                dve.wait_ge(v_turned, 3 * (j - V0) + q + 1)
                h = j - V0
                nc.vector.tensor_copy(g.gdn_v[:, 3 * q:3 * q + 3, DV * h:DV * h + DV],
                                      ps[3 + q][:, 0:3 * P].rearrange("p (i v) -> p i v", i=3)).then_inc(v_done, 1)

        @block.sync
        def _(sp):
            for t in range(CW):
                sp.dma_start(taps[:, :, t], d["conv_w"][0, t].rearrange("(k p) -> p k", p=P), allow_slow_non_contiguous=True).then_inc(loaded, 16)
            for t in range(CW - 1):
                sp.dma_start(history[:, :, t], d["cache_gdn_conv"][0, 0, t].rearrange("(k p) -> p k", p=P),
                             allow_slow_non_contiguous=True).then_inc(loaded, 16)
            sp.dma_start(w_ba[:], w_in[:, :, COL["beta"]:COL["beta"] + 2 * HEADS]).then_inc(ba_loaded, 16)
            for j in range(NCV):
                if j >= 2:
                    sp.wait_ge(psum, 3 * (j - 1))
                sp.dma_start(w[:, j % 2], w_in[:, :, COL["qkv"] + P * j:COL["qkv"] + P * j + P]).then_inc(w_loaded[j % 2], 16)
            sp.wait_ge(tails_done, NCV)
            for who in range(2):
                for t in range(CW - 1):
                    sp.dma_start(out["conv"][who][0, 0, t].rearrange("(k p) -> p k", p=P), tails[:, :, who, t],
                                 allow_slow_non_contiguous=True).then_inc(stored, 16)
            sp.wait_ge(stored, 16 * 2 * (CW - 1))

        @block.gpsimd
        def _(pool):
            for n, t in enumerate((v_cols[:, :, TOK:TP], g.gdn_qk[:, :, TOK:TP], ba_cols[:, TOK:TP], raw[:, :, 0:CW - 1])):
                if n:
                    pool.wait_ge(pads, n)
                nc.gpsimd.memset(t, 0.0).then_inc(pads, 1)
            pool.wait_ge(pads, 4)
            pool.wait_ge(loaded, 16 * (2 * CW - 1))
            for j in range(NCV):
                if j >= 2:
                    pool.wait_ge(conv, CW * (j - 1))
                    pool.wait_ge(tails_done, j - 1)
                if j:
                    pool.wait_ge(edges, j)
                nc.gpsimd.tensor_copy(raw[:, j % 2, SEQ + CW - 1:S0], history[:, j]).then_inc(edges, 1)
                pool.wait_ge(raw_done, 4 * (j + 1))
                src = raw[:, j % 2, SEQ:SEQ + CW - 1]
                pool.wait_ge(edges, j + 1)
                nc.gpsimd.tensor_copy(tails[:, j, 0], src)
                nc.gpsimd.tensor_copy(tails[:, j, 1], raw[:, j % 2, RAW - CW + 1:RAW]).then_inc(tails_done, 1)

        @block.tensor
        def _(pe):
            def turn_v(j):
                pe.wait_ge(silu_done, 2 * (j + 1))
                if j == V0:
                    pe.wait_ge(pads, 4)
                for q in range(3):
                    n = 3 * (j - V0) + q
                    if n >= 3:
                        pe.wait_ge(v_done, n - 2)
                    for a in range(3):
                        i = 3 * q + a
                        last = nc.tensor.transpose(ps[3 + q][:, P * a:P * a + P], v_cols[:, j % 2, P * i:P * i + P], g.ident[:])
                    last.then_inc(v_turned, 1)

            for j in range(NCV):
                pe.wait_ge(w_loaded[j % 2], 16 * (j // 2 + 1))
                for n, (at, width) in enumerate(PIECES):
                    if j:
                        pe.wait_ge(raw_done, 4 * (j - 1) + n + (2 if n == 2 else 1))
                    for k in range(KD):
                        last = nc.tensor.matmul(ps[n][:, 0:width], w[:, j % 2, k], g.h[:, k, at:at + width], start=k == 0, stop=k == KD - 1)
                    last.then_inc(psum, 1)
                if j > V0:
                    turn_v(j - 1)
            pe.wait_ge(ba_loaded, 16)
            for n, (at, width) in enumerate(PIECES):
                pe.wait_ge(raw_done, 4 * (NCV - 1) + n + (2 if n == 2 else 1))
                for k in range(KD):
                    last = nc.tensor.matmul(ps[n][0:2 * HEADS, 0:width], w_ba[:, k], g.h[:, k, at:at + width], start=k == 0, stop=k == KD - 1)
                last.then_inc(ba_psum, 1)
            turn_v(NCV - 1)
            pe.wait_ge(ba_out, 3)
            for i in range(NT):
                last = nc.tensor.transpose(ps[7][:, 2 * HEADS * i:2 * HEADS * i + 2 * HEADS], ba_cols[:, P * i:P * i + P],
                                           g.ident[0:2 * HEADS, 0:2 * HEADS])
            last.then_inc(ba_turned, 1)
            for j in range(V0):
                pe.wait_ge(sq_done, j + 1)
                for n, (at, width) in enumerate(PIECES):
                    if j:
                        pe.wait_ge(root_done, 3 * (j - 1) + n + 1)
                    nc.tensor.matmul(ps[n][:, 0:width], g.ones[:], squares[:, j % 2, at:at + width], start=True, stop=True).then_inc(sq_psum, 1)

        @block.scalar
        def _(act):
            def silu(j):
                act.wait_ge(conv, CW * (j + 1))
                dst = g.gdn_qk[:, j] if j < V0 else v_cols[:, j % 2]
                if j >= V0 + 2:
                    act.wait_ge(v_turned, 3 * (j - 1 - V0))
                nc.scalar.activation(dst[:, 0:SEQ], acc[:, j % 2, 0:SEQ], ACT.Silu).then_inc(silu_done, 1)
                nc.scalar.activation(dst[:, SEQ:TOK], acc[:, j % 2, SEQ + CW - 1:RUN], ACT.Silu).then_inc(silu_done, 1)

            for j in range(NCV):
                if j >= 2:
                    act.wait_ge(conv, CW * (j - 1))
                    act.wait_ge(tails_done, j - 1)
                for n, (at, width) in enumerate(PIECES):
                    act.wait_ge(psum, 3 * j + n + 1)
                    end = min(at + width, SEQ)
                    nc.scalar.activation(raw[:, j % 2, CW - 1 + at:CW - 1 + end], ps[n][:, 0:end - at], ACT.Copy).then_inc(raw_done, 1)
                nc.scalar.activation(raw[:, j % 2, S0:RAW], ps[2][:, width - DEC:width], ACT.Copy).then_inc(raw_done, 1)
                if j:
                    silu(j - 1)
            silu(NCV - 1)
            for n, (at, width) in enumerate(PIECES):
                act.wait_ge(ba_psum, n + 1)
                nc.scalar.activation(ba_cols[:, at:at + width], ps[n][0:2 * HEADS, 0:width], ACT.Copy).then_inc(ba_out, 1)
            act.wait_ge(v_turned, 12)
            for j in range(V0):
                if j >= 2:
                    act.wait_ge(sq_psum, 3 * (j - 1))
                nc.scalar.activation(squares[:, j % 2, 0:TOK], g.gdn_qk[:, j, 0:TOK], ACT.Square).then_inc(sq_done, 1)
                if j >= 1:
                    root(act, j - 1)
            root(act, V0 - 1)

        @block.vector
        def _(dve):
            for j in range(NCV):
                dve.wait_ge(raw_done, 4 * (j + 1))
                dve.wait_ge(edges, j + 1)
                dve.wait_ge(pads, 4)
                if j >= 2:
                    dve.wait_ge(silu_done, 2 * (j - 1))
                a = acc[:, j % 2]
                nc.vector.tensor_scalar(a, raw[:, j % 2, 0:RUN], taps[:, j, 0:1], None, ALU.mult).then_inc(conv, 1)
                for t in range(1, CW):
                    dve.wait_ge(conv, CW * j + t)
                    nc.vector.scalar_tensor_tensor(a, raw[:, j % 2, t:t + RUN], taps[:, j, t:t + 1], a, ALU.mult, ALU.add).then_inc(conv, 1)
                if j > V0:
                    out_v(dve, j - 1)
            out_v(dve, NCV - 1)
            dve.wait_ge(ba_turned, 1)
            nc.vector.tensor_copy(g.gdn_ba[:], ps[7][:, 0:NT * 2 * HEADS].rearrange("p (i c) -> p i c", i=NT)).then_inc(ba_done, 1)
            for j in range(V0):
                dve.wait_ge(root_done, 3 * (j + 1))
                r = inv[:, j % 2, 0:TOK]
                nc.vector.reciprocal(r, r).then_inc(inv_done, 1)
                dve.wait_ge(inv_done, j + 1)
                x = g.gdn_qk[:, j, 0:TOK]
                nc.vector.scalar_tensor_tensor(x, x, DV ** -0.5 if j < HEADS else 1.0, r, ALU.mult, ALU.mult).then_inc(unit_done, 1)


def stage_gdn(nc, g, d, out):
    with ExitStack() as ctx:
        def sb(name, shape=(P, HEADS, P)):
            return ctx.enter_context(nc.sbuf_tensor("gd_" + name, list(shape), F32))

        def sem(name):
            return ctx.enter_context(nc.semaphore("gd_" + name))

        NG_ = NT * HEADS
        blocks = sb("blocks", [P, 4, P])
        rate = sb("rate", [P, HEADS])
        dt_bias = sb("dt_bias", [P, HEADS])
        beta = sb("beta", [P, NT, HEADS])
        log_g = sb("log_g", [P, NT, HEADS])
        grow = sb("grow", [P, 4, NT, HEADS])
        beta_grow = sb("beta_grow", [P, NT, HEADS])
        soft = beta_grow
        k_in = sb("k_in")
        k_out = [sb(f"k_out{b}") for b in range(2)]
        v_in = [sb(f"v_in{b}") for b in range(2)]
        att = [sb(f"att{b}") for b in range(2)]
        solve_t = [sb(f"solve_t{b}") for b in range(2)]
        wk = [sb(f"wk{b}") for b in range(2)]
        slot = [sb(f"slot{b}") for b in range(4)]
        steps, power2 = slot[0], slot[0]
        decay_t, power2_t = slot[1], slot[1]
        decay, power4 = slot[2], slot[2]
        a_mat, joint = slot[3], slot[3]
        x = [sb(f"x{b}") for b in range(2)]
        xt = [sb(f"xt{b}") for b in range(2)]
        between = [sb(f"between{b}") for b in range(3)]
        u = sb("u")
        q_state = x[1]
        state = [sb(f"state{b}") for b in range(2)]
        w_gate = sb("w_gate", [P, 2, KD, P])
        JOBS = [(c, t) for c in range(BR // P) for t in range(NT)]
        PER_TILE = len(JOBS) // NT

        names = ("loaded masks rate_done sig_done soft_done step g_done pre_psum grow_done bg_done "
                 "kt_psum k_in k_out v_in steps dec_psum dec_exp dec_mask kk_psum qk_psum a att at_psum dt between d x1 x1t "
                 "p2_psum p2 p4_psum p4 x2_psum x2 x3_psum x3 p16_psum p16 x4_psum x4 p32_psum p32 x5_psum x5 p64_psum p64 x6_psum x6 "
                 "gate_w0 gate_w1 gate_psum gate_out wk_psum wk u_psum qs_psum u_out ds_psum state o_psum qs_out o_out stored state_in").split()
        S = {n: sem(n) for n in names}
        ps = [ctx.enter_context(nc.psum_tensor(f"gd_ps{b}", [P, HEADS, P], F32)) for b in range(8)]
        block = ctx.enter_context(nc.Block())
        q_all, k_all = g.gdn_qk[:, 0:HEADS], g.gdn_qk[:, HEADS:2 * HEADS]

        def heads(mask):
            return mask.unsqueeze(1).broadcast_to([P, HEADS, P])

        def per_head(cols, n=P):
            return cols.unsqueeze(2).broadcast_to([n, HEADS, P])

        def tile(i):
            return slice(P * i, P * i + P)

        def chunks_of(i):
            return (0, 1) if i < NT - 1 else (0,)

        def rows(c):
            return slice(CHUNK * c, CHUNK * c + CHUNK)

        @block.sync
        def _(sp):
            sp.dma_start(rate[:], d["gdn_a_log"].broadcast_to([P, HEADS]), allow_slow_non_contiguous=True).then_inc(S["loaded"], 16)
            sp.dma_start(dt_bias[:], d["gdn_dt_bias"].broadcast_to([P, HEADS]), allow_slow_non_contiguous=True).then_inc(S["loaded"], 16)
            gate_view = rows_view(d["w_in"][0])[:, :, COL["gb"]:COL["gb"] + BR]
            for c in range(BR // P):
                if c >= 2:
                    sp.wait_ge(S["gate_psum"], NT * (c - 1))
                sp.dma_start(w_gate[:, c % 2], gate_view[:, :, P * c:P * c + P]).then_inc(S[f"gate_w{c % 2}"], 16)
            sp.wait_ge(S["state"], 16)
            sp.dma_start(out["gdn"][0][0, 0].rearrange("h k v -> k h v"), state[0][:]).then_inc(S["stored"], 16)
            sp.wait_ge(S["stored"], 16)
            sp.dma_start(state[0][:], d["state_gdn"][0, 0].rearrange("h k v -> k h v")).then_inc(S["state_in"], 16)
            sp.wait_ge(S["state"], 17)
            sp.dma_start(out["gdn"][1][0, 0].rearrange("h k v -> k h v"), state[1][:]).then_inc(S["stored"], 16)
            sp.wait_ge(S["stored"], 32)

        @block.gpsimd
        def _(pool):
            n = 0

            def done(ins):
                nonlocal n
                ins.then_inc(S["masks"], 1)
                n += 1
                pool.wait_ge(S["masks"], n)

            done(nc.gpsimd.memset(blocks[:], 1.0))
            for m in range(4):
                size = 8 << m
                view = blocks[:, m].rearrange("p (a b) -> p a b", b=size)
                for base, step, cm in ((0, -size, 1), (size - 1, size, -1)):
                    done(nc.gpsimd.affine_select(out=view, in_=view, compare_op=ALU.is_ge, fill=0.0, base=base,
                                                 pattern=[[step, P // size], [0, size]], channel_multiplier=cm))
            for m in (3, 2, 1):
                done(nc.gpsimd.tensor_tensor(blocks[:, m], blocks[:, m], blocks[:, m - 1], ALU.subtract))
            done(nc.gpsimd.memset(state[0][:], 0.0))
            pool.wait_ge(S["g_done"], 1)
            for i in range(NT):
                b = i % 2
                if i >= 2:
                    pool.wait_ge(S["u_psum"], 2 * (i - 1))
                nc.gpsimd.tensor_tensor(v_in[b][:], g.gdn_v[:, i].rearrange("p (h v) -> p h v", h=HEADS), per_head(beta[:, i]),
                                        ALU.mult).then_inc(S["v_in"], 1)
                if i:
                    pool.wait_ge(S["x3_psum"], 2 * i)
                nc.gpsimd.tensor_tensor(steps[:], heads(g.after[:]), per_head(log_g[:, i]), ALU.mult).then_inc(S["steps"], 1)
                pool.wait_ge(S["dec_exp"], 2 * i + 1)
                nc.gpsimd.tensor_tensor(decay_t[:], decay_t[:], heads(g.upto[:]), ALU.mult).then_inc(S["dec_mask"], 1)
                pool.wait_ge(S["dec_exp"], 2 * i + 2)
                nc.gpsimd.tensor_tensor(decay[:], decay[:], heads(g.after[:]), ALU.mult).then_inc(S["dec_mask"], 1)
                pool.wait_ge(S["a"], i + 1)
                nc.gpsimd.tensor_tensor(x[1][:], a_mat[:], heads(blocks[:, 0]), ALU.mult).then_inc(S["d"], 1)
                pool.wait_ge(S["d"], i + 1)
                nc.gpsimd.tensor_tensor(x[0][:], heads(g.ident[:]), x[1][:], ALU.subtract).then_inc(S["x1"], 1)

        @block.scalar
        def _(act):
            act.wait_ge(S["loaded"], 32)
            nc.scalar.activation(rate[:], rate[:], ACT.Exp).then_inc(S["rate_done"], 1)
            nc.scalar.activation(beta[:], g.gdn_ba[:, :, 0:HEADS], ACT.Sigmoid).then_inc(S["sig_done"], 1)
            act.wait_ge(S["step"], 1)
            nc.scalar.activation(soft[:], log_g[:], ACT.Abs).then_inc(S["soft_done"], 1)
            act.wait_ge(S["soft_done"], 1)
            nc.scalar.activation(soft[:], soft[:], ACT.Exp, scale=-1.0).then_inc(S["soft_done"], 1)
            act.wait_ge(S["soft_done"], 2)
            nc.scalar.activation(soft[:], soft[:], ACT.Ln, bias=1.0).then_inc(S["soft_done"], 1)
            act.wait_ge(S["pre_psum"], 1)
            nc.scalar.activation(grow[:].rearrange("p a i h -> p (a i h)"), ps[0][:].rearrange("p h t -> p (h t)")[:, 0:4 * NG_],
                                 ACT.Exp).then_inc(S["grow_done"], 1)
            for i in range(NT):
                b = i % 2
                act.wait_ge(S["dec_psum"], 2 * i + 1)
                if i:
                    act.wait_ge(S["x2_psum"], 2 * i)
                nc.scalar.activation(decay_t[:], ps[1][:], ACT.Exp).then_inc(S["dec_exp"], 1)
                act.wait_ge(S["dec_psum"], 2 * i + 2)
                if i:
                    act.wait_ge(S["x3_psum"], 2 * i)
                nc.scalar.activation(decay[:], ps[2][:], ACT.Exp).then_inc(S["dec_exp"], 1)
                for r, (to, bank) in enumerate(((power2, 2), (power2_t, 3))):
                    act.wait_ge(S["p2_psum"], 2 * i + r + 1)
                    nc.scalar.activation(to[:], ps[bank][:], ACT.Copy).then_inc(S["p2"], 1)
                act.wait_ge(S["p4_psum"], i + 1)
                nc.scalar.activation(power4[:], ps[0][:], ACT.Copy).then_inc(S["p4"], 1)
                act.wait_ge(S["gate_psum"], PER_TILE * (i + 1))
                for q in range(PER_TILE):
                    c, t = JOBS[PER_TILE * i + q]
                    last = nc.scalar.activation(g.gate_rows(t)[:, P * c:P * c + P], ps[7][:, q], ACT.Copy)
                last.then_inc(S["gate_out"], 1)
                for name, bank in (("p16", 1), ("p32", 0), ("p64", 3)):
                    act.wait_ge(S[name + "_psum"], i + 1)
                    nc.scalar.activation(joint[:], ps[bank][:], ACT.Copy).then_inc(S[name], 1)
                act.wait_ge(S["wk_psum"], i + 1)
                nc.scalar.activation(wk[b][:], ps[1][:], ACT.Copy, scale=-1.0).then_inc(S["wk"], 1)

        @block.vector
        def _(dve):
            dve.wait_ge(S["loaded"], 32)
            nc.vector.tensor_tensor(log_g[:], g.gdn_ba[:, :, HEADS:], dt_bias[:].unsqueeze(1).broadcast_to([P, NT, HEADS]),
                                    ALU.add).then_inc(S["step"], 1)
            dve.wait_ge(S["soft_done"], 3)
            nc.vector.scalar_tensor_tensor(log_g[:], log_g[:], 0.0, soft[:], ALU.max, ALU.add).then_inc(S["step"], 1)
            dve.wait_ge(S["step"], 2)
            dve.wait_ge(S["rate_done"], 1)
            nc.vector.scalar_tensor_tensor(log_g[:], log_g[:], -1.0, rate[:].unsqueeze(1).broadcast_to([P, NT, HEADS]),
                                           ALU.mult, ALU.mult).then_inc(S["g_done"], 1)
            dve.wait_ge(S["grow_done"], 1)
            dve.wait_ge(S["sig_done"], 1)
            nc.vector.tensor_tensor(beta_grow[:], beta[:], grow[:, 0], ALU.mult).then_inc(S["bg_done"], 1)
            dve.wait_ge(S["bg_done"], 1)
            dve.wait_ge(S["masks"], 13)

            def prepare(i):
                b = i % 2
                dve.wait_ge(S["kt_psum"], i + 1)
                if i:
                    dve.wait_ge(S["wk_psum"], i)
                nc.vector.tensor_tensor(k_in[:], ps[0][:], per_head(beta_grow[:, i]), ALU.mult).then_inc(S["k_in"], 1)
                nc.vector.tensor_tensor(k_out[b][:], ps[0][:], per_head(grow[:, 1, i]), ALU.mult).then_inc(S["k_out"], 1)
                dve.wait_ge(S["kk_psum"], i + 1)
                dve.wait_ge(S["dec_mask"], 2 * i + 2)
                for h in range(HEADS):
                    last = nc.vector.scalar_tensor_tensor(a_mat[:, h], ps[3][:, h], beta[:, i, h:h + 1], decay[:, h], ALU.mult, ALU.mult)
                last.then_inc(S["a"], 1)
                dve.wait_ge(S["qk_psum"], i + 1)
                nc.vector.tensor_tensor(att[b][:], ps[0][:], decay_t[:], ALU.mult).then_inc(S["att"], 1)
                solved(i - 1, 0)
                dve.wait_ge(S["at_psum"], i + 1)
                nc.vector.tensor_tensor(xt[1][:], ps[1][:], heads(blocks[:, 0]), ALU.mult).then_inc(S["dt"], 1)
                dve.wait_ge(S["dt"], i + 1)
                nc.vector.tensor_tensor(xt[0][:], heads(g.ident[:]), xt[1][:], ALU.subtract).then_inc(S["x1t"], 1)
                for m in range(3):
                    nc.vector.tensor_tensor(between[m][:], ps[1][:], heads(blocks[:, m + 1]), ALU.mult).then_inc(S["between"], 1)

                def join(name, banks, op, src, dst):
                    for r, (bank, old, new) in enumerate(zip(banks, src, dst)):
                        dve.wait_ge(S[name + "_psum"], 2 * i + r + 1)
                        nc.vector.tensor_tensor(new[:], old[:], ps[bank][:], op).then_inc(S[name], 1)

                dve.wait_ge(S["x1"], i + 1)
                dve.wait_ge(S["x1t"], i + 1)
                advance(i - 1, 0)
                join("x2", (1, 2), ALU.add, (x[0], xt[0]), (x[1], xt[1]))
                dve.wait_ge(S["x2"], 2 * i + 2)
                join("x3", (3, 0), ALU.add, (x[1], xt[1]), (x[0], xt[0]))
                solved(i - 1, 1)
                dve.wait_ge(S["x3"], 2 * i + 2)
                join("x4", (2, 3), ALU.subtract, (x[0], xt[0]), (x[1], xt[1]))
                advance(i - 1, 1)
                dve.wait_ge(S["x4"], 2 * i + 2)
                join("x5", (1, 2), ALU.subtract, (x[1], xt[1]), (x[0], xt[0]))
                dve.wait_ge(S["x5"], 2 * i + 2)
                finish(i - 1)
                dve.wait_ge(S["x6_psum"], i + 1)
                nc.vector.tensor_tensor(solve_t[b][:], xt[0][:], ps[0][:], ALU.subtract).then_inc(S["x6"], 1)

            def solved(i, c):
                if i < 0 or c not in chunks_of(i):
                    return
                dve.wait_ge(S["u_psum"], 2 * i + c + 1)
                if c == 0 and i:
                    dve.wait_ge(S["o_psum"], i)
                nc.vector.tensor_copy(u[rows(c)], ps[4][rows(c)]).then_inc(S["u_out"], 1)

            def advance(i, c):
                if i < 0 or c not in chunks_of(i):
                    return
                n = 2 * i + c
                dve.wait_ge(S["ds_psum"], n + 1)
                old, new = state[n % 2], state[(n + 1) % 2]
                if n:
                    dve.wait_ge(S["state"], n)
                    dve.wait_ge(S["qs_psum"], n)
                if n == 16:
                    dve.wait_ge(S["state_in"], 16)
                for h in range(HEADS):
                    last = nc.vector.scalar_tensor_tensor(new[:, h], old[:, h], grow[:, 2 + c, i, h:h + 1], ps[6 + c][:, h],
                                                          ALU.mult, ALU.add)
                last.then_inc(S["state"], 1)

            def finish(i):
                if i < 0:
                    return
                nc_rows = slice(0, P) if i < NT - 1 else rows(0)
                m = P if i < NT - 1 else CHUNK
                dve.wait_ge(S["qs_psum"], 2 * i + len(chunks_of(i)))
                if i:
                    dve.wait_ge(S["o_out"], i)
                nc.vector.tensor_tensor(q_state[nc_rows], ps[5][nc_rows], per_head(grow[nc_rows, 0, i], m), ALU.mult).then_inc(S["qs_out"], 1)
                dve.wait_ge(S["qs_out"], i + 1)
                dve.wait_ge(S["o_psum"], i + 1)
                dve.wait_ge(S["v_in"], i + 1)
                nc.vector.tensor_tensor(g.gdn_v[nc_rows, i].rearrange("p (h v) -> p h v", h=HEADS), q_state[nc_rows], ps[6][nc_rows],
                                        ALU.add).then_inc(S["o_out"], 1)

            for i in range(NT):
                prepare(i)
            solved(NT - 1, 0)
            advance(NT - 1, 0)
            finish(NT - 1)

        @block.tensor
        def _(pe):
            def product(bank, lhs, rhs, done, rowsl=slice(0, P), start=True):
                for h in range(HEADS):
                    last = nc.tensor.matmul(ps[bank][rowsl, h], lhs(h), rhs(h), start=start and h == 0, stop=h == HEADS - 1,
                                            skip_group_check=True)
                if done:
                    last.then_inc(S[done], 1)

            def of(t):
                return lambda h: t[:, h]

            def gate(i, q):
                if i == NT:
                    return
                c, t = JOBS[PER_TILE * i + q]
                pe.wait_ge(S[f"gate_w{c % 2}"], 16 * (c // 2 + 1))
                if i >= 2 and q == 0:
                    pe.wait_ge(S["state"], 2 * (i - 1))
                for k in range(KD):
                    last = nc.tensor.matmul(ps[7][:, q], g.h[:, k, P * t:P * t + P], w_gate[:, c % 2, k], start=q == 0 and k == 0,
                                            stop=q == PER_TILE - 1 and k == KD - 1, skip_group_check=True)
                last.then_inc(S["gate_psum"], 1)

            pe.wait_ge(S["g_done"], 1)
            flat_g = log_g[:].rearrange("p i h -> p (i h)")
            for q, m in enumerate((g.upto[:], g.after[:], g.row_sel[:, 0:P], g.row_sel[:, P:2 * P])):
                last = nc.tensor.matmul(ps[0][:].rearrange("p h t -> p (h t)")[:, NG_ * q:NG_ * q + NG_], m, flat_g,
                                        start=q == 0, stop=q == 3, skip_group_check=True)
            last.then_inc(S["pre_psum"], 1)
            pe.wait_ge(S["grow_done"], 1)

            def prepare(i):
                b = i % 2
                k, q = (lambda h: k_all[:, h, tile(i)]), (lambda h: q_all[:, h, tile(i)])
                if i:
                    pe.wait_ge(S["x6"], i)
                for h in range(HEADS):
                    last = nc.tensor.transpose(ps[0][:, h], k(h), g.ident[:])
                last.then_inc(S["kt_psum"], 1)
                pe.wait_ge(S["steps"], i + 1)
                if i:
                    pe.wait_ge(S["wk"], i)
                product(1, of(steps), lambda h: g.upto[:], "dec_psum")
                nc.tensor.matmul(ps[2][:].rearrange("p h t -> p (h t)"), g.upto[:], steps[:].rearrange("p h t -> p (h t)"),
                                 start=True, stop=True).then_inc(S["dec_psum"], 1)
                product(3, k, k, "kk_psum")
                if i == 0:
                    gate(0, 0)
                    gate(0, 1)
                pe.wait_ge(S["k_out"], i + 1)
                product(0, k, q, "qk_psum")
                solve(i - 1, 0)
                pe.wait_ge(S["a"], i + 1)
                pe.wait_ge(S["dec_exp"], 2 * i + 1)
                for h in range(HEADS):
                    last = nc.tensor.transpose(ps[1][:, h], a_mat[:, h], g.ident[:])
                last.then_inc(S["at_psum"], 1)
                gate(i, 2)
                pe.wait_ge(S["dt"], i + 1)
                pe.wait_ge(S["d"], i + 1)
                product(2, of(xt[1]), of(x[1]), "p2_psum")
                product(3, of(x[1]), of(xt[1]), "p2_psum")
                add_keys(i - 1, 0)
                pe.wait_ge(S["p2"], 2 * i + 2)
                pe.wait_ge(S["att"], i + 1)
                product(0, of(power2_t), of(power2), "p4_psum")
                pe.wait_ge(S["x1"], i + 1)
                pe.wait_ge(S["x1t"], i + 1)
                pe.wait_ge(S["between"], 3 * i + 3)
                product(1, of(xt[0]), of(power2), "x2_psum")
                product(2, of(power2), of(xt[0]), "x2_psum")
                gate(i, 3)
                pe.wait_ge(S["p4"], i + 1)
                pe.wait_ge(S["x2"], 2 * i + 2)
                product(3, of(xt[1]), of(power4), "x3_psum")
                product(0, of(power4), of(xt[1]), "x3_psum")
                solve(i - 1, 1)
                pe.wait_ge(S["x3"], 2 * i + 2)
                product(1, of(between[0]), of(x[0]), "p16_psum")
                pe.wait_ge(S["p16"], i + 1)
                product(2, of(xt[0]), of(joint), "x4_psum")
                product(3, of(joint), of(xt[0]), "x4_psum")
                add_keys(i - 1, 1)
                pe.wait_ge(S["x4"], 2 * i + 2)
                product(0, of(between[1]), of(x[1]), "p32_psum")
                pe.wait_ge(S["p32"], i + 1)
                product(1, of(xt[1]), of(joint), "x5_psum")
                product(2, of(joint), of(xt[1]), "x5_psum")
                attend(i - 1)
                pe.wait_ge(S["x5"], 2 * i + 2)
                product(3, of(between[2]), of(x[0]), "p64_psum")
                gate(i + 1, 0)
                pe.wait_ge(S["p64"], i + 1)
                product(0, of(joint), of(xt[0]), "x6_psum")
                gate(i + 1, 1)
                pe.wait_ge(S["x6"], i + 1)
                product(1, of(k_in), of(solve_t[b]), "wk_psum")

            def solve(i, c):
                if i < 0 or c not in chunks_of(i):
                    return
                b = i % 2
                n = 2 * i + c
                s = state[n % 2]
                if c == 0:
                    pe.wait_ge(S["v_in"], i + 1)
                    if i:
                        pe.wait_ge(S["u_out"], 2 * i)
                    product(4, of(solve_t[b]), of(v_in[b]), None)
                    pe.wait_ge(S["wk"], i + 1)
                if n:
                    pe.wait_ge(S["state"], n)
                if n == 0:
                    pe.wait_ge(S["masks"], 13)
                if n == 16:
                    pe.wait_ge(S["state_in"], 16)
                product(4, lambda h: wk[b][:, h, rows(c)], of(s), "u_psum", rows(c), start=False)
                if i:
                    pe.wait_ge(S["qs_out"], i)
                product(5, lambda h: q_all[:, h, P * i + CHUNK * c:P * i + CHUNK * c + CHUNK], of(s), "qs_psum", rows(c))

            def add_keys(i, c):
                if i < 0 or c not in chunks_of(i):
                    return
                pe.wait_ge(S["u_out"], 2 * i + c + 1)
                if c == 0 and i:
                    pe.wait_ge(S["o_out"], i)
                if c == 1:
                    pe.wait_ge(S["gate_out"], i + 2)
                product(6 + c, lambda h: k_out[i % 2][rows(c), h], lambda h: u[rows(c), h], "ds_psum")

            def attend(i):
                if i < 0:
                    return
                b = i % 2
                pe.wait_ge(S["state"], 2 * i + 1)
                if i < NT - 1:
                    product(6, of(att[b]), of(u), "o_psum")
                else:
                    product(6, lambda h: att[b][rows(0), h, rows(0)], lambda h: u[rows(0), h], "o_psum", rows(0))

            for i in range(NT):
                prepare(i)
            solve(NT - 1, 0)
            add_keys(NT - 1, 0)
            attend(NT - 1)


def stage_gdn_out(nc, g, d):
    with ExitStack() as ctx:
        def sb(name, shape):
            return ctx.enter_context(nc.sbuf_tensor("go_" + name, shape, F32))

        def sem(name):
            return ctx.enter_context(nc.semaphore("go_" + name))

        gate = sb("gate", [P, NT, BR])
        square = sb("square", [P, DV])
        ssq = sb("ssq", [P, NT * HEADS])
        std = sb("std", [P, NT * HEADS])
        norm_col = sb("norm_col", [P, 1])
        loaded, gate_done, ssq_done, std_done, rstd_done, gated, turned, done, pads = (sem(n) for n in (
            "loaded gate_done ssq_done std_done rstd_done gated turned done pads").split())
        ps = [ctx.enter_context(nc.psum_tensor(f"go_ps{b}", [P, 512], F32)) for b in range(8)]
        block = ctx.enter_context(nc.Block())

        @block.sync
        def _(sp):
            sp.dma_start(norm_col[:], d["gdn_norm_w"][0].rearrange("(p o) -> p o", o=1), allow_slow_non_contiguous=True).then_inc(loaded, 16)

        @block.tensor
        def _(pe):
            for i in range(NT):
                n = P if i < NT - 1 else DEC
                pe.wait_ge(gated, i + 1)
                if i == 0:
                    pe.wait_ge(gate_done, NT)
                if i >= 4:
                    pe.wait_ge(done, i - 3)
                for h in range(HEADS):
                    last = nc.tensor.transpose(ps[4 + i % 4][:, P * h:P * h + n], g.gdn_v[0:n, i, DV * h:DV * h + DV], g.ident[0:n, 0:n])
                last.then_inc(turned, 1)

        @block.scalar
        def _(act):
            for i in range(NT):
                nc.scalar.activation(gate[:, i], g.gate_rows(i), ACT.Silu).then_inc(gate_done, 1)
            for i in range(NT):
                n = P if i < NT - 1 else DEC
                for h in range(HEADS):
                    q = HEADS * i + h
                    if q:
                        act.wait_ge(ssq_done, q)
                    nc.scalar.activation(square[0:n], g.gdn_v[0:n, i, DV * h:DV * h + DV], ACT.Square,
                                         accum_out=ssq[0:n, q:q + 1]).then_inc(ssq_done, 1)
            act.wait_ge(ssq_done, NT * HEADS)
            act.wait_ge(pads, 1)
            nc.scalar.activation(std[:], ssq[:], ACT.Sqrt, scale=1.0 / DV, bias=g.eps[:]).then_inc(std_done, 1)
            act.wait_ge(loaded, 16)
            for i in range(NT):
                n = P if i < NT - 1 else DEC
                act.wait_ge(turned, i + 1)
                nc.scalar.activation(g.branch[:, :, P * i:P * i + n], ps[4 + i % 4][:].rearrange("p (h t) -> p h t", h=HEADS)[:, :, 0:n],
                                     ACT.Copy, scale=norm_col[:, 0:1]).then_inc(done, 1)

        @block.vector
        def _(dve):
            nc.vector.memset(ssq[DEC:P, HEADS * (NT - 1):], 1.0).then_inc(pads, 1)
            dve.wait_ge(std_done, 1)
            nc.vector.reciprocal(std[:], std[:]).then_inc(rstd_done, 1)
            dve.wait_ge(rstd_done, 1)
            for i in range(NT):
                n = P if i < NT - 1 else DEC
                dve.wait_ge(gate_done, i + 1)
                for h in range(HEADS):
                    o = g.gdn_v[0:n, i, DV * h:DV * h + DV]
                    last = nc.vector.scalar_tensor_tensor(o, o, std[0:n, HEADS * i + h:HEADS * i + h + 1], gate[0:n, i, DV * h:DV * h + DV],
                                                          ALU.mult, ALU.mult)
                last.then_inc(gated, 1)


XS = MT * P
NL = NG + NE


def tiles_of(t):
    return t[:].rearrange("p k t -> p (k t)").rearrange("p (i c) -> p i c", i=NT)


def stage_project(nc, g, d):
    with ExitStack() as ctx:
        def sb(name, shape):
            return ctx.enter_context(nc.sbuf_tensor("pj_" + name, shape, F32))

        def sem(name):
            return (g.kept if name in SOFTWARE_DMA else ctx).enter_context(nc.semaphore("pj_" + name))

        w = sb("w_out", [P, KD, D])
        rows = sb("rows", [P, 3, 2, D])
        norm_row = sb("norm_row", [P, D])
        w_route = sb("w_route", [P, KD, NL])
        b_route = sb("b_route", [NL, 1])
        h2 = sb("h2", [P, 3, D])
        h2t = sb("h2t", [P, 2, KD, P])
        branch_sum = sb("branch_sum", [P, 2, D])
        square = sb("square", [P, D])
        ssq = sb("ssq", [P, NT])
        std = sb("std", [P, NT])
        rstd = sb("rstd", [P, NT])
        logits = sb("logits", [NL, 2, P])
        S = {n: sem(n) for n in ("w_loaded x_loaded rows_loaded route_loaded pads scale added ssq std rstd scaled h2 stored0 stored1 stored2 "
                                 "proj_psum gated turned h2t logit_psum logit_out logit_turned").split()}
        stored = [S["stored0"], S["stored1"], S["stored2"]]
        ps = [ctx.enter_context(nc.psum_tensor(f"pj_ps{b}", [P, 512], F32)) for b in range(8)]
        block = ctx.enter_context(nc.Block())
        x1 = tiles_of(g.h)

        @block.sync
        def _(sp):
            for q in range(2):
                sp.dma_start(w[:, 4 * q:4 * q + 4], rows_view(d["w_out"][0])[:, 4 * q:4 * q + 4]).then_inc(S["w_loaded"], 16)
            sp.dma_start(x1[:, 0:8, :], d["x_prompt"][0].rearrange("(i p) c -> p i c", p=P)).then_inc(S["x_loaded"], 16)
            sp.dma_start(x1[0:64, 8, :], d["x_sample"][0]).then_inc(S["x_loaded"], 16)
            for i in range(NT):
                n = P if i < NT - 1 else DEC
                sp.wait_ge(S["h2"], i + 1)
                sp.dma_start(g.h2_dram[P * i:P * i + n, :], h2[0:n, i % 3]).then_inc(stored[i % 3], 16)
            for s in stored:
                sp.wait_ge(s, 48)

        @block.gpsimd
        def _(pool):
            for j, chunk in enumerate((2, 4, 3)):
                for who in range(2):
                    pool.dma_start(rows[:, j, who], g.mod_dram[who:who + 1, D * chunk:D * chunk + D].broadcast_to([P, D])).then_inc(S["rows_loaded"], 16)
            pool.dma_start(norm_row[:], d["norm2_w"].broadcast_to([P, D])).then_inc(S["rows_loaded"], 16)
            pool.dma_start(w_route[:, :, 0:NG], rows_view(d["w_route_group"][0])).then_inc(S["route_loaded"], 16)
            pool.dma_start(w_route[:, :, NG:], rows_view(d["w_route_expert"][0])).then_inc(S["route_loaded"], 16)
            pool.dma_start(b_route[0:NG], d["b_route_group"][0].rearrange("(e o) -> e o", o=1)).then_inc(S["route_loaded"], 16)
            pool.dma_start(b_route[NG:], d["b_route_expert"][0].rearrange("(e o) -> e o", o=1)).then_inc(S["route_loaded"], 16)

        @block.tensor
        def _(pe):
            def project(i):
                n = P if i < NT - 1 else DEC
                for c in range(2):
                    for k in range(KD):
                        last = nc.tensor.matmul(ps[2 * (i % 2) + c][0:n], g.mix[:, k, P * i:P * i + n], w[:, k, 512 * c:512 * c + 512],
                                                start=k == 0, stop=k == KD - 1)
                    last.then_inc(S["proj_psum"], 1)

            pe.wait_ge(S["w_loaded"], 32)
            project(0)
            project(1)
            pe.wait_ge(S["route_loaded"], 64)
            for i in range(NT):
                pe.wait_ge(S["h2"], i + 1)
                if i:
                    pe.wait_ge(S["h2t"], 2 * i)
                for k in range(KD):
                    last = nc.tensor.transpose(ps[4 + k // 4][:, P * (k % 4):P * (k % 4) + P], h2[:, i % 3, P * k:P * k + P], g.ident[:])
                last.then_inc(S["turned"], 1)
                if i + 2 < NT:
                    project(i + 2)
                pe.wait_ge(S["h2t"], 2 * i + 2)
                if i:
                    pe.wait_ge(S["logit_out"], i)
                for k in range(KD):
                    last = nc.tensor.matmul(ps[6][0:NL, 0:P], w_route[:, k], h2t[:, i % 2, k], start=k == 0, stop=k == KD - 1)
                last.then_inc(S["logit_psum"], 1)
                if i:
                    nc.tensor.transpose(ps[7][:, NL * (i - 1):NL * i], logits[:, (i - 1) % 2], g.ident[0:NL, 0:NL])
            pe.wait_ge(S["logit_out"], NT)
            nc.tensor.transpose(ps[7][:, NL * (NT - 1):NL * NT], logits[:, (NT - 1) % 2], g.ident[0:NL, 0:NL]).then_inc(S["logit_turned"], 1)

        @block.vector
        def _(dve):
            nc.vector.memset(x1[64:128, 8, :], 0.0).then_inc(S["pads"], 1)
            dve.wait_ge(S["rows_loaded"], 112)
            for who in range(2):
                nc.vector.scalar_tensor_tensor(rows[:, 1, who], rows[:, 1, who], 1.0, norm_row[:], ALU.add, ALU.mult).then_inc(S["scale"], 1)
            dve.wait_ge(S["x_loaded"], 32)
            dve.wait_ge(S["pads"], 1)

            def logit(i):
                dve.wait_ge(S["logit_psum"], i + 1)
                nc.vector.tensor_scalar(logits[:, i % 2], ps[6][0:NL, 0:P], b_route[:, 0:1], None, ALU.add).then_inc(S["logit_out"], 1)

            dve.wait_ge(S["route_loaded"], 64)

            def add_branches(i):
                n, who = (P, 0) if i < NT - 1 else (DEC, 1)
                for c in range(2):
                    half = slice(512 * c, 512 * c + 512)
                    dve.wait_ge(S["proj_psum"], 2 * i + c + 1)
                    nc.vector.tensor_tensor(branch_sum[0:n, i % 2, half], ps[2 * (i % 2) + c][0:n], rows[0:n, 0, who, half], ALU.mult).then_inc(S["gated"], 1)
                dve.wait_ge(S["gated"], 2 * i + 2)
                nc.vector.tensor_tensor(x1[0:n, i], x1[0:n, i], branch_sum[0:n, i % 2], ALU.add).then_inc(S["added"], 1)

            add_branches(0)
            for i in range(NT):
                who = 0 if i < NT - 1 else 1
                dve.wait_ge(S["std"], i + 1)
                nc.vector.reciprocal(rstd[:, i:i + 1], std[:, i:i + 1]).then_inc(S["rstd"], 1)
                dve.wait_ge(S["rstd"], i + 1)
                dve.wait_ge(S["scale"], 2)
                if i >= 3:
                    dve.wait_ge(stored[i % 3], 16 * (i // 3))
                    dve.wait_ge(S["turned"], i - 2)
                nc.vector.scalar_tensor_tensor(h2[:, i % 3], x1[:, i], rstd[:, i:i + 1], rows[:, 1, who], ALU.mult, ALU.mult).then_inc(S["scaled"], 1)
                dve.wait_ge(S["scaled"], i + 1)
                nc.vector.tensor_tensor(h2[:, i % 3], h2[:, i % 3], rows[:, 2, who], ALU.add).then_inc(S["h2"], 1)
                if i >= 1:
                    logit(i - 1)
                if i + 1 < NT:
                    add_branches(i + 1)
            logit(NT - 1)
            dve.wait_ge(S["logit_turned"], 1)
            nc.vector.tensor_copy(g.logits[:].rearrange("p i e -> p (i e)"), ps[7][:, 0:NT * NL])

        @block.scalar
        def _(act):
            def unload(i):
                for c in range(2):
                    act.wait_ge(S["turned"], i + 1)
                    if i >= 2:
                        act.wait_ge(S["logit_psum"], i - 1)
                    nc.scalar.activation(h2t[:, i % 2, 4 * c:4 * c + 4], ps[4 + c][:].rearrange("p (k t) -> p k t", k=4), ACT.Copy).then_inc(S["h2t"], 1)

            for i in range(NT):
                act.wait_ge(S["added"], i + 1)
                nc.scalar.activation(square[:], x1[:, i], ACT.Square, accum_out=ssq[:, i:i + 1]).then_inc(S["ssq"], 1)
                act.wait_ge(S["ssq"], i + 1)
                nc.scalar.activation(std[:, i:i + 1], ssq[:, i:i + 1], ACT.Sqrt, scale=1.0 / D, bias=g.eps[:]).then_inc(S["std"], 1)
                if i:
                    unload(i - 1)
            unload(NT - 1)


LOGIT_STEP, BOTH_STEP, RATIO_STEP, SLOT_STEP = 5, 24, 25, 58


def stage_route(nc, g, d):
    with ExitStack() as ctx:
        def sb(name, shape, dt=F32):
            return ctx.enter_context(nc.sbuf_tensor("rt_" + name, shape, dt))

        def sem(name):
            return (g.kept if name in SOFTWARE_DMA else ctx).enter_context(nc.semaphore("rt_" + name))

        before = sb("before", [P, P])
        token = sb("token", [P, NT])
        token_i = sb("token_i", [P, NT], I32)
        no_tokens = sb("no_tokens", [MT, P])
        count = sb("count", [P, MT])
        rank = sb("rank", [P, NE])
        g_max = sb("g_max", [P, NT])
        g_exp = sb("g_exp", [P, NT, NG])
        p_group = sb("p_group", [P, NT])
        g_hot = sb("g_hot", [P, NT, NG])
        inside = sb("inside", [P, NT, NE])
        cand = sb("cand", [P, NT, NE])
        best = sb("best", [P, NT])
        top = sb("top", [P, 2, NT])
        hot = sb("hot", [P, 2, NT, NE])
        both = sb("both", [P, NT, NE])
        ratio = sb("ratio", [P, NT])
        slot = sb("slot", [P, NT, NE])
        total = sb("total", [P, NT + 1, NE])
        tiles = sb("tiles", [P, 2, NE])
        ends = sb("ends", [P, NE])
        slot_f = sb("slot_f", [P, 2, NT])
        passed = sb("passed", [P, MT, NE])
        owner = sb("owner", [P, MT])
        slot_rows = sb("slot_rows", [MT, P])
        S = {n: sem(n) for n in "step made zero_stored exp_done psum scattered slot_rows turned".split()}
        ps = [ctx.enter_context(nc.psum_tensor(f"rt_ps{b}", [P, 512], F32)) for b in range(3)]
        block = ctx.enter_context(nc.Block())

        @block.gpsimd
        def _(pool):
            nc.gpsimd.memset(before[:], 1.0).then_inc(S["made"], 1)
            pool.wait_ge(S["made"], 1)
            nc.gpsimd.affine_select(out=before[:], in_=before[:], compare_op=ALU.is_gt, fill=0.0, base=0,
                                    pattern=[[1, P]], channel_multiplier=-1).then_inc(S["made"], 1)
            pool.wait_ge(S["made"], 2)
            nc.gpsimd.memset(no_tokens[:], 0.0).then_inc(S["made"], 1)
            pool.wait_ge(S["made"], 3)
            nc.gpsimd.iota(token_i[:], pattern=[[P, NT]], base=0, channel_multiplier=1).then_inc(S["made"], 1)
            pool.wait_ge(S["step"], SLOT_STEP)
            pool.wait_ge(S["zero_stored"], 16)
            for k in range(2):
                for i in range(NT):
                    n = P if i < NT - 1 else DEC
                    nc.gpsimd.indirect_dma_start(g.token_dram, bass.IndirectOffsetOnAxis(ap=g.slot_i[0:n, k, i:i + 1], axis=0),
                                                 token[0:n, i:i + 1], None).then_inc(S["scattered"], 16)
            pool.wait_ge(S["scattered"], 16 * 2 * NT)

        @block.sync
        def _(sp):
            sp.wait_ge(S["made"], 3)
            sp.dma_start(g.token_dram.rearrange("(t r) o -> t (r o)", t=MT), no_tokens[:]).then_inc(S["zero_stored"], 16)
            sp.wait_ge(S["zero_stored"], 16)
            sp.wait_ge(S["scattered"], 16 * 2 * NT)
            sp.dma_start(slot_rows[:], g.token_dram.rearrange("(t r) o -> t (r o)", t=MT)).then_inc(S["slot_rows"], 16)

        @block.scalar
        def _(act):
            act.wait_ge(S["step"], LOGIT_STEP)
            nc.scalar.activation(g_exp[:], g_exp[:], ACT.Exp).then_inc(S["exp_done"], 1)
            act.wait_ge(S["step"], RATIO_STEP)
            nc.scalar.activation(ratio[:], ratio[:], ACT.Exp).then_inc(S["exp_done"], 1)

        @block.tensor
        def _(pe):
            pe.wait_ge(S["made"], 2)
            pe.wait_ge(S["step"], BOTH_STEP)
            flat = both[:].rearrange("p i e -> p (i e)")
            nc.tensor.matmul(ps[0][:, 0:NT * NE], before[:], flat, start=True, stop=True)
            nc.tensor.matmul(ps[1][:, 0:NT * NE], g.ones[:], flat, start=True, stop=True).then_inc(S["psum"], 1)
            pe.wait_ge(S["slot_rows"], 16)
            nc.tensor.transpose(ps[2][:, 0:MT], slot_rows[:], g.ident[0:MT, 0:MT]).then_inc(S["turned"], 1)

        @block.vector
        def _(dve):
            done = 0

            def then(instruction):
                nonlocal done
                instruction.then_inc(S["step"], 1)
                done += 1
                dve.wait_ge(S["step"], done)

            def wide(t, n):
                return t.unsqueeze(2).broadcast_to([P, NT, n])

            def first(values, maxima, out, n):
                then(nc.vector.tensor_tensor(cand[:, :, 0:n], values, wide(maxima, n), ALU.is_equal))
                then(nc.vector.tensor_tensor(cand[:, :, 0:n], cand[:, :, 0:n], rank[:, 0:n].unsqueeze(1).broadcast_to([P, NT, n]), ALU.mult))
                then(nc.vector.tensor_reduce(best[:], cand[:, :, 0:n], AX.X, ALU.max))
                then(nc.vector.tensor_tensor(out, cand[:, :, 0:n], wide(best[:], n), ALU.is_equal))

            groups, experts = g.logits[:, :, 0:NG], g.logits[:, :, NG:]
            then(nc.vector.tensor_tensor_scan(count[:], g.ones[:, 0:MT], g.ones[:, 0:MT], 0.0, ALU.mult, ALU.add))
            then(nc.vector.tensor_scalar(rank[:], count[:, 0:NE], -1.0, NE + 1.0, ALU.mult, ALU.add))
            dve.wait_ge(S["made"], 4)
            then(nc.vector.tensor_copy(token[:], token_i[:]))
            then(nc.vector.tensor_reduce(g_max[:], groups, AX.X, ALU.max))
            then(nc.vector.tensor_tensor(g_exp[:], groups, wide(g_max[:], NG), ALU.subtract))
            assert done == LOGIT_STEP
            first(groups, g_max[:], g_hot[:], NG)
            then(nc.vector.tensor_scalar(g_hot[:], g_hot[:], 1e30, -1e30, ALU.mult, ALU.add))
            then(nc.vector.tensor_tensor(inside[:].rearrange("p i (a b) -> p i a b", a=NG), experts.rearrange("p i (a b) -> p i a b", a=NG),
                                         g_hot[:].unsqueeze(3).broadcast_to([P, NT, NG, NE // NG]), ALU.add))
            then(nc.vector.tensor_reduce(top[:, 0], inside[:], AX.X, ALU.max))
            first(inside[:], top[:, 0], hot[:, 0], NE)
            then(nc.vector.scalar_tensor_tensor(inside[:], hot[:, 0], -1e30, inside[:], ALU.mult, ALU.add))
            then(nc.vector.tensor_reduce(top[:, 1], inside[:], AX.X, ALU.max))
            first(inside[:], top[:, 1], hot[:, 1], NE)
            then(nc.vector.memset(hot[DEC:P, :, NT - 1, :], 0.0))
            then(nc.vector.tensor_tensor(both[:], hot[:, 0], hot[:, 1], ALU.add))
            assert done == BOTH_STEP
            then(nc.vector.tensor_tensor(ratio[:], top[:, 1], top[:, 0], ALU.subtract))
            assert done == RATIO_STEP
            dve.wait_ge(S["exp_done"], 1)
            then(nc.vector.tensor_reduce(p_group[:], g_exp[:], AX.X, ALU.add))
            dve.wait_ge(S["exp_done"], 2)
            then(nc.vector.tensor_scalar(best[:], ratio[:], 1.0, None, ALU.add))
            then(nc.vector.tensor_tensor(p_group[:], p_group[:], best[:], ALU.mult))
            then(nc.vector.reciprocal(g.choice_w[:, 0], p_group[:]))
            then(nc.vector.tensor_tensor(g.choice_w[:, 1], g.choice_w[:, 0], ratio[:], ALU.mult))
            then(nc.vector.memset(total[:, 0], 0.0))
            dve.wait_ge(S["psum"], 1)
            for i in range(NT):
                then(nc.vector.tensor_tensor(total[:, i + 1], total[:, i], ps[1][:, NE * i:NE * i + NE], ALU.add))
            then(nc.vector.tensor_scalar(tiles[:, 0], total[:, NT], 0.0, None, ALU.is_gt))
            for j in range(1, NT):
                then(nc.vector.scalar_tensor_tensor(tiles[:, j % 2], total[:, NT], float(P * j), tiles[:, (j - 1) % 2], ALU.is_gt, ALU.add))
            last = (NT - 1) % 2
            then(nc.vector.tensor_tensor_scan(ends[:], g.ones[:, 0:NE], tiles[:, last], 0.0, ALU.mult, ALU.add))
            then(nc.vector.tensor_tensor(tiles[:, last], ends[:], tiles[:, last], ALU.subtract))
            then(nc.vector.tensor_tensor(slot[:].rearrange("p i e -> p (i e)"), total[:, 0:NT].rearrange("p i e -> p (i e)"), ps[0][:, 0:NT * NE], ALU.add))
            then(nc.vector.scalar_tensor_tensor(slot[:], tiles[:, last].unsqueeze(1).broadcast_to([P, NT, NE]), float(P), slot[:], ALU.mult, ALU.add))
            for k in range(2):
                then(nc.vector.tensor_tensor(hot[:, k], hot[:, k], slot[:], ALU.mult))
                then(nc.vector.tensor_reduce(slot_f[:, k], hot[:, k], AX.X, ALU.add))
            then(nc.vector.tensor_copy(g.slot_i[:], slot_f[:]))
            assert done == SLOT_STEP
            then(nc.vector.tensor_tensor(passed[:], ends[:].unsqueeze(1).broadcast_to([P, MT, NE]), count[:].unsqueeze(2).broadcast_to([P, MT, NE]), ALU.is_lt))
            then(nc.vector.tensor_reduce(owner[:], passed[:], AX.X, ALU.add))
            then(nc.vector.tensor_scalar(owner[:], owner[:], float(NE - 1), None, ALU.min))
            then(nc.vector.tensor_copy(g.owner_i[:], owner[:]))
            dve.wait_ge(S["turned"], 1)
            nc.vector.tensor_copy(g.row_token[:], ps[2][:, 0:MT])


def stage_experts(nc, g, d):
    with ExitStack() as ctx:
        def sb(name, shape):
            return ctx.enter_context(nc.sbuf_tensor("ex_" + name, shape, F32))

        def sem(name):
            return (g.kept if name in SOFTWARE_DMA else ctx).enter_context(nc.semaphore("ex_" + name))

        w_in = sb("w_in", [P, 2, 2, KD, FF])
        w_down = sb("w_down", [P, 2, FF // P, D])
        x = sb("x", [P, 2, D])
        xt = sb("xt", [P, 2, KD, P])
        silu = sb("silu", [P, 2, 2 * P])
        hid = sb("hid", [P, 2, FF // P, P])
        y = sb("y", [P, 2, D])
        S = {n: sem(n) for n in "in_loaded0 in_loaded1 down_loaded0 down_loaded1 x_loaded0 x_loaded1 turned xt_out gu_psum silu hid down_psum y_out stored0 stored1".split()}
        pair = lambda name: (S[name + "0"], S[name + "1"])
        in_loaded, down_loaded, x_loaded, stored = pair("in_loaded"), pair("down_loaded"), pair("x_loaded"), pair("stored")
        ps = [ctx.enter_context(nc.psum_tensor(f"ex_ps{b}", [P, 512], F32)) for b in range(8)]
        block = ctx.enter_context(nc.Block())
        gate_view = d["w_exp_gate"][0].rearrange("e (k p) n -> p (e k) n", p=P)
        up_view = d["w_exp_up"][0].rearrange("e (k p) n -> p (e k) n", p=P)
        down_view = d["w_exp_down"][0].rearrange("e (k p) n -> p (e k) n", p=P)
        ys_view = g.ys_dram.rearrange("(t p) c -> p t c", p=P)

        @block.sync
        def _(sp):
            def load(t, b, rounds):
                if rounds is not None:
                    sp.wait_ge(S["gu_psum"], rounds)
                e = sp.value_load(g.owner_i[0:1, bass.ds(t, 1)], min_val=0, max_val=NE - 1)
                sp.dma_start(w_in[:, b, 0], gate_view[:, bass.ds(e * KD, KD), :]).then_inc(in_loaded[b], 16)
                sp.dma_start(w_in[:, b, 1], up_view[:, bass.ds(e * KD, KD), :]).then_inc(in_loaded[b], 16)
                if rounds is not None:
                    sp.wait_ge(S["down_psum"], rounds * 2)
                sp.dma_start(w_down[:, b], down_view[:, bass.ds(e * (FF // P), FF // P), :]).then_inc(down_loaded[b], 16)

            def store(t, b, count):
                sp.wait_ge(S["y_out"], count)
                sp.dma_start(ys_view[:, bass.ds(t, 1), :], y[:, b:b + 1]).then_inc(stored[b], 16)

            load(0, 0, None)
            load(1, 1, None)
            with sp.Fori(1, MT // 2) as r:
                for b in range(2):
                    load(r * 2 + b, b, r * 2 + (b - 1))
                    store(r * 2 + (b - 2), b, r * 4 + (2 * b - 2))
            for b in range(2):
                store(MT - 2 + b, b, 2 * MT - 2 + 2 * b)
            for b in range(2):
                sp.wait_ge(stored[b], 8 * MT)

        @block.gpsimd
        def _(pool):
            for t in range(MT):
                if t >= 2:
                    pool.wait_ge(S["turned"], t - 1)
                nc.gpsimd.indirect_dma_start(x[:, t % 2], None, g.h2_dram,
                                             bass.IndirectOffsetOnAxis(ap=g.row_token[:, t:t + 1], axis=0)).then_inc(x_loaded[t % 2], 16)

        @block.tensor
        def _(pe):
            def turn(t, b, rounds, freed):
                pe.wait_ge(x_loaded[b], rounds)
                if freed is not None:
                    pe.wait_ge(S["xt_out"], freed)
                for k in range(KD):
                    last = nc.tensor.transpose(ps[k // 4][:, P * (k % 4):P * (k % 4) + P], x[:, b, P * k:P * k + P], g.ident[:])
                last.then_inc(S["turned"], 1)

            def gate_up(t, b, rounds, freed):
                pe.wait_ge(in_loaded[b], rounds)
                pe.wait_ge(S["xt_out"], t * 2 + 2)
                if freed is not None:
                    pe.wait_ge(S["hid"], freed)
                for m in range(4):
                    for k in range(KD):
                        last = nc.tensor.matmul(ps[2 + b][:, P * m:P * m + P], w_in[:, b, m // 2, k, P * (m % 2):P * (m % 2) + P], xt[:, b, k],
                                                start=m == 0 and k == 0, stop=m == 3 and k == KD - 1, skip_group_check=True)
                last.then_inc(S["gu_psum"], 1)

            def down(t, b, rounds, freed):
                pe.wait_ge(down_loaded[b], rounds)
                pe.wait_ge(S["hid"], t + 1)
                if freed is not None:
                    pe.wait_ge(S["y_out"], freed)
                for c in range(2):
                    for k in range(FF // P):
                        last = nc.tensor.matmul(ps[4 + 2 * b + c][:], hid[:, b, k], w_down[:, b, k, 512 * c:512 * c + 512],
                                                start=k == 0, stop=k == FF // P - 1)
                    last.then_inc(S["down_psum"], 1)

            turn(0, 0, 16, None)
            gate_up(0, 0, 32, None)
            turn(1, 1, 16, 2)
            down(0, 0, 16, None)
            gate_up(1, 1, 32, None)
            turn(2, 0, 32, 4)
            down(1, 1, 16, None)
            with pe.Fori(1, MT // 2 - 1) as r:
                for b in range(2):
                    gate_up(r * 2 + b, b, r * 32 + 32, r * 2 + (b - 1))
                    turn(r * 2 + (b + 1), 1 - b, r * 16 + (16 + 16 * b), r * 4 + (2 * b + 2))
                    down(r * 2 + b, b, r * 16 + 16, r * 4 + (2 * b - 2))
            t = MT - 2
            gate_up(t, 0, 16 * MT, t - 1)
            turn(t + 1, 1, 8 * MT, 2 * t + 2)
            down(t, 0, 8 * MT, 2 * t - 2)
            gate_up(t + 1, 1, 16 * MT, t)
            down(t + 1, 1, 8 * MT, 2 * t)

        @block.scalar
        def _(act):
            def unload(t, b, freed):
                act.wait_ge(S["turned"], t + 1)
                if freed is not None:
                    act.wait_ge(S["gu_psum"], freed)
                nc.scalar.activation(xt[:, b, 0:4], ps[0][:].rearrange("p (k t) -> p k t", k=4), ACT.Copy).then_inc(S["xt_out"], 1)

            def silu_of(t, b, freed):
                act.wait_ge(S["gu_psum"], t + 1)
                if freed is not None:
                    act.wait_ge(S["hid"], freed)
                nc.scalar.activation(silu[:, b], ps[2 + b][:, 0:2 * P], ACT.Silu).then_inc(S["silu"], 1)

            def store_half(t, b, freed):
                act.wait_ge(S["down_psum"], t * 2 + 1)
                if freed is not None:
                    act.wait_ge(stored[b], freed)
                nc.scalar.activation(y[:, b, 0:512], ps[4 + 2 * b][:], ACT.Copy).then_inc(S["y_out"], 1)

            act.preload_act_table(ACT.Silu)
            unload(0, 0, None)
            silu_of(0, 0, None)
            unload(1, 1, None)
            store_half(0, 0, None)
            silu_of(1, 1, None)
            unload(2, 0, 1)
            store_half(1, 1, None)
            with act.Fori(1, MT // 2 - 1) as r:
                for b in range(2):
                    silu_of(r * 2 + b, b, r * 2 + (b - 1))
                    unload(r * 2 + (b + 1), 1 - b, r * 2 + b)
                    store_half(r * 2 + b, b, r * 16)
            t = MT - 2
            silu_of(t, 0, t - 1)
            unload(t + 1, 1, t)
            store_half(t, 0, 8 * t)
            silu_of(t + 1, 1, t)
            store_half(t + 1, 1, 8 * t)

        @block.vector
        def _(dve):
            def unload(t, b, freed):
                dve.wait_ge(S["turned"], t + 1)
                if freed is not None:
                    dve.wait_ge(S["gu_psum"], freed)
                nc.vector.tensor_copy(xt[:, b, 4:8], ps[1][:].rearrange("p (k t) -> p k t", k=4)).then_inc(S["xt_out"], 1)

            def hidden(t, b, freed):
                dve.wait_ge(S["silu"], t + 1)
                if freed is not None:
                    dve.wait_ge(S["down_psum"], freed)
                nc.vector.tensor_tensor(hid[:, b].rearrange("p k t -> p (k t)"), silu[:, b], ps[2 + b][:, 2 * P:], ALU.mult).then_inc(S["hid"], 1)

            def store_half(t, b, freed):
                dve.wait_ge(S["down_psum"], t * 2 + 2)
                if freed is not None:
                    dve.wait_ge(stored[b], freed)
                nc.vector.tensor_copy(y[:, b, 512:], ps[5 + 2 * b][:]).then_inc(S["y_out"], 1)

            unload(0, 0, None)
            hidden(0, 0, None)
            unload(1, 1, None)
            store_half(0, 0, None)
            hidden(1, 1, None)
            unload(2, 0, 1)
            store_half(1, 1, None)
            with dve.Fori(1, MT // 2 - 1) as r:
                for b in range(2):
                    hidden(r * 2 + b, b, r * 4 + (2 * b - 2))
                    unload(r * 2 + (b + 1), 1 - b, r * 2 + b)
                    store_half(r * 2 + b, b, r * 16)
            t = MT - 2
            hidden(t, 0, 2 * t - 2)
            unload(t + 1, 1, t)
            store_half(t, 0, 8 * t)
            hidden(t + 1, 1, 2 * t)
            store_half(t + 1, 1, 8 * t)



def stage_combine(nc, g, d, out):
    with ExitStack() as ctx:
        def sb(name, shape):
            return ctx.enter_context(nc.sbuf_tensor("co_" + name, shape, F32))

        def sem(name):
            return (g.kept if name in SOFTWARE_DMA else ctx).enter_context(nc.semaphore("co_" + name))

        rows = sb("rows", [P, 3, 2, D])
        weights = sb("weights", [P, 2, 2, P])
        gated = sb("gated", [P, 2, D])
        gain = sb("gain", [P, 2, D])
        final_w = sb("final_w", [P, D])
        square = sb("square", [P, D])
        ssq = sb("ssq", [P, NT])
        std = sb("std", [P, NT])
        rstd = sb("rstd", [P, NT])
        S = {n: sem(n) for n in "gathered0 gathered1 gathered2 gains_loaded weights psum gated added ssq std rstd y stored".split()}
        gathered = [S[f"gathered{b}"] for b in range(3)]
        ps = [ctx.enter_context(nc.psum_tensor(f"co_ps{b}", [P, 512], F32)) for b in range(4)]
        block = ctx.enter_context(nc.Block())
        x1 = tiles_of(g.h)

        def size(i):
            return P if i < NT - 1 else DEC

        @block.gpsimd
        def _(pool):
            def gather(i):
                n = size(i)
                for k in range(2):
                    if i >= 3:
                        pool.wait_ge(S["psum"], 2 * (i - 2))
                    nc.gpsimd.indirect_dma_start(rows[0:n, i % 3, k], None, g.ys_dram,
                                                 bass.IndirectOffsetOnAxis(ap=g.slot_i[0:n, k, i:i + 1], axis=0)).then_inc(gathered[i % 3], 16)

            for i in range(3):
                gather(i)
            for i in range(NT):
                n = size(i)
                if i + 3 < NT:
                    gather(i + 3)
                pool.wait_ge(S["gated"], 2 * i + 2)
                nc.gpsimd.tensor_tensor(x1[0:n, i], x1[0:n, i], gated[0:n, i % 2], ALU.add).then_inc(S["added"], 1)

        @block.sync
        def _(sp):
            for who in range(2):
                sp.dma_start(gain[:, who], g.mod_dram[who:who + 1, 5 * D:6 * D].broadcast_to([P, D])).then_inc(S["gains_loaded"], 16)
            sp.dma_start(final_w[:], d["final_norm_w"].rearrange("(o c) -> o c", o=1).broadcast_to([P, D])).then_inc(S["gains_loaded"], 16)
            for i in range(NT):
                sp.wait_ge(S["y"], i + 1)
                if i < NT - 1:
                    sp.dma_start(out["y"][0][0, P * i:P * i + P, :], x1[:, i]).then_inc(S["stored"], 16)
                else:
                    sp.dma_start(out["y"][1][0], x1[0:DEC, i]).then_inc(S["stored"], 16)
            sp.wait_ge(S["stored"], 16 * NT)

        @block.tensor
        def _(pe):
            for i in range(NT):
                n = size(i)
                pe.wait_ge(S["weights"], i + 1)
                pe.wait_ge(gathered[i % 3], 32 * (i // 3 + 1))
                for c in range(2):
                    if i >= 2:
                        pe.wait_ge(S["gated"], 2 * (i - 2) + c + 1)
                    for k in range(2):
                        last = nc.tensor.matmul(ps[2 * (i % 2) + c][0:n], weights[0:n, i % 2, k, 0:n], rows[0:n, i % 3, k, 512 * c:512 * c + 512],
                                                start=k == 0, stop=k == 1)
                    last.then_inc(S["psum"], 1)

        @block.scalar
        def _(act):
            for i in range(NT):
                n = size(i)
                act.wait_ge(S["added"], i + 1)
                nc.scalar.activation(square[0:n], x1[0:n, i], ACT.Square, accum_out=ssq[0:n, i:i + 1]).then_inc(S["ssq"], 1)
                act.wait_ge(S["ssq"], i + 1)
                nc.scalar.activation(std[0:n, i:i + 1], ssq[0:n, i:i + 1], ACT.Sqrt, scale=1.0 / D, bias=g.eps[0:n]).then_inc(S["std"], 1)

        @block.vector
        def _(dve):
            def weigh(i):
                n = size(i)
                if i >= 2:
                    dve.wait_ge(S["psum"], 2 * (i - 1))
                for k in range(2):
                    last = nc.vector.tensor_scalar(weights[0:n, i % 2, k, 0:n], g.ident[0:n, 0:n], g.choice_w[0:n, k, i:i + 1], None, ALU.mult)
                last.then_inc(S["weights"], 1)

            def finish(i):
                n = size(i)
                dve.wait_ge(S["std"], i + 1)
                nc.vector.reciprocal(rstd[0:n, i:i + 1], std[0:n, i:i + 1]).then_inc(S["rstd"], 1)
                dve.wait_ge(S["rstd"], i + 1)
                nc.vector.scalar_tensor_tensor(x1[0:n, i], x1[0:n, i], rstd[0:n, i:i + 1], final_w[0:n], ALU.mult, ALU.mult).then_inc(S["y"], 1)

            weigh(0)
            weigh(1)
            dve.wait_ge(S["gains_loaded"], 48)
            for i in range(NT):
                n, who = size(i), 0 if i < NT - 1 else 1
                if i >= 2:
                    dve.wait_ge(S["added"], i - 1)
                for c in range(2):
                    half = slice(512 * c, 512 * c + 512)
                    dve.wait_ge(S["psum"], 2 * i + c + 1)
                    nc.vector.tensor_tensor(gated[0:n, i % 2, half], ps[2 * (i % 2) + c][0:n], gain[0:n, who, half], ALU.mult).then_inc(S["gated"], 1)
                if i + 2 < NT:
                    weigh(i + 2)
                if i:
                    finish(i - 1)
            finish(NT - 1)


def reuse_semaphores(nc):
    left = sorted(nc.released_uncleared_semaphores)
    while left:
        run = next((n for n in range(1, len(left)) if left[n] != left[0] + n), len(left))
        nc.gpsimd.sem_clear(range(left[0], left[0] + run))
        left = left[run:]
    nc.all_engine_barrier()


OUT_SHAPES = [(1, SEQ, D), (1, DEC, D)] + 2 * [(1, 1, HEADS, GDK, DV), (1, 1, HEADS, DV, DV), (1, 1, CW - 1, CONVCH),
                                               (1, 1, GROUPS, ST), (1, 1, GROUPS, ST)]


def build(nc, d, out):
    g = Shared()
    out = dict(y=out[0:2], gla=(out[2], out[7]), gdn=(out[3], out[8]), conv=(out[4], out[9]), s5=(out[5:7], out[10:12]))
    with ExitStack() as ctx:
        g.kept = ctx.enter_context(ExitStack())

        def sb(name, shape, stack=ctx):
            return stack.enter_context(nc.sbuf_tensor(name, shape, F32))

        g.mod_dram = nc.dram_tensor("mod_dram", [2, 6 * D], F32, kind="Internal").ap()
        g.ident = sb("ident", [P, P])
        g.upto = sb("upto", [P, P])
        g.after = sb("after", [P, P])
        g.ones = sb("ones", [P, P])
        g.row_sel = sb("row_sel", [P, 2 * P])
        g.eps = sb("eps", [P, 1])
        g.mod_cols = sb("mod_cols", [P, 48, 2])
        g.h = sb("h", [P, KD, TP])
        g.h2_dram = nc.dram_tensor("h2_dram", [TOK, D], F32, kind="Internal").ap()
        g.ys_dram = nc.dram_tensor("ys_dram", [XS, D], F32, kind="Internal").ap()
        g.token_dram = nc.dram_tensor("token_dram", [XS, 1], F32, kind="Internal").ap()
        stage_start(nc, g, d)
        g.mix = sb("mix", [P, KD, TOK])
        branches = ctx.enter_context(ExitStack())
        g.branch = sb("branch", [P, KB, TOK], branches)
        with ExitStack() as tables:
            g.s5_toeplitz = sb("s5_toeplitz", [P, GROUPS, LB, GC], tables)
            g.s5_b_cols = sb("s5_b_cols", [P, 2, PAIRS, P], tables)
            g.s5_c_pow = sb("s5_c_pow", [P, 2, PAIRS, LB + 1, GC], tables)
            g.s5_step = sb("s5_step_mul", [P, 2, 2, PAIRS], tables)
            stage_s5_tables(nc, g, d)
            stage_s5(nc, g, d, out)
        reuse_semaphores(nc)
        stage_glu(nc, g, d)
        with ExitStack() as inner:
            g.gla_qk = sb("gla_qk", [P, 4, TP], inner)
            g.gla_low = sb("gla_low", [LOWR, TOK], inner)
            g.gla_v = sb("gla_v", [P, NT, BR], inner)
            g.gla_gate = sb("gla_gate", [P, NT, BR], inner)
            stage_gla(nc, g, d, out)
        stage_merge(nc, g, d, "a", 0, False)
        reuse_semaphores(nc)
        with ExitStack() as inner:
            g.gdn_qk = sb("gdn_qk", [P, 2 * HEADS, TP], inner)
            g.gdn_v = sb("gdn_v", [P, NT, BR], inner)
            g.gdn_ba = sb("gdn_ba", [P, NT, 2 * HEADS], inner)
            gate_p = g.branch[:].rearrange("p k t -> p (k t)")[:, 0:8 * BR].rearrange("p (i c) -> p i c", i=8)
            gate_s = sb("gdn_gate_s", [P, BR], inner)
            g.gate_rows = lambda i: gate_p[:, i] if i < 8 else gate_s[:]
            stage_gdn_in(nc, g, d, out)
            stage_gdn(nc, g, d, out)
            stage_gdn_out(nc, g, d)
        stage_merge(nc, g, d, "b", 1, False)

        branches.close()
        finish(nc, g, d, out)


def finish(nc, g, d, out):
    with ExitStack() as ctx:
        def sb(name, shape, dt=F32):
            return ctx.enter_context(nc.sbuf_tensor(name, shape, dt))

        g.logits = sb("route_logits", [P, NT, NL])
        g.choice_w = sb("choice_w", [P, 2, NT])
        g.slot_i = sb("slot_i", [P, 2, NT], U32)
        g.row_token = sb("row_token", [P, MT], U32)
        g.owner_i = sb("owner_i", [P, MT], I32)
        reuse_semaphores(nc)
        stage_project(nc, g, d)
        stage_route(nc, g, d)
        stage_experts(nc, g, d)
        stage_combine(nc, g, d, out)


INS = """x_prompt x_sample c_prompt c_sample state_gla state_gdn cache_gdn_conv state_s5_re state_s5_im
norm1_w norm2_w final_norm_w w_ada b_ada w_in w_alpha_up b_alpha gla_norm_w conv_w gdn_a_log gdn_dt_bias gdn_norm_w
s5_a_re s5_a_im s5_log_dt s5_b_re s5_b_im s5_c_re s5_c_im s5_d w_glu b_glu w_br_a w_br_b w_br_c w_gate b_gate w_out
w_route_group b_route_group w_route_expert b_route_expert w_exp_gate w_exp_up w_exp_down""".split()


def kernel(**inputs):
    import concourse.bacc as _bacc
    from concourse.bass_utils import run_bass_kernel_spmd as _run

    nc = _bacc.Bacc("TRN2", target_bir_lowering=False, num_devices=1)
    arrays, d = {}, {}
    for name in INS:
        arrays["in_" + name] = np.ascontiguousarray(inputs[name])
        d[name] = nc.dram_tensor("in_" + name, arrays["in_" + name].shape, F32, kind="ExternalInput").ap()
    out = [nc.dram_tensor(f"out_{i}", shape, F32, kind="ExternalOutput").ap() for i, shape in enumerate(OUT_SHAPES)]
    build(nc, d, out)
    result = _run(nc, [arrays], core_ids=[0])
    return tuple(result.results[0][f"out_{i}"] for i in range(len(OUT_SHAPES)))
```
